# Optimizing a Trainium2 kernel written in Bass

```python
import jax, jax.numpy as jnp
from jax import lax
import numpy as np

D_MODEL = 1024
BATCH = 1
SEQ = 512
DEPTH = 1
DEC_BATCH = 1
DEC_SEQ = 1024
PAST_LEN = 128

N_MEM = 256
GRID_W = 64
HEAD_DIM = 64
D_MIX = D_MODEL
D_SGU = D_MIX // 2
SGU_HEADS = D_SGU // HEAD_DIM
D_NA = D_MIX - D_SGU
NA_HEADS = D_NA // HEAD_DIM
D_IN = 2 * D_SGU + 3 * D_NA
CHUNK = 128
NA_KH_MAX = 8
NA_KW = 16
NA_QCOLS = 16
NA_KCOLS = 2 * NA_KW
N_COL_BLOCKS = GRID_W // NA_QCOLS
XA_HEADS = 4
XA_HEAD_DIM = 128
D_XA = XA_HEADS * XA_HEAD_DIM
N_GROUPS = 4
EXPERTS_PER_GROUP = 8
N_EXPERTS = N_GROUPS * EXPERTS_PER_GROUP
TOP_K_IN_GROUP = 2
D_EXPERT = 128
EPS = 1e-6

kernel_name = 'hymba_gmlp_natten_hmoe_encoder'

def rmsnorm(x, g):
    xf = x.astype(jnp.float32)
    y = xf * lax.rsqrt(jnp.mean(xf * xf, axis=-1, keepdims=True) + EPS)
    return (y * g.astype(jnp.float32)).astype(x.dtype)

def _na_col_tables():
    c0 = np.arange(N_COL_BLOCKS) * NA_QCOLS
    cs = np.clip(c0 - NA_KW // 2, 0, GRID_W - NA_KCOLS)
    qcol = c0[:, None] + np.arange(NA_QCOLS)[None, :]
    kcol = cs[:, None] + np.arange(NA_KCOLS)[None, :]
    wstart = np.clip(qcol - NA_KW // 2, 0, GRID_W - NA_KW)
    kc = kcol[:, None, :]
    inwin = (kc >= wstart[..., None]) & (kc < wstart[..., None] + NA_KW)
    rel = kc - qcol[:, :, None]
    rel_idx = np.clip(rel, -(NA_KW - 1), NA_KW - 1) + NA_KW - 1
    return kcol, inwin, rel_idx

def spatial_gating(a, w_s, b_s, g_v):
    bsz, t = a.shape[:2]
    u, v = jnp.split(a, 2, axis=-1)
    v = rmsnorm(v, g_v).reshape(bsz, t // CHUNK, CHUNK, SGU_HEADS, HEAD_DIM)
    mixed = jnp.einsum('hpq,bcqhd->bcphd', w_s, v) + b_s.T[None, None, :, :, None]
    return u * mixed.reshape(bsz, t, D_SGU)

def neighbourhood_attention(q, k, v, rpb):
    bsz, t = q.shape[:2]
    rows = t // GRID_W
    kh = min(NA_KH_MAX, rows)
    qg = q.reshape(bsz, rows, GRID_W, NA_HEADS, HEAD_DIM)
    kg = k.reshape(bsz, rows, GRID_W, NA_HEADS, HEAD_DIM)
    vg = v.reshape(bsz, rows, GRID_W, NA_HEADS, HEAD_DIM)
    kcol, inwin, rel_col = _na_col_tables()
    col_bias = rpb[:, :, rel_col]
    mask = jnp.asarray(inwin)[None, None, :, :, None, :]
    scale = HEAD_DIM ** -0.5

    def row_block(r):
        rs = jnp.clip(r - kh // 2, 0, rows - kh)
        qr = lax.dynamic_index_in_dim(qg, r, axis=1, keepdims=False)
        qr = qr.reshape(bsz, N_COL_BLOCKS, NA_QCOLS, NA_HEADS, HEAD_DIM)
        kr = lax.dynamic_slice_in_dim(kg, rs, kh, axis=1)[:, :, kcol]
        vr = lax.dynamic_slice_in_dim(vg, rs, kh, axis=1)[:, :, kcol]
        s = jnp.einsum('bnqhd,brnchd->bhnqrc', qr, kr).astype(jnp.float32) * scale
        row_off = rs + jnp.arange(kh) - r + NA_KH_MAX - 1
        bias = jnp.take(col_bias, row_off, axis=1).transpose(0, 2, 3, 1, 4)
        s = jnp.where(mask, s + bias.astype(jnp.float32), -jnp.inf)
        p = jax.nn.softmax(s.reshape(s.shape[:4] + (-1,)), axis=-1).reshape(s.shape).astype(vr.dtype)
        o = jnp.einsum('bhnqrc,brnchd->bnqhd', p, vr)
        return o.reshape(bsz, GRID_W, D_NA)

    out = lax.map(row_block, jnp.arange(rows))
    return out.transpose(1, 0, 2, 3).reshape(bsz, t, D_NA)

def parallel_mixer(hn, w_in, g_sgu_v, sgu_w, sgu_b, na_rpb, g_out_a, g_out_b, w_out):
    bsz, t, _ = hn.shape
    proj = hn @ w_in
    a = jax.nn.gelu(proj[..., :2 * D_SGU])
    y_a = spatial_gating(a, sgu_w, sgu_b, g_sgu_v)
    q, k, v = jnp.split(proj[..., 2 * D_SGU:], 3, axis=-1)
    shp = (bsz, t, NA_HEADS, HEAD_DIM)
    y_b = neighbourhood_attention(q.reshape(shp), k.reshape(shp), v.reshape(shp), na_rpb)
    y = jnp.concatenate([rmsnorm(y_a, g_out_a), rmsnorm(y_b, g_out_b)], axis=-1)
    return y @ w_out

def memory_cross_attention(hn, memn, w_q, w_kv, w_o):
    bsz, t, _ = hn.shape
    q = (hn @ w_q).reshape(bsz, t, XA_HEADS, XA_HEAD_DIM)
    k, v = jnp.split(memn @ w_kv, 2, axis=-1)
    k = k.reshape(bsz, N_MEM, XA_HEADS, XA_HEAD_DIM)
    v = v.reshape(bsz, N_MEM, XA_HEADS, XA_HEAD_DIM)
    s = jnp.einsum('bthd,bmhd->bhtm', q, k).astype(jnp.float32) * (XA_HEAD_DIM ** -0.5)
    p = jax.nn.softmax(s, axis=-1).astype(v.dtype)
    o = jnp.einsum('bhtm,bmhd->bthd', p, v).reshape(bsz, t, D_XA)
    return o @ w_o

def hierarchical_moe(hn, w_rg, w_re, w_gate, w_up, w_down):
    bsz, t, d = hn.shape
    xf = hn.reshape(-1, d)
    g_prob = jax.nn.softmax((xf @ w_rg).astype(jnp.float32), axis=-1)
    g_top, g_idx = lax.top_k(g_prob, 1)
    e_logits = (xf @ w_re).astype(jnp.float32).reshape(-1, N_GROUPS, EXPERTS_PER_GROUP)
    e_sel = jnp.take_along_axis(e_logits, g_idx[:, :, None], axis=1)[:, 0]
    e_top, e_idx = lax.top_k(jax.nn.softmax(e_sel, axis=-1), TOP_K_IN_GROUP)
    e_top = e_top / jnp.sum(e_top, axis=-1, keepdims=True)
    weights = g_top * e_top
    expert_id = g_idx * EXPERTS_PER_GROUP + e_idx
    gates = jnp.sum(jax.nn.one_hot(expert_id, N_EXPERTS, dtype=jnp.float32) * weights[..., None], axis=1)
    hg = jnp.einsum('nd,edf->nef', xf, w_gate)
    hu = jnp.einsum('nd,edf->nef', xf, w_up)
    act = jax.nn.silu(hg) * hu * gates[..., None].astype(hn.dtype)
    out = jnp.einsum('nef,efd->nd', act, w_down)
    return out.reshape(bsz, t, d)

def encoder_trunk(x, mem, g_mix, w_in, g_sgu_v, sgu_w, sgu_b, na_rpb, g_out_a, g_out_b, w_out,
                  g_xattn, g_mem, w_xq, w_xkv, w_xo, g_moe, w_router_group, w_router_expert,
                  w_exp_gate, w_exp_up, w_exp_down, g_final):
    h = x
    for l in range(DEPTH):
        h = h + parallel_mixer(rmsnorm(h, g_mix[l]), w_in[l], g_sgu_v[l], sgu_w[l], sgu_b[l],
                               na_rpb[l], g_out_a[l], g_out_b[l], w_out[l])
        h = h + memory_cross_attention(rmsnorm(h, g_xattn[l]), rmsnorm(mem, g_mem[l]),
                                       w_xq[l], w_xkv[l], w_xo[l])
        h = h + hierarchical_moe(rmsnorm(h, g_moe[l]), w_router_group[l], w_router_expert[l],
                                 w_exp_gate[l], w_exp_up[l], w_exp_down[l])
    return rmsnorm(h, g_final)

def setup_inputs(seed: int = 0) -> dict:
    key = jax.random.key(seed)
    ks = jax.random.split(key, 32)
    nrm = lambda k, shape, s: jax.random.normal(k, shape, jnp.float32) * s
    gain = lambda k, shape: 1.0 + 0.02 * jax.random.normal(k, shape, jnp.float32)
    L = DEPTH
    return {
        'x_prompt': nrm(ks[0], (BATCH, SEQ, D_MODEL), 1.0),
        'x_sample': nrm(ks[1], (DEC_BATCH, DEC_SEQ, D_MODEL), 1.0),
        'mem_prompt': nrm(ks[2], (BATCH, N_MEM, D_MODEL), 1.0),
        'mem_sample': nrm(ks[3], (DEC_BATCH, N_MEM, D_MODEL), 1.0),
        'g_mix': gain(ks[4], (L, D_MODEL)),
        'w_in': nrm(ks[5], (L, D_MODEL, D_IN), D_MODEL ** -0.5),
        'g_sgu_v': gain(ks[6], (L, D_SGU)),
        'sgu_w': nrm(ks[7], (L, SGU_HEADS, CHUNK, CHUNK), CHUNK ** -0.5),
        'sgu_b': 1.0 + nrm(ks[8], (L, SGU_HEADS, CHUNK), 0.02),
        'na_rpb': nrm(ks[9], (L, NA_HEADS, 2 * NA_KH_MAX - 1, 2 * NA_KW - 1), 0.1),
        'g_out_a': gain(ks[10], (L, D_SGU)),
        'g_out_b': gain(ks[11], (L, D_NA)),
        'w_out': nrm(ks[12], (L, D_MIX, D_MODEL), D_MIX ** -0.5),
        'g_xattn': gain(ks[13], (L, D_MODEL)),
        'g_mem': gain(ks[14], (L, D_MODEL)),
        'w_xq': nrm(ks[15], (L, D_MODEL, D_XA), D_MODEL ** -0.5),
        'w_xkv': nrm(ks[16], (L, D_MODEL, 2 * D_XA), D_MODEL ** -0.5),
        'w_xo': nrm(ks[17], (L, D_XA, D_MODEL), D_XA ** -0.5),
        'g_moe': gain(ks[18], (L, D_MODEL)),
        'w_router_group': nrm(ks[19], (L, D_MODEL, N_GROUPS), D_MODEL ** -0.5),
        'w_router_expert': nrm(ks[20], (L, D_MODEL, N_EXPERTS), D_MODEL ** -0.5),
        'w_exp_gate': nrm(ks[21], (L, N_EXPERTS, D_MODEL, D_EXPERT), D_MODEL ** -0.5),
        'w_exp_up': nrm(ks[22], (L, N_EXPERTS, D_MODEL, D_EXPERT), D_MODEL ** -0.5),
        'w_exp_down': nrm(ks[23], (L, N_EXPERTS, D_EXPERT, D_MODEL), D_EXPERT ** -0.5),
        'g_final': gain(ks[24], (D_MODEL,)),
    }

def reference(x_prompt, x_sample, mem_prompt, mem_sample, g_mix, w_in, g_sgu_v, sgu_w, sgu_b, na_rpb,
              g_out_a, g_out_b, w_out, g_xattn, g_mem, w_xq, w_xkv, w_xo, g_moe, w_router_group,
              w_router_expert, w_exp_gate, w_exp_up, w_exp_down, g_final):
    y_prompt = encoder_trunk(x_prompt, mem_prompt, g_mix, w_in, g_sgu_v, sgu_w, sgu_b, na_rpb, g_out_a,
                             g_out_b, w_out, g_xattn, g_mem, w_xq, w_xkv, w_xo, g_moe, w_router_group,
                             w_router_expert, w_exp_gate, w_exp_up, w_exp_down, g_final)
    y_sample = encoder_trunk(x_sample, mem_sample, g_mix, w_in, g_sgu_v, sgu_w, sgu_b, na_rpb, g_out_a,
                             g_out_b, w_out, g_xattn, g_mem, w_xq, w_xkv, w_xo, g_moe, w_router_group,
                             w_router_expert, w_exp_gate, w_exp_up, w_exp_down, g_final)
    return (y_prompt, y_sample)


_drawn_inputs = setup_inputs


def setup_inputs(seed=0):
    import zlib

    import numpy as np

    out = dict(_drawn_inputs(seed))
    spreads = {}
    factors = {'g_sgu_v': 3.302,
     'sgu_b': 3.382,
     'g_out_a': 2.897,
     'g_out_b': 2.825,
     'g_xattn': 8.0,
     'g_mem': 5.429,
     'g_final': 8.114,
     'g_moe': 8.0}
    for name, (base, spread) in spreads.items():
        noise = np.random.default_rng([zlib.crc32(name.encode()), seed]).standard_normal(out[name].shape)
        drawn = base * np.exp(spread * noise) if base else spread * noise
        out[name] = __import__('jax').numpy.asarray(drawn.astype(out[name].dtype))
    for name, factor in factors.items():
        out[name] = (out[name] * factor).astype(out[name].dtype)
    return out
```

```python
import concourse.bass as bass
from concourse import mybir
from contextlib import ExitStack

F32 = mybir.dt.float32
I32 = mybir.dt.int32
ALU = mybir.AluOpType
ACT = mybir.ActivationFunctionType
AX = mybir.AxisListType.X

P = 128
D = 1024
KT = D // P
SEQ_P, SEQ_S = 512, 1024
T = SEQ_P + SEQ_S
NT = T // P
CH = 512
NCH = T // CH
N_MEM = 256
HALF = 512
NH = 8
HD = 64
NPAIR = NH // 2
GW = 64
KC = 32
QC = 16
QROWS = 4
GTOK = QROWS * GW
NKG = T // GTOK
KREL = 12
XH = 4
NG, EPG = 4, 8
NE = NG * EPG
FE = 128
EPS = 1e-6
MASKED = -1.0e30
NA_SCALE = HD ** -0.5
XA_SCALE = P ** -0.5
NA_GROUPS = [((0, 1), 4, False), ((0, 1), 0, False),
             ((2, 3), 4, False), ((2, 3, 4), 0, True), ((3, 4, 5), 0, True), ((4, 5), 0, False)]
COL_START = [0, 8, 24, 32]
NOVER = (2 * T + NE * (P - 1)) // P - NE
NOVER += -NOVER % 4
NBLK = NE + NOVER
RING = 8


def hymba_encoder(nc, a, y_prompt, y_sample):
    ctx = ExitStack()
    with ctx:
        def sem(name):
            return ctx.enter_context(nc.semaphore(name))

        def pair(name):
            return [sem(f"{name}_{j}") for j in range(2)]

        used = [0]

        def at(kb, *shape, dt=F32):
            used[0] += 1
            base = nc.sbuf_base + (-nc.sbuf_base) % 32
            return nc.alloc_sbuf_tensor_at(f"at_{kb}_{used[0]}".replace(".", "_"), [P, *shape], dt, offset=base + int(kb * 1024))[:]

        bank = [ctx.enter_context(nc.psum_tensor(f"bank{i}", [P, 512], F32)) for i in range(8)]

        def dram(name, shape, dt=F32):
            return nc.dram_tensor(name, shape, dt, kind="Internal").ap()

        y_mix = dram("y_mix", [T, 2 * HALF])
        v_att = dram("v_att", [T, HALF])
        rpb_pad = dram("rpb_pad", [NH * 15, 96])
        xn_moe = dram("xn_moe", [T, D])
        slot_tok = dram("slot_tok", [NBLK * P, 1], I32)
        y_exp = dram("y_exp", [NBLK * P, D])

        ident = at(192, P)
        small = at(192.5, 384)
        g_mix, g_xattn, g_mem, g_moe, g_out = (small[:, 8 * n:8 * n + 8] for n in range(5))
        sgu_b = small[:, 40:48]
        neg_half = small[:, 48:49]
        eps = small[:, 49:50]
        ms = small[:, 64:96]
        ms_eps = small[:, 96:128]
        rs = small[:, 128:160]
        na_st = small[:, 160:192]
        xa_st = small[:, 192:224]
        w_uvv = [at(16 * n, KT, HALF) for n in range(3)]
        xT = at(48, KT, T)
        x_in = [at(144 + 4 * j, D) for j in range(2)]
        xs = [at(152 + 4 * j, D) for j in range(2)]
        xf = [at(160 + 4 * j, KT, P) for j in range(2)]
        v_g, v_n, u_g, mixed, y_a = (at(168 + 2 * n, HALF) for n in range(5))
        y_an = [at(178 + 2 * j, HALF) for j in range(2)]
        v_st = [at(182 + 2 * j, HALF) for j in range(2)]
        sq_junk = at(186, HALF)
        sgu_nat = at(188, NH, P)
        sgu_wT = at(194, NH, P)
        gv_row = at(198, HALF)
        na_bias = at(96, NPAIR, 3, KREL, KC)
        na_bias_row = at(114, NPAIR, 3, KREL, KC)
        w_qk = [at(132 + 4 * j, KT, P) for j in range(2)]
        bias_src = at(200, 3, 15, KC)
        pad_t = at(206, 96)
        qk = at(144, NH, T)
        vals = at(0, NKG * 4, HALF)
        q_diag = [at(132 + 2 * j, 4, 2, QROWS, QC) for j in range(2)]
        na_o = [at(136 + j, 4, HD) for j in range(2)]
        na_p = [at(138 + 3 * j, 2, KREL * KC) for j in range(2)]
        na_pT = [at(194 + 3 * j, 2, KREL * KC) for j in range(2)]

        H = at(0, NT, D)
        w_out = at(48, KT, D)
        y_cat = [at(96 + 4 * j, D) for j in range(2)]
        x_res = [at(104 + 4 * j, D) for j in range(2)]
        y_T = [at(112 + 4 * j, KT, P) for j in range(2)]
        yb_junk = at(198, HALF)
        mem_in = [at(120 + 4 * j, D) for j in range(2)]
        w_xkv = at(144, KT, D)
        mem_T = at(176, KT, 4 * P)
        k_mem = at(128, XH, 4 * P)
        v_mem = at(136, 4, HALF)
        hs = [at(194 + 4 * j, D) for j in range(2)]
        w_xq = at(80, KT, HALF)
        w_xo = at(144, XH, D)
        h_T = at(176, KT, CH)
        q_x = [at(160, XH, CH), at(96 + 24, XH, CH)]
        p_x = [at(72 + 2 * n, 2, N_MEM) for n in range(4)]
        pT_x = at(96, XH, 2, CH)
        o_T = at(112, XH, CH)
        r_T = [at(168 + 4 * j, KT, P) for j in range(2)]
        w_rt = at(202, KT, NG + NE)
        logit = at(203.25, NT, NG + NE)
        gate = at(205, 2, NT)
        slot = at(205.25, 2, NT, dt=I32)
        slot_src = at(205.5, NBLK, dt=I32)
        over_e = at(205.75, NOVER, dt=I32)
        token = at(206, NT, dt=I32)
        zeros = at(206.5, 256)
        over_n = at(206.25, 1, dt=I32)
        rt = [at(144 + 1.5 * n, NT, NE) for n in range(10)]
        rs8 = [at(160 + 0.375 * n, NT, EPG) for n in range(12)]
        rs1 = [at(164.5 + 0.0625 * n, NT) for n in range(16)]
        re = [at(165.5 + 0.125 * n, NE) for n in range(10)]
        r11 = at(176, NE, NT - 1)
        r23 = at(178, NOVER, NE)
        over_f = at(181, NOVER)
        iota_e = at(181.25, NE)
        iota_b = at(181.5, NOVER)
        iota_j = at(181.75, NT - 1)
        first_g = at(182, NG)
        first_e = at(182.25, EPG)
        before = at(182.5, P)
        ones = at(183, P)
        slot_rows = at(183.5, P, dt=I32)
        slot_rows_f = at(184, P)
        iota_i = at(184.5, P, dt=I32)
        zeros_i = at(185, P, dt=I32)
        slots_kb = [48 + 12 * n for n in range(RING)]
        w_gu = [at(kb, 2, KT, FE) for kb in slots_kb]
        w_dn = [at(kb + 8, D) for kb in slots_kb]
        x_g = [at(144 + 4 * j, D) for j in range(2)]
        x_gT = [at(152 + 4 * j, KT, P) for j in range(2)]
        silu_g = at(160, FE)
        act_e = [at(160.5 + 0.5 * j, FE) for j in range(2)]
        act_T = [at(161.5 + 0.5 * j, P) for j in range(2)]
        y_st = [at(164 + 4 * j, D) for j in range(2)]
        y_g = [[at(144 + 8 * j + 4 * n, D) for n in range(2)] for j in range(2)]
        out_st = [at(160 + 4 * j, D) for j in range(2)]
        gf_row = at(172, D)

        blk = ctx.enter_context(nc.Block())

        w_in_here = [sem(f"w_in_here_{n}") for n in range(3)]
        consts_here = sem("consts_here")
        sgu_w_here = sem("sgu_w_here")
        x_here = pair("x_here")
        w_qk_here = pair("w_qk_here")
        pad_here, pad_stored, spread_here, bias_here = (sem(n) for n in ("pad_here", "pad_stored", "spread_here", "bias_here"))
        vals_here = sem("vals_here")
        v_stored, ya_stored = pair("v_stored"), pair("ya_stored")
        na_stored = pair("na_stored")
        const_made, ident_made, fill_made, bias_neg = (sem(n) for n in ("const_made", "ident_made", "fill_made", "bias_neg"))
        x_sq, x_eps, x_rs, xs_ready, xt_done = (pair(n) for n in ("x_sq", "x_eps", "x_rs", "xs_ready", "xt_done"))
        xf_evac = sem("xf_evac")
        xT_copied = pair("xT_copied")
        sgu_t, sgu_evac = sem("sgu_t"), sem("sgu_evac")
        v_done, u_done, v_gelu, u_gelu, v_sq, v_eps, v_rs, vn_ready, mix_done, mix_bias, ya_mul, ya_sq, ya_eps, ya_rs, yan_ready = (
            sem(n) for n in ("v_done", "u_done", "v_gelu", "u_gelu", "v_sq", "v_eps", "v_rs", "vn_ready", "mix_done",
                             "mix_bias", "ya_mul", "ya_sq", "ya_eps", "ya_rs", "yan_ready"))
        att_done, att_copied = sem("att_done"), sem("att_copied")
        qk_done, qk_evac_v, qk_evac_s = pair("qk_done"), pair("qk_evac_v"), pair("qk_evac_s")
        diag_zero, diag_ready, s_done, s_biased, s_min, p_exp, s_rcp = (
            sem(n) for n in ("diag_zero", "diag_ready", "s_done", "s_biased", "s_min", "p_exp", "s_rcp"))
        pt_done, pt_evac_s, pt_evac_v, o_done, o_evac = (
            sem(n) for n in ("pt_done", "pt_evac_s", "pt_evac_v", "o_done", "o_evac"))

        w_out_here, w_xkv_here, w_xq_here, w_xo_here, w_rt_here = (sem(n) for n in ("w_out_here", "w_xkv_here", "w_xq_here", "w_xo_here", "w_rt_here"))
        y_here, xr_here = pair("y_here"), pair("xr_here")
        yb_ready, yt_done = pair("yb_ready"), pair("yt_done")
        yT_evac, wo_done, h_added = sem("yT_evac"), sem("wo_done"), pair("h_added")
        mem_here = pair("mem_here")
        n_sq, n_eps, n_rs, n_ready, nt_done, nt_evac = (sem(n) for n in ("n_sq", "n_eps", "n_rs", "n_ready", "nt_done", "nt_evac"))
        xn_stored = pair("xn_stored")
        mm_done, mm_evac = sem("mm_done"), sem("mm_evac")
        sx_done, sx_max, sx_neg, px_exp, sx_rcp, px_ready, ptx_done, ptx_evac = (
            sem(n) for n in ("sx_done", "sx_max", "sx_neg", "px_exp", "sx_rcp", "px_ready", "ptx_done", "ptx_evac"))
        route, route_exp, exp_done, chosen, route_const, count_done, slot_ready = (
            sem(n) for n in ("route", "route_exp", "exp_done", "chosen", "route_const", "count_done", "slot_ready"))
        table_zero, table_sent, table_here, rows_f, rows_T, table_ready = (
            sem(n) for n in ("table_zero", "table_sent", "table_here", "rows_f", "rows_T", "table_ready"))
        w_e_here = [sem(f"w_e_here_{n}") for n in range(RING)]
        xg_here = pair("xg_here")
        xgt_done, xgt_evac, gu_done, e_silu, e_act, et_done, et_evac, y_done, y_evac_s, y_evac_v = (
            sem(n) for n in ("xgt_done", "xgt_evac", "gu_done", "e_silu", "e_act", "et_done", "et_evac", "y_done", "y_evac_s", "y_evac_v"))
        y_sent, all_sent, unused_filled = pair("y_sent"), sem("all_sent"), sem("unused_filled")
        gf_here, f_add, f_out = (sem(n) for n in ("gf_here", "f_add", "f_out"))
        yg_here, out_sent = pair("yg_here"), pair("out_sent")

        TPC = CH // P
        norms = [("mem", n) for n in range(4)] + [("h", t) for t in range(TPC)]
        norms += [("h", TPC + t) for t in range(TPC)]
        norms += [("h", 2 * TPC + t) for t in range(TPC)]
        norms += [("moe", t) for t in range(TPC)]
        norms += [("moe", TPC + t) for t in range(TPC)] + [("moe", 2 * TPC + t) for t in range(TPC)]
        groups = [("k_mem", h) for h in range(XH)] + [("v_mem", n) for n in range(4)]
        groups += [("q", 0, h) for h in range(XH)]
        stages = []
        stages += [("T", n) for n in range(4)] + [("mm", g) for g in range(8)] + [("T", n) for n in range(4, 8)]
        stages += [("mm", g) for g in range(8, 12)]
        for c in range(NCH):
            nxt = []
            if c + 1 < NCH:
                stages += [("T", norms.index(("h", TPC * (c + 1) + n))) for n in range(TPC)]
                nxt = [("q", c + 1, h) for h in range(XH)]
            stages += [("S", 8 * c + s) for s in range(4)]
            for s in range(8):
                if s < len(nxt):
                    stages.append(("mm", len(groups)))
                    groups.append(nxt[s])
                stages.append(("PT", 8 * c + s))
                if s < 4:
                    stages.append(("S", 8 * c + 4 + s))
            for h in range(XH):
                stages.append(("mm", len(groups)))
                groups.append(("o", c, h))
            if c > 0:
                for n in range(TPC):
                    stages.append(("T", norms.index(("moe", TPC * (c - 1) + n))))
                    stages.append(("mm", len(groups)))
                    groups.append(("route", TPC * (c - 1) + n))
            for t in range(TPC):
                for half in range(2):
                    stages.append(("mm", len(groups)))
                    groups.append(("xo", TPC * c + t, half))
        for n in range(TPC):
            stages.append(("T", norms.index(("moe", 2 * TPC + n))))
            stages.append(("mm", len(groups)))
            groups.append(("route", 2 * TPC + n))
        place = {st: n for n, st in enumerate(stages)}
        order = []
        ahead = {}
        for n in range(1, len(norms)):
            ahead[n] = place["T", n - 1]
            if norms[n][0] == "moe":
                ahead[n] = max(ahead[n], place["mm", groups.index(("xo", norms[n][1], 1))] + 1)
        order.append(("pre", 0))
        scaled = 0
        for k, st in enumerate(stages):
            order += [("pre", n) for n in range(1, len(norms)) if ahead[n] == k]
            if st[0] == "PT":
                order += [("px", n) for n in range(scaled, st[1] + 1)]
                scaled = max(scaled, st[1] + 1)
            order.append(st)
            if st[0] == "S" and st[1] - 1 >= scaled:
                order += [("px", n) for n in range(scaled, st[1])]
                scaled = st[1]
        n_groups = {g: n for n, g in enumerate(groups)}
        n_norms = {g: n for n, g in enumerate(norms)}

        def expert_blocks(eng, body):
            rounds = NE // RING
            for n in range(RING):
                body(n, n // 2, n, 0, False)
            with eng.Fori(1, rounds - 1) as r:
                for n in range(RING):
                    body(RING * r + n, RING // 2 * r + n // 2, n, r, False)
            for n in range(RING):
                r = rounds - 1
                body(RING * r + n, RING // 2 * r + n // 2, n, r, n == RING - 1)

        def overflow_blocks(eng, body):
            used = eng.value_load(over_n[0:1, 0:1], min_val=0, max_val=NOVER)
            with eng.Fori(0, NOVER // 4) as i:
                for n in range(4):
                    with eng.If(used > 4 * i + n):
                        body(NE + 4 * i + n, NE // 2 + 2 * i + n // 2, n, NE // RING + i)

        NSTEP = 2 * NKG

        def na_steps():
            return [(2 * g + n, g, (2 * n, 2 * n + 1)) for g in range(NKG) for n in range(2)]

        def first_then_loop(eng, n, body):
            body(0)
            with eng.Fori(1, n) as i:
                body(i)

        def tiles(eng, body, pairs=NT // 2):
            for j in range(2):
                body(0, j, False)
            with eng.Fori(1, pairs - 1) as i:
                for j in range(2):
                    body(i, j, False)
            for j in range(2):
                body(pairs - 1, j, j == 1)

        @blk.sync
        def _(sp):
            w_in = a["w_in"][0].rearrange("(k p) n -> p k n", p=P)

            def column(name):
                return a[name][0].rearrange("(k p) -> p k", p=P)

            sp.dma_start(sgu_nat, a["sgu_w"][0].rearrange("h p q -> p h q")).then_inc(sgu_w_here, 16)
            sp.dma_start(g_mix, column("g_mix"), allow_slow_non_contiguous=True).then_inc(consts_here, 16)
            sp.dma_start(g_xattn, column("g_xattn"), allow_slow_non_contiguous=True).then_inc(consts_here, 16)
            sp.dma_start(g_mem, column("g_mem"), allow_slow_non_contiguous=True).then_inc(consts_here, 16)
            sp.dma_start(g_moe, column("g_moe"), allow_slow_non_contiguous=True).then_inc(consts_here, 16)
            sp.dma_start(g_out[:, 0:4], column("g_out_a"), allow_slow_non_contiguous=True).then_inc(consts_here, 16)
            sp.dma_start(g_out[:, 4:8], column("g_out_b"), allow_slow_non_contiguous=True).then_inc(consts_here, 16)
            sp.dma_start(sgu_b, a["sgu_b"][0].rearrange("h p -> p h"), allow_slow_non_contiguous=True).then_inc(consts_here, 16)
            sp.dma_start(gv_row, a["g_sgu_v"][0].partition_broadcast(P)).then_inc(consts_here, 16)
            sp.dma_start(w_uvv[1], w_in[:, :, HALF:2 * HALF]).then_inc(w_in_here[1], 16)
            sp.dma_start(w_uvv[0], w_in[:, :, 0:HALF]).then_inc(w_in_here[0], 16)
            sp.dma_start(w_uvv[2], w_in[:, :, 4 * HALF:5 * HALF]).then_inc(w_in_here[2], 16)

            rpb = a["na_rpb"][0]
            sp.wait_ge(fill_made, 1)
            sp.dma_start(pad_t[0:NH * 15, 39:55], rpb.rearrange("h r c -> (h r) c")[:, 7:23]).then_inc(pad_here, 16)
            sp.wait_ge(pad_here, 16)
            sp.dma_start(rpb_pad, pad_t[0:NH * 15, :]).then_inc(pad_stored, 16)
            sp.wait_ge(pad_stored, 16)
            sp.wait_ge(fill_made, 2)
            pad = rpb_pad.rearrange("(h r) c -> h r c", r=15)
            spread = 0
            for qc in range(QC):
                dst = bias_src[qc:P:QC]
                for kind in range(3):
                    start = (47, 39, 31)[kind] - qc
                    if kind == 0 and qc < 8:
                        d, s = dst[:, 0, :, 0:QC], rpb[:, :, 15 - qc:31 - qc]
                    elif kind == 2 and qc > 8:
                        d, s = dst[:, 2, :, QC:KC], rpb[:, :, 15 - qc:31 - qc]
                    else:
                        d, s = dst[:, kind], pad[:, :, start:start + KC]
                    sp.dma_start(d, s).then_inc(spread_here, 16)
                    spread += 16
            sp.wait_ge(spread_here, spread)
            sp.wait_ge(bias_neg, 1)
            sp.wait_ge(fill_made, 3)
            for h in range(NH):
                for qr in range(QROWS):
                    p0 = (h % 2) * HD + qr * QC
                    src = bias_src[h * QC:(h + 1) * QC]
                    sp.dma_start(na_bias[p0:p0 + QC, h // 2], src[:, :, 3 - qr:15 - qr]).then_inc(bias_here, 16)
                    sp.dma_start(na_bias_row[p0:p0 + QC, h // 2, :, qr:qr + 8], src[:, :, 3:11]).then_inc(bias_here, 16)

            def channel_tiles(i):
                for j in range(2):
                    sp.wait_ge(qk_done[j], i)
                    sp.dma_start(w_qk[j], w_in[:, :, bass.ds(2 * HALF + (2 * i + j) * P, P)]).then_inc(w_qk_here[j], 16)

            first_then_loop(sp, NH // 2, channel_tiles)

            sp.wait_ge(fill_made, 4)
            for b in range(NE, NBLK):
                sp.dma_start(y_exp[b * P:(b + 1) * P].rearrange("p (a c) -> p a c", c=256),
                             zeros.unsqueeze(1).to_broadcast([P, D // 256, 256])).then_inc(unused_filled, 16)

            sp.wait_ge(att_done, NT)
            for j in range(2):
                sp.wait_ge(v_stored[j], 16 * NT // 2)
            for g in range(NKG):
                rows = v_att[g * GTOK:(g + 1) * GTOK].rearrange("(r c) n -> r c n", c=GW)
                for n in range(4):
                    sp.dma_start(vals[:, 4 * g + n], rows[:, COL_START[n]:COL_START[n] + KC]).then_inc(vals_here, 16)

            for j in range(2):
                sp.wait_ge(qk_done[j], NH // 2)
            sp.dma_start(w_out, a["w_out"][0].rearrange("(k p) n -> p k n", p=P)).then_inc(w_out_here, 16)
            sp.dma_start(w_xq, a["w_xq"][0].rearrange("(k p) n -> p k n", p=P)).then_inc(w_xq_here, 16)

            def head_pair(hp):
                for g in range(NKG):
                    sp.wait_ge(o_evac, 4 * (NKG * hp + g + 1))
                    for half in range(2):
                        dst = y_mix[g * GTOK:(g + 1) * GTOK, bass.ds(HALF + (2 * hp + half) * HD, HD)]
                        sp.dma_start(dst.rearrange("(n q) d -> q n d", n=4),
                                     na_o[g % 2][half * HD:(half + 1) * HD]).then_inc(na_stored[g % 2], 16)

            first_then_loop(sp, NPAIR, head_pair)

            for j in range(2):
                sp.wait_ge(na_stored[j], 16 * 2 * NPAIR * NKG // 2)
                sp.wait_ge(ya_stored[j], 16 * 2 * NT // 2)

            def load_rows(i, j, x_rows):
                sp.wait_ge(yt_done[j], i)
                sp.dma_start(y_cat[j], y_mix[bass.ds((2 * i + j) * P, P)]).then_inc(y_here[j], 16)
                sp.wait_ge(h_added[j], 2 * i)
                x_rows = x_rows.rearrange("(r n c) d -> n r c d", n=4, c=QC)
                for n in range(2):
                    sp.dma_start(x_res[j][n * HD:(n + 1) * HD], x_rows[2 * j + n]).then_inc(xr_here[j], 16)

            for j in range(2):
                load_rows(0, j, a["x_prompt"][0][0:GTOK])
            sp.dma_start(w_xkv, a["w_xkv"][0].rearrange("(k p) n -> p k n", p=P)).then_inc(w_xkv_here, 16)
            sp.dma_start(w_rt[:, :, 0:NG], a["w_router_group"][0].rearrange("(k p) n -> p k n", p=P)).then_inc(w_rt_here, 16)
            sp.dma_start(w_rt[:, :, NG:], a["w_router_expert"][0].rearrange("(k p) n -> p k n", p=P)).then_inc(w_rt_here, 16)
            for j in range(2):
                sp.dma_start(mem_in[j], a["mem_prompt"][0][j * P:(j + 1) * P]).then_inc(mem_here[j], 16)
            for j in range(2):
                load_rows(1, j, a["x_prompt"][0][GTOK:2 * GTOK])
            with sp.Fori(2, NT // 2) as i:
                for j in range(2):
                    load_rows(i, j, a["x_sample"][0][bass.ds(i * GTOK - SEQ_P, GTOK)])
            for j in range(2):
                sp.wait_ge(n_ready, j + 1)
                sp.dma_start(mem_in[j], a["mem_sample"][0][j * P:(j + 1) * P]).then_inc(mem_here[j], 16)

            def load_expert(e, n, used):
                if used is not None:
                    sp.wait_ge(y_done, used)
                one = slice(e, e + 1) if isinstance(e, int) else bass.ds(e, 1)
                sp.dma_start(w_gu[n][:, 0], a["w_exp_gate"][0, one].rearrange("e (k p) f -> p (e k) f", p=P)).then_inc(w_e_here[n], 16)
                sp.dma_start(w_gu[n][:, 1], a["w_exp_up"][0, one].rearrange("e (k p) f -> p (e k) f", p=P)).then_inc(w_e_here[n], 16)
                sp.dma_start(w_dn[n], a["w_exp_down"][0, one].rearrange("e p d -> (e p) d")).then_inc(w_e_here[n], 16)

            sp.wait_ge(mm_done, 2 * XH)
            sp.dma_start(w_xo, a["w_xo"][0].rearrange("(k p) n -> p k n", p=P)).then_inc(w_xo_here, 16)
            for e in (0, 1):
                load_expert(e, e, None)
            first_moe = n_norms["moe", 0]
            for n in range(first_moe, len(norms)):
                t = norms[n][1]
                sp.wait_ge(n_ready, n + 1)
                sp.dma_start(xn_moe[t * P:(t + 1) * P], hs[n % 2]).then_inc(xn_stored[n % 2], 16)
                if t == TPC - 1:
                    sp.wait_ge(mm_done, n_groups["q", NCH - 1, XH - 1] + 1)
                    load_expert(3, 3, None)
            sp.wait_ge(mm_done, len(groups))
            for e in (2, 4, 5, 6, 7):
                load_expert(e, e, None)

            with sp.Fori(0, NE // RING - 1) as r:
                for n in range(RING):
                    load_expert(RING * (r + 1) + n, n, RING * r + n + 1)

            sp.wait_ge(table_ready, 1)

            def load_overflow(b, half, n, r):
                e = sp.value_load(over_e[0:1, bass.ds(b - NE, 1)], min_val=0, max_val=NE - 1)
                load_expert(e, n, b - 3)

            overflow_blocks(sp, load_overflow)

            sp.dma_start(gf_row, a["g_final"].partition_broadcast(P)).then_inc(gf_here, 16)
            for t in range(NT):
                sp.wait_ge(f_out, t + 1)
                g, base = t // 2, 0 if t < SEQ_P // P else SEQ_P // GTOK
                y = y_prompt if t < SEQ_P // P else y_sample
                y = y[0, (g - base) * GTOK:(g - base + 1) * GTOK].rearrange("(r n c) d -> n r c d", n=4, c=QC)
                for n in range(2):
                    sp.dma_start(y[2 * (t % 2) + n], out_st[t % 2][n * HD:(n + 1) * HD]).then_inc(out_sent[t % 2], 16)
            for j in range(2):
                sp.wait_ge(out_sent[j], 32 * NT // 2)
                sp.wait_ge(xn_stored[j], 16 * NT // 2)

        @blk.gpsimd
        def _(pool):
            xp, xsm = a["x_prompt"][0], a["x_sample"][0]
            for j in range(2):
                pool.dma_start(x_in[j], xp[j * P:(j + 1) * P]).then_inc(x_here[j], 16)
            pool.memset(neg_half, -0.5).then_inc(const_made, 1)
            pool.memset(eps, EPS).then_inc(const_made, 1)
            pool.memset(ident, 0.0).then_inc(ident_made, 1)
            pool.wait_ge(ident_made, 1)
            pool.affine_select(out=ident, in_=ident, compare_op=ALU.not_equal, fill=1.0, base=0,
                               pattern=[[-1, P]], channel_multiplier=1).then_inc(ident_made, 1)
            pool.wait_ge(const_made, 2)

            def rsqrt(col, squares, n_sq, eps_sem, n_eps, out_sem):
                pool.wait_ge(squares, n_sq)
                pool.tensor_tensor(ms_eps[:, col:col + 1], ms[:, col:col + 1], eps, ALU.add).then_inc(eps_sem, 1)
                pool.wait_ge(eps_sem, n_eps)
                pool.tensor_tensor(rs[:, col:col + 1], ms_eps[:, col:col + 1], neg_half, ALU.pow).then_inc(out_sem, 1)

            def load_x(rows, i, j):
                pool.wait_ge(xs_ready[j], i)
                pool.dma_start(x_in[j], rows).then_inc(x_here[j], 16)

            def norm_x(i, j):
                rsqrt(j, x_sq[j], i + 1, x_eps[j], i + 1, x_rs[j])

            def tile_work(i, j, last, next_rows):
                t = 2 * i + j
                if j == 0:
                    norm_x(i, 1)
                elif not last:
                    norm_x(i + 1, 0)
                if next_rows is not None:
                    load_x(next_rows(j), i + 1, j)
                rsqrt(2, v_sq, t + 1, v_eps, t + 1, v_rs)
                rsqrt(3, ya_sq, t + 1, ya_eps, t + 1, ya_rs)

            norm_x(0, 0)
            for j in range(2):
                tile_work(0, j, False, lambda j: xp[(2 + j) * P:(3 + j) * P])
            pool.wait_ge(spread_here, 16 * 3 * QC)
            pool.tensor_scalar(bias_src, bias_src, -1.0, 0.0, ALU.mult, ALU.add).then_inc(bias_neg, 1)
            with pool.Fori(1, NT // 2 - 1) as i:
                for j in range(2):
                    tile_work(i, j, False, lambda j: xsm[bass.ds((2 * (i + 1) + j) * P - SEQ_P, P)])
            for j in range(2):
                tile_work(NT // 2 - 1, j, j == 1, None)

            for j in range(2):
                pool.wait_ge(qk_done[j], NH // 2)
            for j in range(2):
                pool.memset(q_diag[j], 0.0).then_inc(diag_zero, 1)
            pool.wait_ge(diag_zero, 2)
            for j in range(2):
                pool.wait_ge(qk_evac_v[j], 2 * (NH // 2))
                pool.wait_ge(qk_evac_s[j], NH // 2)
            def head_pair(hp):
                for g in range(NKG):
                    pool.wait_ge(s_done, 2 * (NSTEP * hp + max(2 * g - 2, 0)))
                    for half in range(2):
                        rows = slice(half * HD, (half + 1) * HD)
                        q = qk[rows, hp, g * GTOK:(g + 1) * GTOK].rearrange("p (r n c) -> p n r c", n=4, c=QC)
                        pool.tensor_copy(q_diag[g % 2][rows, :, half], q).then_inc(diag_ready, 1)

            first_then_loop(pool, NPAIR, head_pair)

            def rsqrt_pair(i, j):
                n = i + 1 + NT // 2
                rsqrt(j, x_sq[j], n, x_eps[j], n, x_rs[j])

            tiles(pool, lambda i, j, last: rsqrt_pair(i, j))
            for n in range(len(norms)):
                rsqrt(4 + n % 2, n_sq, n + 1, n_eps, n + 1, n_rs)

            pool.wait_ge(mm_done, n_groups["q", NCH - 1, XH - 1] + 1)
            for dst, pattern, base, cm in ((iota_e, [[P, NE]], 0, 0), (iota_b, [[1, NOVER]], 0, 0),
                                           (iota_j, [[P, NT - 1]], P, 0), (first_g, [[-1, NG]], NG, 0),
                                           (first_e, [[-1, EPG]], EPG, 0), (token, [[P, NT]], 0, 1)):
                pool.iota(dst, pattern=pattern, base=base, channel_multiplier=cm,
                          allow_small_or_imprecise_dtypes=True).then_inc(route_const, 1)
            pool.memset(ones, 1.0).then_inc(route_const, 1)
            pool.memset(before, 1.0).then_inc(route_const, 1)
            pool.memset(zeros_i, 0).then_inc(route_const, 1)
            pool.wait_ge(route_const, 9)
            pool.affine_select(out=before, in_=before, compare_op=ALU.is_gt, fill=0.0, base=0,
                               pattern=[[1, P]], channel_multiplier=-1).then_inc(route_const, 1)

            table = slot_tok.rearrange("(b p) o -> b (p o)", p=P)
            pool.dma_start(table, zeros_i[0:NBLK]).then_inc(table_zero, 16)
            pool.wait_ge(table_zero, 16)
            pool.wait_ge(slot_ready, 2)
            for k in range(2):
                for t in range(NT):
                    pool.indirect_dma_start(out=slot_tok, out_offset=bass.IndirectOffsetOnAxis(ap=slot[:, k, t:t + 1], axis=0),
                                            in_=token[:, t:t + 1], in_offset=None).then_inc(table_sent, 16)
            pool.wait_ge(table_sent, 16 * 2 * NT)
            pool.dma_start(slot_rows[0:NBLK], table).then_inc(table_here, 16)

            pool.wait_ge(table_ready, 1)
            for j in range(2):
                pool.wait_ge(xn_stored[j], 16 * NT // 2)

            def gather(rows, j):
                pool.indirect_dma_start(out=x_g[j], out_offset=None, in_=xn_moe,
                                        in_offset=bass.IndirectOffsetOnAxis(ap=rows, axis=0)).then_inc(xg_here[j], 16)

            for b in range(NE):
                if b >= 2:
                    pool.wait_ge(xgt_done, b - 1)
                gather(slot_src[:, b:b + 1], b % 2)
            used = pool.value_load(over_n[0:1, 0:1], min_val=0, max_val=NOVER)
            for b in range(NE, NBLK):
                with pool.If(used > b - NE):
                    pool.wait_ge(xgt_done, b - 1)
                    gather(slot_src[:, b:b + 1], b % 2)

            pool.wait_ge(all_sent, 1)

            def gather_y(t):
                if t >= 2:
                    pool.wait_ge(f_add, 2 * (t - 1))
                for k in range(2):
                    pool.indirect_dma_start(out=y_g[t % 2][k], out_offset=None, in_=y_exp,
                                            in_offset=bass.IndirectOffsetOnAxis(ap=slot[:, k, t:t + 1], axis=0)).then_inc(yg_here[t % 2], 16)

            gather_y(0)
            for t in range(NT):
                if t + 1 < NT:
                    gather_y(t + 1)
                n = len(norms) + t
                rsqrt(4 + n % 2, n_sq, n + 1, n_eps, n + 1, n_rs)

        @blk.scalar
        def _(act):
            def square_x(i, j):
                act.wait_ge(x_here[j], 16 * (i + 1))
                act.wait_ge(xt_done[j], i)
                nc.scalar.activation(xs[j], x_in[j], ACT.Square, scale=D ** -0.5,
                                     accum_out=ms[:, j:j + 1]).then_inc(x_sq[j], 1)

            def copy_xT(i, j):
                t = 2 * i + j
                act.wait_ge(xf_evac, 2 * (t + 1))
                nc.scalar.activation(xT[:, :, bass.ds(t * P, P)], xf[j], ACT.Copy).then_inc(xT_copied[j], 1)

            square_x(0, 0)
            copy_xT(0, 0)

            def tile_work(i, j, last):
                t = 2 * i + j
                nxt = (i, 1) if j == 0 else (i + 1, 0)
                if not last:
                    square_x(*nxt)
                act.wait_ge(v_done, t + 1)
                act.wait_ge(vn_ready, t)
                nc.scalar.activation(v_g, bank[2][:], ACT.Gelu_apprx_tanh).then_inc(v_gelu, 1)
                act.wait_ge(v_gelu, t + 1)
                act.wait_ge(ya_sq, t)
                nc.scalar.activation(sq_junk, v_g, ACT.Square, scale=HALF ** -0.5,
                                     accum_out=ms[:, 2:3]).then_inc(v_sq, 1)
                act.wait_ge(u_done, t + 1)
                act.wait_ge(ya_mul, t)
                nc.scalar.activation(u_g, bank[3][:], ACT.Gelu_apprx_tanh).then_inc(u_gelu, 1)
                if not last:
                    copy_xT(*nxt)
                act.wait_ge(att_done, t + 1)
                act.wait_ge(v_stored[j], 16 * i)
                nc.scalar.activation(v_st[j], bank[4][:], ACT.Copy).then_inc(att_copied, 1)
                act.wait_ge(att_copied, t + 1)
                act.dma_start(v_att[bass.ds(t * P, P)], v_st[j]).then_inc(v_stored[j], 16)
                act.wait_ge(ya_mul, t + 1)
                act.wait_ge(v_sq, t + 1)
                nc.scalar.activation(sq_junk, y_a, ACT.Square, scale=HALF ** -0.5,
                                     accum_out=ms[:, 3:4]).then_inc(ya_sq, 1)
                act.wait_ge(yan_ready, t + 1)
                for r in range(2):
                    dst = y_mix[bass.ds(i * GTOK, GTOK), 0:HALF].rearrange("(n r c) d -> n r c d", n=4, r=QROWS)
                    act.dma_start(dst[:, 2 * j + r], y_an[j][r * GW:(r + 1) * GW]).then_inc(ya_stored[j], 16)

            tiles(act, tile_work)

            for j in range(2):
                act.wait_ge(ya_stored[j], 16 * 2 * NT // 2)
                act.wait_ge(v_stored[j], 16 * NT // 2)
            def channel_tiles(i):
                for j in range(2):
                    act.wait_ge(qk_done[j], i + 1)
                    nc.scalar.activation(qk[:, 2 * i + j, CH:2 * CH], bank[3 * j + 1][:], ACT.Copy).then_inc(qk_evac_s[j], 1)

            first_then_loop(act, NH // 2, channel_tiles)

            def head_pair(hp):
                base = NSTEP * hp

                def exps(s):
                    width = len(NA_GROUPS[s // 2][0]) * P
                    act.wait_ge(s_min, base + s + 1)
                    for n in range(2):
                        p = na_p[s % 2][:, n, 0:width]
                        nc.scalar.activation(p, p, ACT.Exp, bias=na_st[:, 2 * (s % 2) + n:2 * (s % 2) + n + 1], scale=-1.0,
                                             accum_out=na_st[:, 4 + 2 * (s % 2) + n:5 + 2 * (s % 2) + n]).then_inc(p_exp, 1)

                def evac_pT(s):
                    width = len(NA_GROUPS[s // 2][0]) * P
                    act.wait_ge(pt_done, base + s + 1)
                    act.wait_ge(o_done, base + s - 1 if s >= 1 else base)
                    nc.scalar.activation(na_pT[s % 2][:, 0, 0:width], bank[4][:, 0:width], ACT.Copy).then_inc(pt_evac_s, 1)

                for s in range(NSTEP + 1):
                    if s < NSTEP:
                        exps(s)
                    if s >= 1:
                        evac_pT(s - 1)

            first_then_loop(act, NPAIR, head_pair)

            def square_y(i, j):
                act.wait_ge(y_here[j], 16 * (i + 1))
                act.wait_ge(x_sq[1 - j], NT // 2 + i + j)
                nc.scalar.activation(yb_junk, y_cat[j][:, HALF:], ACT.Square, scale=HALF ** -0.5,
                                     accum_out=ms[:, j:j + 1]).then_inc(x_sq[j], 1)

            tiles(act, lambda i, j, last: square_y(i, j))

            def source(n):
                kind, t = norms[n]
                return mem_in[n % 2] if kind == "mem" else H[:, t]

            def wait_source(eng, n):
                kind, t = norms[n]
                if kind == "mem":
                    eng.wait_ge(mem_here[n % 2], 16 * (n // 2 + 1))
                elif kind == "h":
                    eng.wait_ge(h_added[t % 2], 2 * (t // 2 + 1))
                else:
                    eng.wait_ge(mm_evac, n_groups["xo", t, 1] + 1)

            act.wait_ge(x_sq[1], NT)
            for what, n in order:
                if what == "pre":
                    wait_source(act, n)
                    if n >= 2:
                        act.wait_ge(nt_done, n - 1)
                    stored = (n - n_norms["moe", 0]) // 2
                    if stored > 0:
                        act.wait_ge(xn_stored[n % 2], 16 * stored)
                    nc.scalar.activation(hs[n % 2], source(n), ACT.Square, scale=D ** -0.5,
                                         accum_out=ms[:, 4 + n % 2:5 + n % 2]).then_inc(n_sq, 1)
                elif what == "S":
                    act.wait_ge(sx_neg, n + 1)
                    if n >= 4:
                        act.wait_ge(ptx_done, n - 3)
                    for h in range(2):
                        k = 2 * (n % 4) + h
                        nc.scalar.activation(p_x[n % 4][:, h], bank[6 + n % 2][:, h * N_MEM:(h + 1) * N_MEM], ACT.Exp,
                                             bias=xa_st[:, 8 + k:9 + k], scale=XA_SCALE,
                                             accum_out=xa_st[:, 16 + k:17 + k]).then_inc(px_exp, 1)
                elif what == "PT":
                    c, t, hp = n // 8, (n % 8) // 2, n % 2
                    act.wait_ge(ptx_done, n + 1)
                    if n % 8 == 0 and c > 0:
                        act.wait_ge(mm_done, n_groups["o", c - 1, XH - 1] + 1)
                    nc.scalar.activation(pT_x[:, 2 * hp:2 * hp + 2, :, t * P:(t + 1) * P],
                                         bank[2 + n % 2][:].rearrange("p (h m t) -> p h m t", h=2, m=2), ACT.Copy).then_inc(ptx_evac, 1)

            act.wait_ge(route_exp, 1)
            nc.scalar.activation(rs8[1][:, :, 0:NG], rs8[0][:, :, 0:NG], ACT.Exp).then_inc(exp_done, 1)
            act.wait_ge(route_exp, 2)
            nc.scalar.activation(rs1[9], rs1[8], ACT.Exp).then_inc(exp_done, 1)

            def expert(b, half, n, r, last=False):
                act.wait_ge(gu_done, b + 1)
                nc.scalar.activation(silu_g, bank[2][:, 0:FE], ACT.Silu).then_inc(e_silu, 1)
                act.wait_ge(y_done, b + 1)
                act.wait_ge(y_sent[n % 2], 16 * half)
                nc.scalar.activation(y_st[n % 2][:, 0:HALF], bank[5][:], ACT.Copy).then_inc(y_evac_s, 1)
                act.wait_ge(y_evac_s, b + 1)
                act.wait_ge(y_evac_v, b + 1)
                act.dma_start(y_exp[bass.ds(b * P, P)], y_st[n % 2]).then_inc(y_sent[n % 2], 16)

            expert_blocks(act, expert)
            act.wait_ge(table_ready, 1)
            act.wait_ge(unused_filled, 16 * NOVER)
            overflow_blocks(act, expert)
            used = act.value_load(over_n[0:1, 0:1], min_val=0, max_val=NOVER)
            act.wait_ge(y_sent[0], 16 * (NE // 2) + 16 * ((used + 1) // 2))
            act.wait_ge(y_sent[1], 16 * (NE // 2) + 16 * (used // 2))
            nc.scalar.activation(xa_st[:, 0:1], xa_st[:, 0:1], ACT.Copy).then_inc(all_sent, 1)

            for t in range(NT):
                act.wait_ge(f_add, 2 * (t + 1))
                if t >= 2:
                    act.wait_ge(out_sent[t % 2], 32 * (t // 2))
                n = len(norms) + t
                nc.scalar.activation(out_st[t % 2], H[:, t], ACT.Square, scale=D ** -0.5,
                                     accum_out=ms[:, 4 + n % 2:5 + n % 2]).then_inc(n_sq, 1)

        @blk.vector
        def _(dve):
            nc.vector.memset(pad_t, MASKED).then_inc(fill_made, 1)
            nc.vector.memset(bias_src, MASKED).then_inc(fill_made, 1)
            nc.vector.memset(na_bias_row, -MASKED).then_inc(fill_made, 1)
            nc.vector.memset(zeros, 0.0).then_inc(fill_made, 1)
            for n in range(2):
                dve.wait_ge(sgu_t, n + 1)
                nc.vector.tensor_copy(sgu_wT[:, 4 * n:4 * n + 4], bank[n][:].rearrange("p (h q) -> p h q", h=4)).then_inc(sgu_evac, 1)
            dve.wait_ge(consts_here, 16 * 8)

            def scale_x(i, j):
                dve.wait_ge(x_rs[j], i + 1)
                nc.vector.tensor_scalar(xs[j], x_in[j], rs[:, j:j + 1], None, ALU.mult).then_inc(xs_ready[j], 1)

            def evac_xT(i, j):
                dve.wait_ge(xt_done[j], i + 1)
                dve.wait_ge(att_done, 2 * i)
                dve.wait_ge(xT_copied[j], i)
                for n in range(2):
                    g = g_mix[:, 4 * n:4 * n + 4].unsqueeze(2).to_broadcast([P, 4, P])
                    nc.vector.tensor_tensor(xf[j][:, 4 * n:4 * n + 4], bank[n][:].rearrange("p (k t) -> p k t", k=4), g,
                                            ALU.mult).then_inc(xf_evac, 1)

            scale_x(0, 0)
            evac_xT(0, 0)

            def tile_work(i, j, last):
                t = 2 * i + j
                nxt = (i, 1) if j == 0 else (i + 1, 0)
                if not last:
                    scale_x(*nxt)
                dve.wait_ge(v_rs, t + 1)
                dve.wait_ge(mix_done, t)
                nc.vector.scalar_tensor_tensor(v_n, v_g, rs[:, 2:3], gv_row, ALU.mult, ALU.mult).then_inc(vn_ready, 1)
                if not last:
                    evac_xT(*nxt)
                dve.wait_ge(mix_done, t + 1)
                dve.wait_ge(ya_mul, t)
                nc.vector.tensor_tensor(mixed.rearrange("p (h d) -> p h d", h=NH), bank[5][:].rearrange("p (h d) -> p h d", h=NH),
                                        sgu_b.unsqueeze(2).to_broadcast([P, NH, HD]), ALU.add).then_inc(mix_bias, 1)
                dve.wait_ge(mix_bias, t + 1)
                dve.wait_ge(u_gelu, t + 1)
                dve.wait_ge(yan_ready, t)
                nc.vector.tensor_tensor(y_a, mixed, u_g, ALU.mult).then_inc(ya_mul, 1)
                dve.wait_ge(ya_rs, t + 1)
                dve.wait_ge(ya_stored[j], 32 * i)
                nc.vector.tensor_scalar(y_an[j], y_a, rs[:, 3:4], None, ALU.mult).then_inc(yan_ready, 1)

            tiles(dve, tile_work)

            for j in range(2):
                dve.wait_ge(ya_stored[j], 16 * 2 * NT // 2)
                dve.wait_ge(v_stored[j], 16 * NT // 2)
            def channel_tiles(i):
                for j in range(2):
                    dve.wait_ge(qk_done[j], i + 1)
                    for n in (0, 2):
                        nc.vector.tensor_copy(qk[:, 2 * i + j, n * CH:(n + 1) * CH], bank[3 * j + n][:]).then_inc(qk_evac_v[j], 1)

            first_then_loop(dve, NH // 2, channel_tiles)

            dve.wait_ge(bias_here, 16 * 2 * NH * QROWS)
            def head_pair(hp):
                base = NSTEP * hp

                def scores(s):
                    keys, first, row_masked = NA_GROUPS[s // 2]
                    width = len(keys) * P
                    kind = s % 2
                    bias = (na_bias_row if row_masked else na_bias)[:, hp, kind:kind + 2, first:first + width // KC]
                    for n in range(2):
                        dve.wait_ge(s_done, 2 * (base + s) + n + 1)
                        if n == 0:
                            dve.wait_ge(pt_done, base + s - 1 if s >= 1 else base)
                        nc.vector.scalar_tensor_tensor(
                            na_p[s % 2][:, n, 0:width].rearrange("p (r c) -> p r c", c=KC),
                            bank[2 * (s % 2) + n][:, 0:width].rearrange("p (r c) -> p r c", c=KC), -NA_SCALE,
                            bias[:, n], ALU.mult, ALU.add).then_inc(s_biased, 1)
                    dve.wait_ge(s_biased, 2 * (base + s + 1))
                    nc.vector.tensor_reduce(na_st[:, 2 * (s % 2):2 * (s % 2) + 2], na_p[s % 2][:, :, 0:width], AX, ALU.min).then_inc(s_min, 1)

                def evac_pT(s):
                    width = len(NA_GROUPS[s // 2][0]) * P
                    dve.wait_ge(p_exp, 2 * (base + s + 1))
                    dve.wait_ge(o_evac, 2 * (base + s - 1) if s >= 1 else 2 * base)
                    nc.vector.reciprocal(na_st[:, 8 + 2 * (s % 2):10 + 2 * (s % 2)], na_st[:, 4 + 2 * (s % 2):6 + 2 * (s % 2)]).then_inc(s_rcp, 1)
                    dve.wait_ge(pt_done, base + s + 1)
                    dve.wait_ge(o_done, base + s - 1 if s >= 1 else base)
                    nc.vector.tensor_copy(na_pT[s % 2][:, 1, 0:width], bank[5][:, 0:width]).then_inc(pt_evac_v, 1)

                def evac_o(s):
                    g = s // 2
                    dve.wait_ge(o_done, base + s + 1)
                    dve.wait_ge(s_rcp, base + s + 1)
                    if s % 2 == 0:
                        dve.wait_ge(na_stored[g % 2], 32 * (3 * hp + g // 2))
                    for half in range(2):
                        rows = slice(half * HD, (half + 1) * HD)
                        o = bank[6 + s % 2][rows, 0:2 * P].rearrange("p (n d) -> p n d", n=2)[:, :, half * HD:(half + 1) * HD]
                        r = na_st[rows, 8 + 2 * (s % 2):10 + 2 * (s % 2)].unsqueeze(2).to_broadcast([HD, 2, HD])
                        nc.vector.tensor_tensor(na_o[g % 2][rows, 2 * (s % 2):2 * (s % 2) + 2], o, r, ALU.mult).then_inc(o_evac, 1)

                for s in range(NSTEP + 2):
                    if s < NSTEP:
                        scores(s)
                    if 1 <= s <= NSTEP:
                        evac_pT(s - 1)
                    if s >= 2:
                        evac_o(s - 2)

            first_then_loop(dve, NPAIR, head_pair)

            def scale_y(i, j):
                dve.wait_ge(x_rs[j], NT // 2 + i + 1)
                nc.vector.tensor_scalar(y_cat[j][:, HALF:], y_cat[j][:, HALF:], rs[:, j:j + 1], None, ALU.mult).then_inc(yb_ready[j], 1)

            def gain_evac(dst, n, gain, done):
                g = gain[:, 4 * n:4 * n + 4].unsqueeze(2).to_broadcast([P, 4, P])
                nc.vector.tensor_tensor(dst, bank[n][:].rearrange("p (k t) -> p k t", k=4), g, ALU.mult).then_inc(done, 1)

            def evac_yT(i, j):
                dve.wait_ge(yt_done[j], i + 1)
                dve.wait_ge(wo_done, 2 * i)
                for n in range(2):
                    gain_evac(y_T[j][:, 4 * n:4 * n + 4], n, g_out, yT_evac)

            scale_y(0, 0)
            evac_yT(0, 0)

            def add_rows(i, j, last):
                if not last:
                    nxt = (i, 1) if j == 0 else (i + 1, 0)
                    scale_y(*nxt)
                    evac_yT(*nxt)
                t = 2 * i + j
                dve.wait_ge(wo_done, t + 1)
                dve.wait_ge(xr_here[j], 32 * (i + 1))
                for n in range(2):
                    cols = slice(n * HALF, (n + 1) * HALF)
                    nc.vector.tensor_tensor(H[:, t, cols], bank[2 + 2 * j + n][:], x_res[j][:, cols], ALU.add).then_inc(h_added[j], 1)

            tiles(dve, add_rows)

            for what, n in order:
                if what == "pre":
                    dve.wait_ge(n_rs, n + 1)
                    src = mem_in[n % 2] if norms[n][0] == "mem" else H[:, norms[n][1]]
                    nc.vector.tensor_scalar(hs[n % 2], src, rs[:, 4 + n % 2:5 + n % 2], None, ALU.mult).then_inc(n_ready, 1)
                elif what == "T":
                    kind, t = norms[n]
                    dve.wait_ge(nt_done, n + 1)
                    if kind == "mem":
                        dst, gain = mem_T[:, :, t * P:(t + 1) * P], g_mem
                    elif kind == "h":
                        if t % TPC == 0 and t > 0:
                            dve.wait_ge(mm_done, n_groups["q", t // TPC - 1, XH - 1] + 1)
                        dst, gain = h_T[:, :, (t % TPC) * P:(t % TPC + 1) * P], g_xattn
                    else:
                        if t >= 2:
                            dve.wait_ge(mm_done, n_groups["route", t - 2] + 1)
                        dst, gain = r_T[t % 2], g_moe
                    for b in range(2):
                        gain_evac(dst[:, 4 * b:4 * b + 4], b, gain, nt_evac)
                elif what == "mm":
                    kind, *which = groups[n]
                    dve.wait_ge(mm_done, n + 1)
                    b = bank[4 + n % 2]
                    if kind == "xo":
                        t, half = which
                        cols = slice(half * HALF, (half + 1) * HALF)
                        nc.vector.tensor_tensor(H[:, t, cols], H[:, t, cols], b[:], ALU.add).then_inc(mm_evac, 1)
                    elif kind == "route":
                        nc.vector.tensor_copy(logit[:, which[0]], b[:, 0:NG + NE]).then_inc(mm_evac, 1)
                    else:
                        dst = {"k_mem": lambda: k_mem[:, which[0]], "v_mem": lambda: v_mem[:, which[0]],
                               "q": lambda: q_x[which[0] % 2][:, which[1]], "o": lambda: o_T[:, which[1]]}[kind]()
                        nc.vector.tensor_copy(dst, b[:]).then_inc(mm_evac, 1)
                elif what == "S":
                    k = 2 * (n % 4)
                    dve.wait_ge(sx_done, n + 1)
                    if n >= 4:
                        dve.wait_ge(px_ready, n - 3)
                    nc.vector.tensor_reduce(xa_st[:, k:k + 2], bank[6 + n % 2][:].rearrange("p (h m) -> p h m", h=2), AX, ALU.max).then_inc(sx_max, 1)
                    dve.wait_ge(sx_max, n + 1)
                    nc.vector.tensor_scalar(xa_st[:, 8 + k:10 + k], xa_st[:, k:k + 2], -XA_SCALE, None, ALU.mult).then_inc(sx_neg, 1)
                elif what == "px":
                    k = 2 * (n % 4)
                    dve.wait_ge(px_exp, 2 * (n + 1))
                    nc.vector.reciprocal(xa_st[:, 24 + k:26 + k], xa_st[:, 16 + k:18 + k]).then_inc(sx_rcp, 1)
                    dve.wait_ge(sx_rcp, n + 1)
                    r = xa_st[:, 24 + k:26 + k].unsqueeze(2).to_broadcast([P, 2, N_MEM])
                    nc.vector.tensor_tensor(p_x[n % 4], p_x[n % 4], r, ALU.mult).then_inc(px_ready, 1)

            done = [0]

            def step(ins):
                done[0] += 1
                ins.then_inc(route, 1)
                dve.wait_ge(route, done[0])

            def over_tokens(v, n):
                return v.unsqueeze(2).to_broadcast([P, NT, n])

            def first_max(out, scores, peak, order_of, tmp, best):
                n = scores.shape[-1]
                step(nc.vector.tensor_tensor(tmp, scores, over_tokens(peak, n), ALU.is_equal))
                step(nc.vector.tensor_tensor(tmp, tmp, order_of.unsqueeze(1).to_broadcast([P, NT, n]), ALU.mult))
                step(nc.vector.tensor_reduce(best, tmp, AX, ALU.max))
                step(nc.vector.tensor_tensor(out, tmp, over_tokens(best, n), ALU.is_equal))

            dve.wait_ge(route_const, 10)
            dve.wait_ge(mm_evac, len(groups))
            dve.wait_ge(mm_done, len(groups))
            lg, le = logit[:, :, 0:NG], logit[:, :, NG:]
            g_max, g_best, g_sum, g_top, e_max, e_best, e_max2, e_best2 = rs1[:8]
            e_diff, e_exp, e_sum, e_rcp = rs1[8:12]
            g_one = rs8[4][:, :, 0:NG]
            step(nc.vector.tensor_reduce(g_max, lg, AX, ALU.max))
            nc.vector.tensor_tensor(rs8[0][:, :, 0:NG], lg, over_tokens(g_max, NG), ALU.subtract).then_inc(route_exp, 1)
            first_max(g_one, lg, g_max, first_g, rs8[3][:, :, 0:NG], g_best)
            by_group = "p t (g e) -> p t g e"
            step(nc.vector.tensor_tensor(rt[0].rearrange(by_group, g=NG), le.rearrange(by_group, g=NG),
                                         g_one.unsqueeze(3).to_broadcast([P, NT, NG, EPG]), ALU.mult))
            e_sel, e_sel2, one1, one2 = rs8[5], rs8[6], rs8[9], rs8[11]
            step(nc.vector.tensor_reduce(e_sel, rt[0].rearrange("p t (g e) -> p t e g", g=NG), AX, ALU.add))
            step(nc.vector.tensor_reduce(e_max, e_sel, AX, ALU.max))
            first_max(one1, e_sel, e_max, first_e, rs8[7], e_best)
            step(nc.vector.scalar_tensor_tensor(e_sel2, one1, -3.0e38, e_sel, ALU.mult, ALU.add))
            step(nc.vector.tensor_reduce(e_max2, e_sel2, AX, ALU.max))
            first_max(one2, e_sel2, e_max2, first_e, rs8[8], e_best2)
            nc.vector.tensor_tensor(e_diff, e_max2, e_max, ALU.subtract).then_inc(route_exp, 1)
            for k, one in ((0, one1), (1, one2)):
                step(nc.vector.tensor_tensor(rt[1 + k].rearrange(by_group, g=NG), g_one.unsqueeze(3).to_broadcast([P, NT, NG, EPG]),
                                             one.unsqueeze(2).to_broadcast([P, NT, NG, EPG]), ALU.mult))
            nc.vector.tensor_tensor(rt[3], rt[1], rt[2], ALU.add).then_inc(chosen, 1)
            dve.wait_ge(exp_done, 2)
            step(nc.vector.tensor_reduce(g_sum, rs8[1][:, :, 0:NG], AX, ALU.add))
            step(nc.vector.reciprocal(g_top, g_sum))
            step(nc.vector.tensor_scalar(e_sum, e_exp, 1.0, None, ALU.add))
            step(nc.vector.reciprocal(e_rcp, e_sum))
            step(nc.vector.tensor_tensor(gate[:, 0], g_top, e_rcp, ALU.mult))
            step(nc.vector.tensor_tensor(gate[:, 1], gate[:, 0], e_exp, ALU.mult))
            earlier, rank, count = rt[5], rt[4], re[0]
            step(nc.vector.memset(earlier[:, 0], 0.0))
            dve.wait_ge(count_done, 1)
            per_tile = bank[3][:, 0:NT * NE].rearrange("p (t e) -> p t e", t=NT)
            for t in range(1, NT):
                step(nc.vector.tensor_tensor(earlier[:, t], per_tile[:, t - 1], earlier[:, t - 1], ALU.add))
            step(nc.vector.tensor_tensor(count, per_tile[:, NT - 1], earlier[:, NT - 1], ALU.add))
            step(nc.vector.tensor_tensor(rank, bank[2][:, 0:NT * NE].rearrange("p (t e) -> p t e", t=NT), earlier, ALU.add))
            n_over, over_incl, over_at, shift = re[1], re[2], re[3], re[4]
            step(nc.vector.tensor_tensor(r11, count.unsqueeze(2).to_broadcast([P, NE, NT - 1]),
                                         iota_j.unsqueeze(1).to_broadcast([P, NE, NT - 1]), ALU.is_gt))
            step(nc.vector.tensor_reduce(n_over, r11, AX, ALU.add))
            step(nc.vector.tensor_tensor_scan(over_incl, ones[:, 0:NE], n_over, 0.0, ALU.mult, ALU.add))
            step(nc.vector.tensor_tensor(over_at, over_incl, n_over, ALU.subtract))
            step(nc.vector.tensor_scalar(shift, over_at, float(P), float(P * (NE - 1)), ALU.mult, ALU.add))
            step(nc.vector.tensor_tensor(re[5], shift, iota_e, ALU.subtract))
            step(nc.vector.tensor_scalar(rt[6], rank, float(P), None, ALU.is_ge))
            step(nc.vector.tensor_tensor(rt[7], rt[6], re[5].unsqueeze(1).to_broadcast([P, NT, NE]), ALU.mult))
            step(nc.vector.tensor_tensor(rt[8], rt[7], rank, ALU.add))
            step(nc.vector.tensor_tensor(rt[9], rt[8], iota_e.unsqueeze(1).to_broadcast([P, NT, NE]), ALU.add))
            for k in range(2):
                step(nc.vector.tensor_tensor(rt[6 + k], rt[1 + k], rt[9], ALU.mult))
                step(nc.vector.tensor_reduce(rs1[12 + k], rt[6 + k], AX, ALU.add))
                nc.vector.tensor_copy(slot[:, k], rs1[12 + k]).then_inc(slot_ready, 1)
            step(nc.vector.tensor_tensor(r23, over_incl.unsqueeze(1).to_broadcast([P, NOVER, NE]),
                                         iota_b.unsqueeze(2).to_broadcast([P, NOVER, NE]), ALU.is_le))
            step(nc.vector.tensor_reduce(over_f, r23, AX, ALU.add))
            step(nc.vector.tensor_scalar(over_e, over_f, float(NE - 1), None, ALU.min))
            step(nc.vector.tensor_copy(over_n, over_incl[:, NE - 1:NE]))
            dve.wait_ge(table_here, 16)
            nc.vector.tensor_copy(slot_rows_f[0:NBLK], slot_rows[0:NBLK]).then_inc(rows_f, 1)
            dve.wait_ge(rows_T, 1)
            nc.vector.tensor_copy(slot_src, bank[2][:, 0:NBLK]).then_inc(table_ready, 1)

            def evac_xg(b, n):
                dve.wait_ge(xgt_done, b + 1)
                for k in range(2):
                    gain_evac(x_gT[n % 2][:, 4 * k:4 * k + 4], k, g_moe, xgt_evac)

            def expert(b, half, n, r, ahead):
                if ahead:
                    evac_xg(b + 1, n + 1)
                dve.wait_ge(e_silu, b + 1)
                nc.vector.tensor_tensor(act_e[n % 2], silu_g, bank[2][:, FE:2 * FE], ALU.mult).then_inc(e_act, 1)
                dve.wait_ge(et_done, b + 1)
                nc.vector.tensor_copy(act_T[n % 2], bank[4][:, 0:P]).then_inc(et_evac, 1)
                dve.wait_ge(y_done, b + 1)
                dve.wait_ge(y_sent[n % 2], 16 * half)
                nc.vector.tensor_copy(y_st[n % 2][:, HALF:], bank[6][:]).then_inc(y_evac_v, 1)

            evac_xg(0, 0)
            expert_blocks(dve, lambda b, half, n, r, last: expert(b, half, n, r, not last))

            def expert_overflow(b, half, n, r):
                evac_xg(b, n)
                expert(b, half, n, r, False)

            overflow_blocks(dve, expert_overflow)

            dve.wait_ge(gf_here, 16)

            def add_experts(t):
                dve.wait_ge(yg_here[t % 2], 32 * (t // 2 + 1))
                for k in range(2):
                    if k == 1:
                        dve.wait_ge(f_add, 2 * t + 1)
                    nc.vector.scalar_tensor_tensor(H[:, t], y_g[t % 2][k], gate[:, k, t:t + 1], H[:, t], ALU.mult, ALU.add).then_inc(f_add, 1)

            add_experts(0)
            for t in range(NT):
                if t + 1 < NT:
                    add_experts(t + 1)
                dve.wait_ge(n_rs, len(norms) + t + 1)
                n = len(norms) + t
                nc.vector.scalar_tensor_tensor(out_st[t % 2], H[:, t], rs[:, 4 + n % 2:5 + n % 2], gf_row, ALU.mult, ALU.mult).then_inc(f_out, 1)

        @blk.tensor
        def _(pe):
            def transposes(banks, src, blocks, done, waits=()):
                for s, w in waits:
                    pe.wait_ge(s, w)
                for k in range(blocks):
                    last = nc.tensor.transpose(banks[k // 4][:, (k % 4) * P:(k % 4 + 1) * P], src(k), ident)
                last.then_inc(done, 1)

            pe.wait_ge(ident_made, 2)
            pe.wait_ge(sgu_w_here, 16)
            for n in range(2):
                for h in range(4 * n, 4 * n + 4):
                    last = nc.tensor.transpose(bank[n][:, (h % 4) * P:(h % 4 + 1) * P], sgu_nat[:, h], ident)
                last.then_inc(sgu_t, 1)
            pe.wait_ge(sgu_evac, 2)

            def transpose_x(i, j):
                pe.wait_ge(xs_ready[j], i + 1)
                pe.wait_ge(xf_evac, 2 * (2 * i + j))
                for k in range(KT):
                    last = nc.tensor.transpose(bank[k // 4][:, (k % 4) * P:(k % 4 + 1) * P], xs[j][:, k * P:(k + 1) * P], ident)
                last.then_inc(xt_done[j], 1)

            def project(i, j, out, w, done):
                for k in range(KT):
                    last = nc.tensor.matmul(out[:], xf[j][:, k], w[:, k], start=(k == 0), stop=(k == KT - 1))
                last.then_inc(done, 1)

            transpose_x(0, 0)

            def tile_work(i, j, last):
                t = 2 * i + j
                pe.wait_ge(xf_evac, 2 * (t + 1))
                pe.wait_ge(w_in_here[1], 16)
                pe.wait_ge(v_gelu, t)
                project(i, j, bank[2], w_uvv[1], v_done)
                pe.wait_ge(w_in_here[0], 16)
                pe.wait_ge(u_gelu, t)
                project(i, j, bank[3], w_uvv[0], u_done)
                if j == 0:
                    transpose_x(i, 1)
                elif not last:
                    transpose_x(i + 1, 0)
                pe.wait_ge(w_in_here[2], 16)
                pe.wait_ge(att_copied, t)
                project(i, j, bank[4], w_uvv[2], att_done)
                pe.wait_ge(vn_ready, t + 1)
                pe.wait_ge(mix_bias, t)
                for h in range(NH):
                    mm = nc.tensor.matmul(bank[5][:, h * HD:(h + 1) * HD], sgu_wT[:, h], v_n[:, h * HD:(h + 1) * HD],
                                          start=True, stop=True)
                mm.then_inc(mix_done, 1)

            tiles(pe, tile_work)

            for j in range(2):
                pe.wait_ge(xT_copied[j], NT // 2)
            pe.wait_ge(mix_bias, NT)
            pe.wait_ge(att_copied, NT)
            def channel_tiles(i):
                for j in range(2):
                    pe.wait_ge(w_qk_here[j], 16 * (i + 1))
                    pe.wait_ge(qk_evac_v[j], 2 * i)
                    pe.wait_ge(qk_evac_s[j], i)
                    for n in range(NCH):
                        for k in range(KT):
                            last = nc.tensor.matmul(bank[3 * j + n][:], w_qk[j][:, k], xT[:, k, n * CH:(n + 1) * CH],
                                                    start=(k == 0), stop=(k == KT - 1))
                    last.then_inc(qk_done[j], 1)

            first_then_loop(pe, NH // 2, channel_tiles)

            for j in range(2):
                pe.wait_ge(qk_evac_v[j], NH)
                pe.wait_ge(qk_evac_s[j], NH // 2)
            def head_pair(hp):
                base = NSTEP * hp

                def scores(s):
                    g = s // 2
                    keys = NA_GROUPS[g][0]
                    if s % 2 == 0:
                        pe.wait_ge(diag_ready, 2 * (NKG * hp + g + 1))
                    pe.wait_ge(s_biased, 2 * (base + s) - 2 if s >= 1 else 2 * base)
                    for n in range(2):
                        block = 2 * (s % 2) + n
                        q = q_diag[g % 2][:, block].rearrange("p h r c -> p (h r c)")
                        row0 = keys[0] * QROWS
                        k = qk[:, NPAIR + hp].rearrange("p (r c) -> p r c", c=GW)
                        k = k[:, row0:row0 + QROWS * len(keys), COL_START[block]:COL_START[block] + KC]
                        nc.tensor.matmul(bank[2 * (s % 2) + n][:, 0:P * len(keys)], q, k, start=True, stop=True).then_inc(s_done, 1)

                def transpose_p(s):
                    nk = len(NA_GROUPS[s // 2][0])
                    pe.wait_ge(p_exp, 2 * (base + s + 1))
                    pe.wait_ge(pt_evac_s, base + s)
                    pe.wait_ge(pt_evac_v, base + s)
                    for n in range(2):
                        for k in range(nk):
                            last = nc.tensor.transpose(bank[4 + n][:, k * P:(k + 1) * P], na_p[s % 2][:, n, k * P:(k + 1) * P], ident)
                    last.then_inc(pt_done, 1)

                def values(s):
                    keys = NA_GROUPS[s // 2][0]
                    pe.wait_ge(pt_evac_s, base + s + 1)
                    pe.wait_ge(pt_evac_v, base + s + 1)
                    pe.wait_ge(vals_here, 16 * 4 * NKG)
                    pe.wait_ge(o_evac, 2 * (base + s - 1) if s >= 1 else 2 * base)
                    for n in range(2):
                        for k, kg in enumerate(keys):
                            last = nc.tensor.matmul(bank[6 + s % 2][:, n * P:(n + 1) * P], na_pT[s % 2][:, n, k * P:(k + 1) * P],
                                                    vals[:, 4 * kg + 2 * (s % 2) + n, bass.ds(hp * P, P)],
                                                    start=(k == 0), stop=(k == len(keys) - 1))
                    last.then_inc(o_done, 1)

                for s in range(NSTEP + 2):
                    if s < NSTEP:
                        scores(s)
                    if 1 <= s <= NSTEP:
                        transpose_p(s - 1)
                    if s >= 2:
                        values(s - 2)

            first_then_loop(pe, NPAIR, head_pair)

            for j in range(2):
                pe.wait_ge(na_stored[j], 16 * 2 * NPAIR * NKG // 2)

            def transpose_y(i, j):
                pe.wait_ge(yb_ready[j], i + 1)
                pe.wait_ge(yT_evac, 2 * (2 * i + j))
                for k in range(KT):
                    last = nc.tensor.transpose(bank[k // 4][:, (k % 4) * P:(k % 4 + 1) * P], y_cat[j][:, k * P:(k + 1) * P], ident)
                last.then_inc(yt_done[j], 1)

            transpose_y(0, 0)

            def out_tile(i, j, last):
                if j == 0:
                    transpose_y(i, 1)
                elif not last:
                    transpose_y(i + 1, 0)
                t = 2 * i + j
                pe.wait_ge(w_out_here, 16)
                pe.wait_ge(yT_evac, 2 * (t + 1))
                pe.wait_ge(h_added[j], 2 * i)
                for n in range(2):
                    for k in range(KT):
                        mm = nc.tensor.matmul(bank[2 + 2 * j + n][:], y_T[j][:, k], w_out[:, k, n * HALF:(n + 1) * HALF],
                                              start=(k == 0), stop=(k == KT - 1))
                mm.then_inc(wo_done, 1)

            tiles(pe, out_tile)
            for j in range(2):
                pe.wait_ge(h_added[j], NT)

            for what, n in stages:
                if what == "T":
                    pe.wait_ge(n_ready, n + 1)
                    pe.wait_ge(nt_evac, 2 * n)
                    for k in range(KT):
                        last = nc.tensor.transpose(bank[k // 4][:, (k % 4) * P:(k % 4 + 1) * P], hs[n % 2][:, k * P:(k + 1) * P], ident)
                    last.then_inc(nt_done, 1)
                elif what == "mm":
                    kind, *which = groups[n]
                    b = bank[4 + n % 2]
                    if n >= 2:
                        pe.wait_ge(mm_evac, n - 1)
                    if kind == "k_mem":
                        pe.wait_ge(w_xkv_here, 16)
                        pe.wait_ge(nt_evac, 2 * 4)
                        h = which[0]
                        steps = [(w_xkv[:, k, h * P:(h + 1) * P], mem_T[:, k]) for k in range(KT)]
                    elif kind == "v_mem":
                        m = which[0]
                        steps = [(mem_T[:, k, m * P:(m + 1) * P], w_xkv[:, k, HALF:]) for k in range(KT)]
                    elif kind == "q":
                        c, h = which
                        pe.wait_ge(w_xq_here, 16)
                        pe.wait_ge(nt_evac, 2 * (n_norms["h", TPC * c + TPC - 1] + 1))
                        steps = [(w_xq[:, k, h * P:(h + 1) * P], h_T[:, k]) for k in range(KT)]
                    elif kind == "o":
                        c, h = which
                        pe.wait_ge(ptx_evac, 8 * (c + 1))
                        seq = 0 if c * CH < SEQ_P else 1
                        steps = [(v_mem[:, 2 * seq + m, h * P:(h + 1) * P], pT_x[:, h, m]) for m in range(2)]
                    elif kind == "xo":
                        t, half = which
                        pe.wait_ge(w_xo_here, 16)
                        pe.wait_ge(mm_evac, n_groups["o", t // TPC, XH - 1] + 1)
                        q = t % TPC
                        steps = [(o_T[:, h, q * P:(q + 1) * P], w_xo[:, h, half * HALF:(half + 1) * HALF]) for h in range(XH)]
                    else:
                        t = which[0]
                        pe.wait_ge(w_rt_here, 32)
                        pe.wait_ge(nt_evac, 2 * (n_norms["moe", t] + 1))
                        b = b[:, 0:NG + NE]
                        steps = [(r_T[t % 2][:, k], w_rt[:, k]) for k in range(KT)]
                    for k, (w, x) in enumerate(steps):
                        mm = nc.tensor.matmul(b if kind == "route" else b[:], w, x, start=(k == 0), stop=(k == len(steps) - 1))
                    mm.then_inc(mm_done, 1)
                elif what == "S":
                    c, t, hp = n // 8, (n % 8) // 2, n % 2
                    seq = 0 if c * CH < SEQ_P else 1
                    pe.wait_ge(mm_evac, n_groups["q", c, XH - 1] + 1)
                    if n >= 2:
                        pe.wait_ge(px_exp, 2 * (n - 1))
                    for h in (2 * hp, 2 * hp + 1):
                        mm = nc.tensor.matmul(bank[6 + n % 2][:, (h % 2) * N_MEM:(h % 2 + 1) * N_MEM],
                                              q_x[c % 2][:, h, t * P:(t + 1) * P], k_mem[:, h, seq * N_MEM:(seq + 1) * N_MEM],
                                              start=True, stop=True)
                    mm.then_inc(sx_done, 1)
                elif what == "PT":
                    pe.wait_ge(px_ready, n + 1)
                    if n >= 2:
                        pe.wait_ge(ptx_evac, n - 1)
                    for h in range(2):
                        for m in range(2):
                            last = nc.tensor.transpose(bank[2 + n % 2][:, (2 * h + m) * P:(2 * h + m + 1) * P],
                                                       p_x[n % 4][:, h, m * P:(m + 1) * P], ident)
                    last.then_inc(ptx_done, 1)

            pe.wait_ge(route_const, 10)
            pe.wait_ge(chosen, 1)
            pe.wait_ge(ptx_evac, 8 * NCH)
            flat = rt[3].rearrange("p t e -> p (t e)")
            nc.tensor.matmul(bank[2][:, 0:NT * NE], before, flat, start=True, stop=True)
            nc.tensor.matmul(bank[3][:, 0:NT * NE], ones, flat, start=True, stop=True).then_inc(count_done, 1)
            pe.wait_ge(rows_f, 1)
            nc.tensor.transpose(bank[2][:, 0:NBLK], slot_rows_f[0:NBLK], ident[0:NBLK, 0:NBLK]).then_inc(rows_T, 1)
            pe.wait_ge(table_ready, 1)

            def transpose_xg(b, half, n):
                pe.wait_ge(xg_here[n % 2], 16 * (half + 1))
                pe.wait_ge(xgt_evac, 2 * b)
                for k in range(KT):
                    last = nc.tensor.transpose(bank[k // 4][:, (k % 4) * P:(k % 4 + 1) * P], x_g[n % 2][:, k * P:(k + 1) * P], ident)
                last.then_inc(xgt_done, 1)

            def expert(b, half, n, r, ahead):
                pe.wait_ge(xgt_evac, 2 * (b + 1))
                pe.wait_ge(w_e_here[n], 48 * (r + 1))
                for k in range(KT):
                    mm = nc.tensor.matmul(bank[2][:, 0:2 * FE], x_gT[n % 2][:, k], w_gu[n][:, :, k], start=(k == 0), stop=(k == KT - 1))
                mm.then_inc(gu_done, 1)
                if ahead:
                    transpose_xg(b + 1, half + n % 2, n + 1)
                pe.wait_ge(e_act, b + 1)
                nc.tensor.transpose(bank[4][:, 0:P], act_e[n % 2], ident).then_inc(et_done, 1)
                pe.wait_ge(et_evac, b + 1)
                pe.wait_ge(y_evac_s, b)
                pe.wait_ge(y_evac_v, b)
                for k in range(2):
                    mm = nc.tensor.matmul(bank[5 + k][:], act_T[n % 2], w_dn[n][:, k * HALF:(k + 1) * HALF], start=True, stop=True)
                mm.then_inc(y_done, 1)

            transpose_xg(0, 0, 0)
            expert_blocks(pe, lambda b, half, n, r, last: expert(b, half, n, r, not last))

            def expert_overflow(b, half, n, r):
                transpose_xg(b, half, n)
                expert(b, half, n, r, False)

            overflow_blocks(pe, expert_overflow)

        return nc


INPUTS = ["x_prompt", "x_sample", "mem_prompt", "mem_sample", "g_mix", "w_in", "g_sgu_v", "sgu_w", "sgu_b", "na_rpb",
          "g_out_a", "g_out_b", "w_out", "g_xattn", "g_mem", "w_xq", "w_xkv", "w_xo", "g_moe", "w_router_group",
          "w_router_expert", "w_exp_gate", "w_exp_up", "w_exp_down", "g_final"]


def kernel(**inputs):
    import numpy as np
    import concourse.bacc as bacc
    from concourse.bass_utils import run_bass_kernel_spmd

    nc = bacc.Bacc("TRN2", target_bir_lowering=False, num_devices=1)
    arrays, aps = {}, {}
    for name in INPUTS:
        v = np.ascontiguousarray(inputs[name])
        arrays[f"in_{name}"] = v
        aps[name] = nc.dram_tensor(f"in_{name}", v.shape, mybir.dt.from_np(v.dtype), kind="ExternalInput").ap()
    outs = [nc.dram_tensor(f"out_{n}", (1, rows, D), F32, kind="ExternalOutput").ap() for n, rows in (("prompt", SEQ_P), ("sample", SEQ_S))]
    hymba_encoder(nc, aps, *outs)
    r = run_bass_kernel_spmd(nc, [arrays], core_ids=[0])
    return tuple(r.results[0][n] for n in ("out_prompt", "out_sample"))
```

```python
import concourse.bass as bass
from concourse import mybir
from contextlib import ExitStack

F32 = mybir.dt.float32
F32R = mybir.dt.float32r
I32 = mybir.dt.int32
ALU = mybir.AluOpType
ACT = mybir.ActivationFunctionType
AX = mybir.AxisListType.X

P = 128
D = 1024
KT = D // P
SEQ_P, SEQ_S = 512, 1024
T = SEQ_P + SEQ_S
NT = T // P
CH = 512
NCH = T // CH
N_MEM = 256
HALF = 512
NH = 8
HD = 64
NPAIR = NH // 2
GW = 64
KC = 32
QC = 16
QROWS = 4
GTOK = QROWS * GW
NKG = T // GTOK
KREL = 12
XH = 4
NG, EPG = 4, 8
NE = NG * EPG
FE = 128
EPS = 1e-6
MASKED = -1.0e30
NA_SCALE = HD ** -0.5
XA_SCALE = P ** -0.5
NA_GROUPS = [((0, 1), 4, False), ((0, 1), 0, False),
             ((2, 3), 4, False), ((2, 3, 4), 0, True), ((3, 4, 5), 0, True), ((4, 5), 0, False)]
COL_START = [0, 8, 24, 32]
NOVER = (2 * T + NE * (P - 1)) // P - NE
NOVER += 4 - NOVER % 4
NBLK = NE + NOVER
RING = 8


def hymba_encoder(nc, a, y_prompt, y_sample):
    ctx = ExitStack()
    with ctx:
        def sem(name):
            return ctx.enter_context(nc.semaphore(name))

        def pair(name):
            return [sem(f"{name}_{j}") for j in range(2)]

        used = [0]

        def at(kb, *shape, dt=F32):
            used[0] += 1
            base = nc.sbuf_base + (-nc.sbuf_base) % 32
            return nc.alloc_sbuf_tensor_at(f"at_{kb}_{used[0]}".replace(".", "_"), [P, *shape], dt, offset=base + int(kb * 1024))[:]

        bank = [ctx.enter_context(nc.psum_tensor(f"bank{i}", [P, 512], F32)) for i in range(8)]

        def dram(name, shape, dt=F32):
            return nc.dram_tensor(name, shape, dt, kind="Internal").ap()

        y_mix = dram("y_mix", [T, 2 * HALF])
        v_att = dram("v_att", [T, HALF])
        rpb_pad = dram("rpb_pad", [NH * 15, 96])
        xn_moe = dram("xn_moe", [T, D])
        slot_tok = dram("slot_tok", [NBLK * P, 1], I32)
        y_exp = dram("y_exp", [NBLK * P, D])

        ident = at(192, P)
        small = at(192.5, 384)
        g_mix, g_xattn, g_mem, g_moe, g_out = (small[:, 8 * n:8 * n + 8] for n in range(5))
        sgu_b = small[:, 40:48]
        neg_half = small[:, 48:49]
        eps = small[:, 49:50]
        ms = small[:, 64:96]
        ms_eps = small[:, 96:128]
        rs = small[:, 128:160]
        na_st = small[:, 160:192]
        xa_st = small[:, 192:224]
        w_uvv = [at(16 * n, KT, HALF) for n in range(3)]
        xT = at(48, KT, T)
        x_in = [at(144 + 4 * j, D) for j in range(2)]
        w_uvv_lo = [at(16 * n, KT, HALF, dt=F32R) for n in range(3)]
        w_uvv_hi = [at(96 + 16 * n, KT, HALF, dt=F32R) for n in range(3)]
        x_hi = [at(152 + 4 * j, KT, P, dt=F32R) for j in range(2)]
        x_lo = [at(160 + 4 * j, KT, P, dt=F32R) for j in range(2)]
        v_g, v_n, u_g, mixed, y_a = (at(168 + 2 * n, HALF) for n in range(5))
        y_an = [at(178 + 2 * j, HALF) for j in range(2)]
        v_st = [at(182 + 2 * j, HALF) for j in range(2)]
        sq_junk = at(186, HALF)
        x_junk0, x_junk = at(168, D), at(188, D)
        sgu_nat = at(188, NH, P)
        sgu_wT = at(194, NH, P)
        gv_row = at(198, HALF)
        na_bias = at(96, NPAIR, 3, KREL, KC)
        na_bias_row = at(114, NPAIR, 3, KREL, KC)
        w_qk = [at(132 + 4 * j, KT, P) for j in range(2)]
        w_qk_hi = [at(kb, KT, P, dt=F32R) for kb in (140, 194)]
        w_qk_lo = [at(132 + 4 * j, KT, P, dt=F32R) for j in range(2)]
        xT_hi = at(0, KT, T, dt=F32R)
        xT_lo = at(48, KT, T, dt=F32R)
        bias_src = at(200, 3, 15, KC)
        pad_t = at(206, 96)
        qk = at(144, NH, T)
        vals = at(0, NKG * 4, HALF)
        q_diag = [at(132 + 2 * j, 4, 2, QROWS, QC) for j in range(2)]
        na_o = [at(136 + j, 4, HD) for j in range(2)]
        na_p = [at(138 + 3 * j, 2, KREL * KC) for j in range(2)]
        na_pT = [at(194 + 3 * j, 2, KREL * KC) for j in range(2)]

        H = at(0, NT, D)
        w_out = [at(48 + 16 * n, KT, HALF) for n in range(2)]
        w_out_hi = [at(kb, KT, HALF, dt=F32R) for kb in (80, 128)]
        w_out_lo = [at(48 + 16 * n, KT, HALF, dt=F32R) for n in range(2)]
        y_cat = [at(96 + 4 * j, D) for j in range(2)]
        x_res = [at(104 + 4 * j, D) for j in range(2)]
        y_T = [at(112 + 4 * j, KT, P) for j in range(2)]
        y_hi = [at(176 + 4 * j, KT, P, dt=F32R) for j in range(2)]
        y_lo = [at(112 + 4 * j, KT, P, dt=F32R) for j in range(2)]
        yb_junk = at(198, HALF)
        mem_in = [at(120 + 4 * j, D) for j in range(2)]
        w_xkv = at(144, KT, D)
        mem_T = at(176, KT, 4 * P)
        k_mem = at(128, XH, 4 * P)
        v_mem = at(136, 4, HALF)
        hs = [at(194 + 4 * j, D) for j in range(2)]
        w_xq = at(80, KT, HALF)
        w_xo = at(144, XH, D)
        h_T = at(48, KT, CH)
        q_x = [at(160, XH, CH), at(96 + 24, XH, CH)]
        p_x = [at(72 + 2 * n, 2, N_MEM) for n in range(4)]
        pT_x = at(96, XH, 2, CH)
        o_T = at(112, XH, CH)
        r_T = [at(168 + 4 * j, KT, P) for j in range(2)]
        w_rt = at(202, KT, NG + NE)
        logit = at(203.25, NT, NG + NE)
        gate = at(205, 2, NT)
        slot = at(205.25, 2, NT, dt=I32)
        slot_src = at(205.5, NBLK, dt=I32)
        over_e = at(205.75, NOVER, dt=I32)
        token = at(206, NT, dt=I32)
        zeros = at(206.5, 256)
        over_n = at(206.25, 1, dt=I32)
        rt = [at(144 + 1.5 * n, NT, NE) for n in range(10)]
        rs8 = [at(160 + 0.375 * n, NT, EPG) for n in range(12)]
        rs1 = [at(164.5 + 0.0625 * n, NT) for n in range(16)]
        re = [at(165.5 + 0.125 * n, NE) for n in range(10)]
        r11 = at(176, NE, NT - 1)
        r23 = at(178, NOVER, NE)
        over_f = at(181, NOVER)
        iota_e = at(181.25, NE)
        iota_b = at(181.5, NOVER)
        iota_j = at(181.75, NT - 1)
        first_g = at(182, NG)
        first_e = at(182.25, EPG)
        before = at(182.5, P)
        ones = at(183, P)
        slot_rows = at(183.5, P, dt=I32)
        slot_rows_f = at(184, P)
        iota_i = at(184.5, P, dt=I32)
        zeros_i = at(185, P, dt=I32)
        slots_kb = [48 + 12 * n for n in range(RING)]
        w_gu = [at(kb, 2, KT, FE) for kb in slots_kb]
        w_dn = [at(kb + 8, D) for kb in slots_kb]
        x_g = [at(144 + 4 * j, D) for j in range(2)]
        x_gT = [at(152 + 4 * j, KT, P) for j in range(2)]
        silu_g = at(160, FE)
        act_e = [at(160.5 + 0.5 * j, FE) for j in range(2)]
        act_T = [at(161.5 + 0.5 * j, P) for j in range(2)]
        y_st = [at(164 + 4 * j, D) for j in range(2)]
        y_g = [[at(144 + 8 * j + 4 * n, D) for n in range(2)] for j in range(2)]
        out_st = [at(160 + 4 * j, D) for j in range(2)]
        gf_row = at(172, D)

        blk = ctx.enter_context(nc.Block())

        w_in_here = [sem(f"w_in_here_{n}") for n in range(3)]
        consts_here = sem("consts_here")
        sgu_w_here = sem("sgu_w_here")
        x_here = pair("x_here")
        w_qk_here = pair("w_qk_here")
        pad_here, bias_here = sem("pad_here"), sem("bias_here")
        vals_here = [sem(f"vals_here_{n}") for n in range(NKG // 2)]
        v_stored, ya_stored = pair("v_stored"), pair("ya_stored")
        na_stored = pair("na_stored")
        const_made, ident_made, fill_made, bias_neg = (sem(n) for n in ("const_made", "ident_made", "fill_made", "bias_neg"))
        x_sq, x_eps, x_rs, xs_ready, xt_done = (pair(n) for n in ("x_sq", "x_eps", "x_rs", "xs_ready", "xt_done"))
        xf_evac = sem("xf_evac")
        sgu_t, sgu_evac = sem("sgu_t"), sem("sgu_evac")
        v_done, u_done, v_gelu, u_gelu, v_sq, v_eps, v_rs, vn_ready, mix_done, mix_bias, ya_mul, ya_sq, ya_eps, ya_rs, yan_ready = (
            sem(n) for n in ("v_done", "u_done", "v_gelu", "u_gelu", "v_sq", "v_eps", "v_rs", "vn_ready", "mix_done",
                             "mix_bias", "ya_mul", "ya_sq", "ya_eps", "ya_rs", "yan_ready"))
        att_done, att_copied = sem("att_done"), sem("att_copied")
        qk_done, qk_evac_v, qk_evac_s = pair("qk_done"), pair("qk_evac_v"), pair("qk_evac_s")
        hi_made, lo_made = sem("hi_made"), sem("lo_made")
        diag_zero, diag_ready, s_done, s_biased, s_min, p_exp, s_rcp = (
            sem(n) for n in ("diag_zero", "diag_ready", "s_done", "s_biased", "s_min", "p_exp", "s_rcp"))
        pt_done, pt_evac_s, pt_evac_v, o_done, o_evac = (
            sem(n) for n in ("pt_done", "pt_evac_s", "pt_evac_v", "o_done", "o_evac"))

        w_out_here, w_xkv_here, w_xq_here, w_xo_here, w_rt_here = (sem(n) for n in ("w_out_here", "w_xkv_here", "w_xq_here", "w_xo_here", "w_rt_here"))
        y_here, xr_here = pair("y_here"), pair("xr_here")
        yb_ready, yt_done = pair("yb_ready"), pair("yt_done")
        yT_evac, wo_done, h_added = sem("yT_evac"), sem("wo_done"), pair("h_added")
        mem_here = pair("mem_here")
        n_sq, n_eps, n_rs, n_ready, nt_done, nt_evac = (sem(n) for n in ("n_sq", "n_eps", "n_rs", "n_ready", "nt_done", "nt_evac"))
        xn_stored = pair("xn_stored")
        mm_done, mm_evac = sem("mm_done"), sem("mm_evac")
        sx_done, sx_max, sx_neg, px_exp, sx_rcp, px_ready, ptx_done, ptx_evac = (
            sem(n) for n in ("sx_done", "sx_max", "sx_neg", "px_exp", "sx_rcp", "px_ready", "ptx_done", "ptx_evac"))
        route, route_exp, exp_done, chosen, route_const, count_done, slot_ready = (
            sem(n) for n in ("route", "route_exp", "exp_done", "chosen", "route_const", "count_done", "slot_ready"))
        table_dma, table_sent, rows_f, rows_T, table_ready = (
            sem(n) for n in ("table_dma", "table_sent", "rows_f", "rows_T", "table_ready"))
        w_e_here = [sem(f"w_e_here_{n}") for n in range(RING)]
        xg_here = pair("xg_here")
        xgt_done, xgt_evac, gu_done, e_silu, e_act, et_done, et_evac, y_done, y_evac_s, y_evac_v = (
            sem(n) for n in ("xgt_done", "xgt_evac", "gu_done", "e_silu", "e_act", "et_done", "et_evac", "y_done", "y_evac_s", "y_evac_v"))
        y_sent, all_sent, unused_filled = pair("y_sent"), sem("all_sent"), sem("unused_filled")
        f_add, f_out = sem("f_add"), sem("f_out")
        yg_here, out_sent = pair("yg_here"), pair("out_sent")

        TPC = CH // P
        norms = [("mem", n) for n in range(4)] + [("h", t) for t in range(NT)] + [("moe", t) for t in range(NT)]
        groups = []
        stages = []

        def mm(*group):
            stages.append(("mm", len(groups)))
            groups.append(group)

        def T_of(*norm):
            stages.append(("T", norms.index(norm)))

        def interleave(*lists):
            longest = max(len(calls) for calls in lists)
            for n in range(longest):
                for calls in lists:
                    for m in range(n * len(calls) // longest, (n + 1) * len(calls) // longest):
                        calls[m][0](*calls[m][1:])

        def routing_of(tiles):
            calls = [(T_of, "moe", tiles[0])]
            for t, nxt in zip(tiles, tiles[1:]):
                calls += [(mm, "route", t), (T_of, "moe", nxt)]
            return calls + [(mm, "route", tiles[-1])]

        def S(n):
            stages.append(("S", n))

        def PT(n):
            stages.append(("PT", n))

        for n in range(4):
            T_of("mem", n)
        interleave([(mm, "k_mem", h) for h in range(XH)] + [(mm, "v_mem", n) for n in range(4)],
                   [(T_of, "h", n) for n in range(TPC)])
        for h in range(XH):
            mm("q", 0, h)
        interleave([(S, n) for n in range(4)], [(T_of, "h", TPC + n) for n in range(TPC)])
        for c in range(NCH):
            if c > 0:
                for n in range(4):
                    S(8 * c + n)
            softmax = []
            for n in range(8):
                softmax.append((PT, 8 * c + n))
                if n < 4:
                    softmax.append((S, 8 * c + 4 + n))
            if c + 1 < NCH:
                interleave(softmax, [(mm, "q", c + 1, h) for h in range(XH)])
            else:
                interleave(softmax, routing_of(range(TPC, 2 * TPC)))
            for h in range(XH):
                mm("o", c, h)
            xo = [(mm, "xo", TPC * c + t, half) for t in range(TPC) for half in range(2)]
            if c == 0:
                interleave(xo, [(T_of, "h", 2 * TPC + n) for n in range(TPC)])
            elif c + 1 < NCH:
                interleave(xo, routing_of(range(TPC)))
            else:
                for call in xo[:3]:
                    call[0](*call[1:])
                last = 2 * TPC
                T_of("moe", last)
                for n, call in enumerate(xo[3:]):
                    call[0](*call[1:])
                    if n == 1:
                        mm("route", last)
                        T_of("moe", last + 1)
                    elif n == 3:
                        mm("route", last + 1)
                        T_of("moe", last + 2)
                mm("route", last + 2)
                T_of("moe", last + 3)
                mm("route", last + 3)
        place = {st: n for n, st in enumerate(stages)}
        sq_at, pre_at = {0: 0, 1: 0}, {0: 0}
        for n in range(2, len(norms)):
            sq_at[n] = place["T", n - 2] + 1
        for n in range(1, len(norms)):
            pre_at[n] = place["T", n - 1]
        for n, (kind, t) in enumerate(norms):
            if kind == "moe":
                after = place["mm", groups.index(("xo", t, 1))] + 1
                sq_at[n] = max(sq_at[n], after)
                pre_at[n] = max(pre_at[n], min(after + 1, place["T", n]))
        order = []
        scaled = 0
        for k, st in enumerate(stages):
            order += [("sq", n) for n in range(len(norms)) if sq_at[n] == k]
            order += [("pre", n) for n in range(len(norms)) if pre_at[n] == k]
            if st[0] == "PT":
                order += [("px", n) for n in range(scaled, st[1] + 1)]
                scaled = max(scaled, st[1] + 1)
            order.append(st)
            if st[0] == "S" and st[1] - 1 >= scaled:
                order += [("px", n) for n in range(scaled, st[1])]
                scaled = st[1]
        n_groups = {g: n for n, g in enumerate(groups)}
        n_norms = {g: n for n, g in enumerate(norms)}

        def expert_blocks(eng, body):
            rounds = NE // RING
            for n in range(RING):
                body(n, n // 2, n, 0)
            with eng.Fori(1, rounds - 1) as r:
                for n in range(RING):
                    body(RING * r + n, RING // 2 * r + n // 2, n, r)
            for n in range(RING):
                r = rounds - 1
                body(RING * r + n, RING // 2 * r + n // 2, n, r)

        def overflow_blocks(eng, body):
            used = eng.value_load(over_n[0:1, 0:1], min_val=0, max_val=NOVER)
            with eng.Fori(0, NOVER // 4) as i:
                for n in range(4):
                    with eng.If(used > 4 * i + n):
                        body(NE + 4 * i + n, NE // 2 + 2 * i + n // 2, n, NE // RING + i)

        NSTEP = 2 * NKG

        def na_steps():
            return [(2 * g + n, g, (2 * n, 2 * n + 1)) for g in range(NKG) for n in range(2)]

        def is_first(i, j):
            return isinstance(i, int) and i == 0 and j == 0

        W_UVV_PLACE = {1: 0, 0: 2, 2: 3}

        def split_x(t):
            return 1 if isinstance(t, int) and t == 0 else 3 + t

        def split_xT(n):
            return 3 + NT + (0 if n == 0 else n + 1)

        def split_w_qk(i, j):
            if is_first(i, j):
                return split_xT(0) + 1
            return 3 + NT + NCH + 2 * i + j

        def split_w_out(n):
            return 3 + NT + NCH + NH + n

        def split_y(t):
            return 3 + NT + NCH + NH + 2 + t

        def make_hi(act, place, hi, x):
            nc.scalar.activation(hi, x, ACT.Copy).then_inc(hi_made, 1)

        def make_lo(dve, place, lo, x, hi):
            dve.wait_ge(hi_made, place + 1)
            nc.vector.tensor_tensor(lo, x, hi.bitcast(F32), ALU.subtract).then_inc(lo_made, 1)

        def split_products(out, terms):
            for k, (w_hi, w_lo, x_hi, x_lo) in enumerate(terms):
                nc.tensor.matmul(out, w_hi, x_hi, start=(k == 0), stop=False)
                nc.tensor.matmul(out, w_lo, x_hi, start=False, stop=False)
                last = nc.tensor.matmul(out, w_hi, x_lo, start=False, stop=(k == len(terms) - 1))
            return last

        def first_then_loop(eng, n, body):
            body(0)
            with eng.Fori(1, n) as i:
                body(i)

        def tiles(eng, body, pairs=NT // 2):
            for j in range(2):
                body(0, j, False)
            with eng.Fori(1, pairs - 1) as i:
                for j in range(2):
                    body(i, j, False)
            for j in range(2):
                body(pairs - 1, j, j == 1)

        def out_tiles(eng, body):
            for j in range(2):
                body(0, j, False, False)
            with eng.Fori(1, NT // 2 - 1) as i:
                for j in range(2):
                    body(i, j, False, False)
            for j in range(2):
                body(NT // 2 - 1, j, j == 1, True)

        @blk.sync
        def _(sp):
            w_in = a["w_in"][0].rearrange("(k p) n -> p k n", p=P)

            def column(name):
                return a[name][0].rearrange("(k p) -> p k", p=P)

            sp.dma_start(g_mix, column("g_mix"), allow_slow_non_contiguous=True).then_inc(consts_here, 16)
            sp.dma_start(w_uvv[1], w_in[:, :, HALF:2 * HALF]).then_inc(w_in_here[1], 16)
            sp.dma_start(sgu_nat, a["sgu_w"][0].rearrange("h p q -> p h q")).then_inc(sgu_w_here, 16)
            sp.dma_start(g_xattn, column("g_xattn"), allow_slow_non_contiguous=True).then_inc(consts_here, 16)
            sp.dma_start(g_mem, column("g_mem"), allow_slow_non_contiguous=True).then_inc(consts_here, 16)
            sp.dma_start(g_moe, column("g_moe"), allow_slow_non_contiguous=True).then_inc(consts_here, 16)
            sp.dma_start(g_out[:, 0:4], column("g_out_a"), allow_slow_non_contiguous=True).then_inc(consts_here, 16)
            sp.dma_start(g_out[:, 4:8], column("g_out_b"), allow_slow_non_contiguous=True).then_inc(consts_here, 16)
            sp.dma_start(sgu_b, a["sgu_b"][0].rearrange("h p -> p h"), allow_slow_non_contiguous=True).then_inc(consts_here, 16)
            sp.dma_start(gv_row, a["g_sgu_v"][0].partition_broadcast(P)).then_inc(consts_here, 16)
            sp.dma_start(w_uvv[0], w_in[:, :, 0:HALF]).then_inc(w_in_here[0], 16)
            sp.dma_start(w_uvv[2], w_in[:, :, 4 * HALF:5 * HALF]).then_inc(w_in_here[2], 16)

            rpb = a["na_rpb"][0]
            sp.wait_ge(fill_made, 1)
            sp.dma_start(pad_t[0:NH * 15, 39:55], rpb.rearrange("h r c -> (h r) c")[:, 7:23]).then_inc(pad_here, 16)
            sp.wait_ge(pad_here, 16)
            sp.dma_start(rpb_pad, pad_t[0:NH * 15, :]).then_inc(pad_here, 16)
            sp.wait_ge(pad_here, 32)
            sp.wait_ge(fill_made, 2)
            pad = rpb_pad.rearrange("(h r) c -> h r c", r=15)
            spread = 0
            for qc in range(QC):
                dst = bias_src[qc:P:QC]
                for kind in range(3):
                    start = (47, 39, 31)[kind] - qc
                    if kind == 0 and qc < 8:
                        d, s = dst[:, 0, :, 0:QC], rpb[:, :, 15 - qc:31 - qc]
                    elif kind == 2 and qc > 8:
                        d, s = dst[:, 2, :, QC:KC], rpb[:, :, 15 - qc:31 - qc]
                    else:
                        d, s = dst[:, kind], pad[:, :, start:start + KC]
                    sp.dma_start(d, s).then_inc(bias_here, 16)
                    spread += 16
            sp.wait_ge(bias_here, spread)

            def channel_tiles(i):
                for j in range(2):
                    sp.wait_ge(qk_done[j], i)
                    sp.dma_start(w_qk[j], w_in[:, :, bass.ds(2 * HALF + (2 * i + j) * P, P)]).then_inc(w_qk_here[j], 16)

            def spread_bias(h):
                for qr in range(QROWS):
                    p0 = (h % 2) * HD + qr * QC
                    src = bias_src[h * QC:(h + 1) * QC]
                    sp.dma_start(na_bias[p0:p0 + QC, h // 2], src[:, :, 3 - qr:15 - qr]).then_inc(bias_here, 16)
                    sp.dma_start(na_bias_row[p0:p0 + QC, h // 2, :, qr:qr + 8], src[:, :, 3:11]).then_inc(bias_here, 16)

            sp.wait_ge(att_done, NT)
            channel_tiles(0)
            sp.wait_ge(bias_neg, 2)
            for h in range(NH // 2):
                spread_bias(h)
            channel_tiles(1)
            for h in range(NH // 2, NH):
                spread_bias(h)
            with sp.Fori(2, NH // 2) as i:
                channel_tiles(i)

            sp.wait_ge(fill_made, 3)
            for b in range(NE, NBLK):
                sp.dma_start(y_exp[b * P:(b + 1) * P].rearrange("p (a c) -> p a c", c=256),
                             zeros.unsqueeze(1).to_broadcast([P, D // 256, 256])).then_inc(unused_filled, 16)

            for j in range(2):
                sp.wait_ge(v_stored[j], 16 * NT // 2)
                sp.wait_ge(qk_done[j], NH // 2)
            for g in range(NKG):
                rows = v_att[g * GTOK:(g + 1) * GTOK].rearrange("(r c) n -> r c n", c=GW)
                for n in range(4):
                    sp.dma_start(vals[:, 4 * g + n], rows[:, COL_START[n]:COL_START[n] + KC]).then_inc(vals_here[g // 2], 16)
            for n in range(2):
                cols = a["w_out"][0][:, n * HALF:(n + 1) * HALF]
                sp.dma_start(w_out[n], cols.rearrange("(k p) n -> p k n", p=P)).then_inc(w_out_here, 16)

            def head_pair(hp):
                for g in range(NKG):
                    sp.wait_ge(o_evac, 4 * (NKG * hp + g + 1))
                    for half in range(2):
                        dst = y_mix[g * GTOK:(g + 1) * GTOK, bass.ds(HALF + (2 * hp + half) * HD, HD)]
                        sp.dma_start(dst.rearrange("(n q) d -> q n d", n=4),
                                     na_o[g % 2][half * HD:(half + 1) * HD]).then_inc(na_stored[g % 2], 16)

            first_then_loop(sp, NPAIR, head_pair)

            for j in range(2):
                sp.wait_ge(na_stored[j], 16 * 2 * NPAIR * NKG // 2)
                sp.wait_ge(ya_stored[j], 16 * 2 * NT // 2)

            def load_rows(i, j, x_rows):
                sp.wait_ge(yt_done[j], i)
                sp.dma_start(y_cat[j], y_mix[bass.ds((2 * i + j) * P, P)]).then_inc(y_here[j], 16)
                sp.wait_ge(h_added[j], 2 * i)
                x_rows = x_rows.rearrange("(r n c) d -> n r c d", n=4, c=QC)
                for n in range(2):
                    sp.dma_start(x_res[j][n * HD:(n + 1) * HD], x_rows[2 * j + n]).then_inc(xr_here[j], 16)

            for j in range(2):
                load_rows(0, j, a["x_prompt"][0][0:GTOK])
            sp.dma_start(w_xkv, a["w_xkv"][0].rearrange("(k p) n -> p k n", p=P)).then_inc(w_xkv_here, 16)
            sp.dma_start(w_rt[:, :, 0:NG], a["w_router_group"][0].rearrange("(k p) n -> p k n", p=P)).then_inc(w_rt_here, 16)
            sp.dma_start(w_rt[:, :, NG:], a["w_router_expert"][0].rearrange("(k p) n -> p k n", p=P)).then_inc(w_rt_here, 16)
            for j in range(2):
                sp.dma_start(mem_in[j], a["mem_prompt"][0][j * P:(j + 1) * P]).then_inc(mem_here[j], 16)
            for j in range(2):
                load_rows(1, j, a["x_prompt"][0][GTOK:2 * GTOK])
            with sp.Fori(2, NT // 2) as i:
                for j in range(2):
                    load_rows(i, j, a["x_sample"][0][bass.ds(i * GTOK - SEQ_P, GTOK)])
            sp.wait_ge(wo_done, NT)
            sp.dma_start(w_xq, a["w_xq"][0].rearrange("(k p) n -> p k n", p=P)).then_inc(w_xq_here, 16)
            for j in range(2):
                sp.wait_ge(n_ready, j + 1)
                sp.dma_start(mem_in[j], a["mem_sample"][0][j * P:(j + 1) * P]).then_inc(mem_here[j], 16)

            def load_expert(e, n, used):
                if used is not None:
                    sp.wait_ge(y_done, used)
                one = slice(e, e + 1) if isinstance(e, int) else bass.ds(e, 1)
                sp.dma_start(w_gu[n][:, 0], a["w_exp_gate"][0, one].rearrange("e (k p) f -> p (e k) f", p=P)).then_inc(w_e_here[n], 16)
                sp.dma_start(w_gu[n][:, 1], a["w_exp_up"][0, one].rearrange("e (k p) f -> p (e k) f", p=P)).then_inc(w_e_here[n], 16)
                sp.dma_start(w_dn[n], a["w_exp_down"][0, one].rearrange("e p d -> (e p) d")).then_inc(w_e_here[n], 16)

            sp.wait_ge(mm_done, 2 * XH)
            sp.dma_start(w_xo, a["w_xo"][0].rearrange("(k p) n -> p k n", p=P)).then_inc(w_xo_here, 16)
            first_moe = n_norms["moe", 0]
            for n in range(first_moe, len(norms)):
                t = norms[n][1]
                sp.wait_ge(n_ready, n + 1)
                sp.dma_start(xn_moe[t * P:(t + 1) * P], hs[n % 2]).then_inc(xn_stored[n % 2], 16)
                if t == TPC - 1:
                    sp.wait_ge(mm_done, n_groups["q", NCH - 1, XH - 1] + 1)
                    for e in (0, 1, 3):
                        load_expert(e, e, None)
            sp.wait_ge(mm_done, len(groups))
            for e in (2, 4, 5, 6, 7):
                load_expert(e, e, None)

            with sp.Fori(0, NE // RING - 1) as r:
                for n in range(RING):
                    load_expert(RING * (r + 1) + n, n, RING * r + n + 1)

            sp.wait_ge(table_ready, 1)

            def load_overflow(b, half, n, r):
                e = sp.value_load(over_e[0:1, bass.ds(b - NE, 1)], min_val=0, max_val=NE - 1)
                load_expert(e, n, b - 3)

            overflow_blocks(sp, load_overflow)

            sp.dma_start(gf_row, a["g_final"].partition_broadcast(P)).then_inc(consts_here, 16)
            for t in range(NT):
                sp.wait_ge(f_out, t + 1)
                g, base = t // 2, 0 if t < SEQ_P // P else SEQ_P // GTOK
                y = y_prompt if t < SEQ_P // P else y_sample
                y = y[0, (g - base) * GTOK:(g - base + 1) * GTOK].rearrange("(r n c) d -> n r c d", n=4, c=QC)
                for n in range(2):
                    sp.dma_start(y[2 * (t % 2) + n], out_st[t % 2][n * HD:(n + 1) * HD]).then_inc(out_sent[t % 2], 16)
            for j in range(2):
                sp.wait_ge(out_sent[j], 32 * NT // 2)
                sp.wait_ge(xn_stored[j], 16 * NT // 2)

        @blk.gpsimd
        def _(pool):
            xp, xsm = a["x_prompt"][0], a["x_sample"][0]
            for j in range(2):
                pool.dma_start(x_in[j], xp[j * P:(j + 1) * P]).then_inc(x_here[j], 16)
            pool.memset(neg_half, -0.5).then_inc(const_made, 1)
            pool.memset(eps, EPS).then_inc(const_made, 1)
            pool.memset(ident, 0.0).then_inc(ident_made, 1)
            pool.wait_ge(ident_made, 1)
            pool.affine_select(out=ident, in_=ident, compare_op=ALU.not_equal, fill=1.0, base=0,
                               pattern=[[-1, P]], channel_multiplier=1).then_inc(ident_made, 1)
            pool.wait_ge(const_made, 2)

            def rsqrt(col, squares, n_sq, eps_sem, n_eps, out_sem):
                pool.wait_ge(squares, n_sq)
                pool.tensor_tensor(ms_eps[:, col:col + 1], ms[:, col:col + 1], eps, ALU.add).then_inc(eps_sem, 1)
                pool.wait_ge(eps_sem, n_eps)
                pool.tensor_tensor(rs[:, col:col + 1], ms_eps[:, col:col + 1], neg_half, ALU.pow).then_inc(out_sem, 1)

            def load_x(rows, i, j):
                pool.wait_ge(xt_done[j], i)
                pool.dma_start(x_in[j], rows).then_inc(x_here[j], 16)

            def norm_x(i, j):
                rsqrt(j, x_sq[j], i + 1, x_eps[j], i + 1, x_rs[j])

            def tile_work(i, j, last, next_rows):
                t = 2 * i + j
                if j == 0:
                    norm_x(i, 1)
                elif not last:
                    norm_x(i + 1, 0)
                if next_rows is not None:
                    load_x(next_rows(j), i + 1, j)
                rsqrt(2, v_sq, t + 1, v_eps, t + 1, v_rs)
                rsqrt(3, ya_sq, t + 1, ya_eps, t + 1, ya_rs)

            norm_x(0, 0)
            for j in range(2):
                tile_work(0, j, False, lambda j: xp[(2 + j) * P:(3 + j) * P])
            pool.wait_ge(bias_here, 16 * 3 * QC)
            pool.tensor_scalar(bias_src, bias_src, -1.0, 0.0, ALU.mult, ALU.add).then_inc(bias_neg, 1)
            with pool.Fori(1, NT // 2 - 1) as i:
                for j in range(2):
                    tile_work(i, j, False, lambda j: xsm[bass.ds((2 * (i + 1) + j) * P - SEQ_P, P)])
            for j in range(2):
                tile_work(NT // 2 - 1, j, j == 1, None)

            pool.wait_ge(att_done, NT)
            pool.memset(na_bias_row, -MASKED).then_inc(bias_neg, 1)

            for j in range(2):
                pool.wait_ge(qk_done[j], NH // 2)
            for j in range(2):
                pool.memset(q_diag[j], 0.0).then_inc(diag_zero, 1)
            pool.wait_ge(diag_zero, 2)
            for j in range(2):
                pool.wait_ge(qk_evac_v[j], 2 * (NH // 2))
                pool.wait_ge(qk_evac_s[j], NH // 2)
            def head_pair(hp):
                for g in range(NKG):
                    pool.wait_ge(s_done, 2 * (NSTEP * hp + max(2 * g - 2, 0)))
                    for half in range(2):
                        rows = slice(half * HD, (half + 1) * HD)
                        q = qk[rows, hp, g * GTOK:(g + 1) * GTOK].rearrange("p (r n c) -> p n r c", n=4, c=QC)
                        pool.tensor_copy(q_diag[g % 2][rows, :, half], q).then_inc(diag_ready, 1)

            first_then_loop(pool, NPAIR, head_pair)

            def rsqrt_pair(i, j):
                n = i + 1 + NT // 2
                rsqrt(j, x_sq[j], n, x_eps[j], n, x_rs[j])

            tiles(pool, lambda i, j, last: rsqrt_pair(i, j))
            for n in range(len(norms)):
                rsqrt(4 + n % 2, n_sq, n + 1, n_eps, n + 1, n_rs)

            pool.wait_ge(mm_done, n_groups["q", NCH - 1, XH - 1] + 1)
            for dst, pattern, base, cm in ((iota_e, [[P, NE]], 0, 0), (iota_b, [[1, NOVER]], 0, 0),
                                           (iota_j, [[P, NT - 1]], P, 0), (first_g, [[-1, NG]], NG, 0),
                                           (first_e, [[-1, EPG]], EPG, 0), (token, [[P, NT]], 0, 1)):
                pool.iota(dst, pattern=pattern, base=base, channel_multiplier=cm,
                          allow_small_or_imprecise_dtypes=True).then_inc(route_const, 1)
            pool.memset(ones, 1.0).then_inc(route_const, 1)
            pool.memset(before, 1.0).then_inc(route_const, 1)
            pool.memset(zeros_i, 0).then_inc(route_const, 1)
            pool.wait_ge(route_const, 9)
            pool.affine_select(out=before, in_=before, compare_op=ALU.is_gt, fill=0.0, base=0,
                               pattern=[[1, P]], channel_multiplier=-1).then_inc(route_const, 1)

            table = slot_tok.rearrange("(b p) o -> b (p o)", p=P)
            pool.dma_start(table, zeros_i[0:NBLK]).then_inc(table_dma, 16)
            pool.wait_ge(table_dma, 16)
            pool.wait_ge(slot_ready, 2)
            for k in range(2):
                for t in range(NT):
                    pool.indirect_dma_start(out=slot_tok, out_offset=bass.IndirectOffsetOnAxis(ap=slot[:, k, t:t + 1], axis=0),
                                            in_=token[:, t:t + 1], in_offset=None).then_inc(table_sent, 16)
            pool.wait_ge(table_sent, 16 * 2 * NT)
            pool.dma_start(slot_rows[0:NBLK], table).then_inc(table_dma, 16)

            pool.wait_ge(table_ready, 1)
            for j in range(2):
                pool.wait_ge(xn_stored[j], 16 * NT // 2)

            def gather(rows, j):
                pool.indirect_dma_start(out=x_g[j], out_offset=None, in_=xn_moe,
                                        in_offset=bass.IndirectOffsetOnAxis(ap=rows, axis=0)).then_inc(xg_here[j], 16)

            for b in range(NE + 1):
                if b >= 2:
                    pool.wait_ge(xgt_done, b - 1)
                gather(slot_src[:, b:b + 1], b % 2)
            used = pool.value_load(over_n[0:1, 0:1], min_val=0, max_val=NOVER)
            for b in range(NE + 1, NBLK):
                with pool.If(used > b - NE - 1):
                    pool.wait_ge(xgt_done, b - 1)
                    gather(slot_src[:, b:b + 1], b % 2)

            pool.wait_ge(all_sent, 1)

            def gather_y(t):
                if t >= 2:
                    pool.wait_ge(f_add, 2 * (t - 1))
                for k in range(2):
                    pool.indirect_dma_start(out=y_g[t % 2][k], out_offset=None, in_=y_exp,
                                            in_offset=bass.IndirectOffsetOnAxis(ap=slot[:, k, t:t + 1], axis=0)).then_inc(yg_here[t % 2], 16)

            gather_y(0)
            for t in range(NT):
                if t + 1 < NT:
                    gather_y(t + 1)
                n = len(norms) + t
                rsqrt(4 + n % 2, n_sq, n + 1, n_eps, n + 1, n_rs)

        @blk.scalar
        def _(act):
            def square_x(i, j):
                act.wait_ge(x_here[j], 16 * (i + 1))
                first = is_first(i, j)
                if not first:
                    act.wait_ge(sgu_t, 2)
                    act.wait_ge(x_sq[1 - j], i + j)
                nc.scalar.activation(x_junk0 if first else x_junk, x_in[j], ACT.Square,
                                     scale=D ** -0.5, accum_out=ms[:, j:j + 1]).then_inc(x_sq[j], 1)

            def split_w_in(n):
                act.wait_ge(w_in_here[n], 16)
                make_hi(act, W_UVV_PLACE[n], w_uvv_hi[n], w_uvv[n])

            def split_x_tile(i, j):
                t = 2 * i + j
                act.wait_ge(xf_evac, 2 * (t + 1))
                if not is_first(i, j):
                    act.wait_ge(att_done, t - 1)
                make_hi(act, split_x(t), x_hi[j], xT[:, :, bass.ds(t * P, P)])

            def split_w(i, j):
                act.wait_ge(w_qk_here[j], 16 * (i + 1))
                act.wait_ge(qk_done[j], i)
                make_hi(act, split_w_qk(i, j), w_qk_hi[j], w_qk[j])

            square_x(0, 0)
            split_w_in(1)
            split_x_tile(0, 0)
            split_w_in(0)
            split_w_in(2)

            def tile_work(i, j, last):
                t = 2 * i + j
                nxt = (i, 1) if j == 0 else (i + 1, 0)
                if not last:
                    square_x(*nxt)
                act.wait_ge(v_done, t + 1)
                act.wait_ge(vn_ready, t)
                nc.scalar.activation(v_g, bank[2][:], ACT.Gelu_apprx_tanh).then_inc(v_gelu, 1)
                act.wait_ge(v_gelu, t + 1)
                act.wait_ge(ya_sq, t)
                nc.scalar.activation(sq_junk, v_g, ACT.Square, scale=HALF ** -0.5,
                                     accum_out=ms[:, 2:3]).then_inc(v_sq, 1)
                act.wait_ge(u_done, t + 1)
                act.wait_ge(ya_mul, t)
                nc.scalar.activation(u_g, bank[3][:], ACT.Gelu_apprx_tanh).then_inc(u_gelu, 1)
                if not last:
                    split_x_tile(*nxt)
                act.wait_ge(att_done, t + 1)
                act.wait_ge(v_stored[j], 16 * i)
                nc.scalar.activation(v_st[j], bank[4][:], ACT.Copy).then_inc(att_copied, 1)
                act.wait_ge(att_copied, t + 1)
                act.dma_start(v_att[bass.ds(t * P, P)], v_st[j]).then_inc(v_stored[j], 16)
                if last:
                    make_hi(act, split_xT(0), xT_hi[:, :, 0:CH], xT[:, :, 0:CH])
                    split_w(0, 0)
                act.wait_ge(ya_mul, t + 1)
                act.wait_ge(v_sq, t + 1)
                nc.scalar.activation(sq_junk, y_a, ACT.Square, scale=HALF ** -0.5,
                                     accum_out=ms[:, 3:4]).then_inc(ya_sq, 1)
                act.wait_ge(yan_ready, t + 1)
                for r in range(2):
                    dst = y_mix[bass.ds(i * GTOK, GTOK), 0:HALF].rearrange("(n r c) d -> n r c d", n=4, r=QROWS)
                    act.dma_start(dst[:, 2 * j + r], y_an[j][r * GW:(r + 1) * GW]).then_inc(ya_stored[j], 16)

            tiles(act, tile_work)

            act.wait_ge(mix_done, NT)
            for n in range(1, NCH):
                make_hi(act, split_xT(n), xT_hi[:, :, n * CH:(n + 1) * CH], xT[:, :, n * CH:(n + 1) * CH])
            split_w(0, 1)
            for j in range(2):
                act.wait_ge(ya_stored[j], 16 * 2 * NT // 2)
                act.wait_ge(v_stored[j], 16 * NT // 2)

            def channel_tiles(i, last=False):
                for j in range(2):
                    act.wait_ge(qk_done[j], i + 1)
                    nc.scalar.activation(qk[:, 2 * i + j, CH:2 * CH], bank[3 * j + 1][:], ACT.Copy).then_inc(qk_evac_s[j], 1)
                    if not last:
                        split_w(i + 1, j)

            channel_tiles(0)
            with act.Fori(1, NH // 2 - 1) as i:
                channel_tiles(i)
            channel_tiles(NH // 2 - 1, True)

            def head_pair(hp):
                base = NSTEP * hp

                def exps(s):
                    width = len(NA_GROUPS[s // 2][0]) * P
                    act.wait_ge(s_min, base + s + 1)
                    for n in range(2):
                        p = na_p[s % 2][:, n, 0:width]
                        nc.scalar.activation(p, p, ACT.Exp, bias=na_st[:, 2 * (s % 2) + n:2 * (s % 2) + n + 1], scale=-1.0,
                                             accum_out=na_st[:, 4 + 2 * (s % 2) + n:5 + 2 * (s % 2) + n]).then_inc(p_exp, 1)

                def evac_pT(s):
                    width = len(NA_GROUPS[s // 2][0]) * P
                    act.wait_ge(pt_done, base + s + 1)
                    act.wait_ge(o_done, base + s - 1 if s >= 1 else base)
                    nc.scalar.activation(na_pT[s % 2][:, 0, 0:width], bank[4][:, 0:width], ACT.Copy).then_inc(pt_evac_s, 1)

                for s in range(NSTEP + 1):
                    if s < NSTEP:
                        exps(s)
                    if s >= 1:
                        evac_pT(s - 1)

            head_pair(0)
            act.wait_ge(w_out_here, 32)
            make_hi(act, split_w_out(0), w_out_hi[0], w_out[0])
            with act.Fori(1, NPAIR) as hp:
                head_pair(hp)

            def square_y(i, j):
                act.wait_ge(y_here[j], 16 * (i + 1))
                act.wait_ge(x_sq[1 - j], NT // 2 + i + j)
                nc.scalar.activation(yb_junk, y_cat[j][:, HALF:], ACT.Square, scale=HALF ** -0.5,
                                     accum_out=ms[:, j:j + 1]).then_inc(x_sq[j], 1)

            def split_y_tile(i, j):
                t = 2 * i + j
                act.wait_ge(yT_evac, 2 * (t + 1))
                make_hi(act, split_y(t), y_hi[j], y_T[j])

            for j in range(2):
                square_y(0, j)
            act.wait_ge(pt_done, NPAIR * NSTEP)
            make_hi(act, split_w_out(1), w_out_hi[1], w_out[1])
            split_y_tile(0, 0)

            def out_tile(i, j, last, last_pair):
                if not last_pair:
                    square_y(i + 1, j)
                if not last:
                    split_y_tile(*((i, 1) if j == 0 else (i + 1, 0)))

            out_tiles(act, out_tile)

            def source(n):
                kind, t = norms[n]
                return mem_in[n % 2] if kind == "mem" else H[:, t]

            def wait_source(eng, n):
                kind, t = norms[n]
                if kind == "mem":
                    eng.wait_ge(mem_here[n % 2], 16 * (n // 2 + 1))
                elif kind == "h":
                    eng.wait_ge(h_added[t % 2], 2 * (t // 2 + 1))
                else:
                    eng.wait_ge(mm_evac, n_groups["xo", t, 1] + 1)

            act.wait_ge(x_sq[1], NT)
            for what, n in order:
                if what == "sq":
                    wait_source(act, n)
                    if n >= 2:
                        act.wait_ge(nt_done, n - 1)
                    stored = (n - n_norms["moe", 0]) // 2
                    if stored > 0:
                        act.wait_ge(xn_stored[n % 2], 16 * stored)
                    nc.scalar.activation(hs[n % 2], source(n), ACT.Square, scale=D ** -0.5,
                                         accum_out=ms[:, 4 + n % 2:5 + n % 2]).then_inc(n_sq, 1)
                elif what == "S":
                    act.wait_ge(sx_neg, n + 1)
                    if n >= 4:
                        act.wait_ge(ptx_done, n - 3)
                    for h in range(2):
                        k = 2 * (n % 4) + h
                        nc.scalar.activation(p_x[n % 4][:, h], bank[6 + n % 2][:, h * N_MEM:(h + 1) * N_MEM], ACT.Exp,
                                             bias=xa_st[:, 8 + k:9 + k], scale=XA_SCALE,
                                             accum_out=xa_st[:, 16 + k:17 + k]).then_inc(px_exp, 1)
                elif what == "PT":
                    c, t, hp = n // 8, (n % 8) // 2, n % 2
                    act.wait_ge(ptx_done, n + 1)
                    if n % 8 == 0 and c > 0:
                        act.wait_ge(mm_done, n_groups["o", c - 1, XH - 1] + 1)
                    nc.scalar.activation(pT_x[:, 2 * hp:2 * hp + 2, :, t * P:(t + 1) * P],
                                         bank[2 + n % 2][:].rearrange("p (h m t) -> p h m t", h=2, m=2), ACT.Copy).then_inc(ptx_evac, 1)

            act.wait_ge(route_exp, 1)
            nc.scalar.activation(rs8[1][:, :, 0:NG], rs8[0][:, :, 0:NG], ACT.Exp).then_inc(exp_done, 1)
            act.wait_ge(route_exp, 2)
            nc.scalar.activation(rs1[9], rs1[8], ACT.Exp).then_inc(exp_done, 1)

            def expert(b, half, n, r):
                act.wait_ge(gu_done, b + 1)
                nc.scalar.activation(silu_g, bank[2][:, 0:FE], ACT.Silu).then_inc(e_silu, 1)
                act.wait_ge(y_done, b + 1)
                act.wait_ge(y_sent[n % 2], 16 * half)
                nc.scalar.activation(y_st[n % 2][:, 0:HALF], bank[5][:], ACT.Copy).then_inc(y_evac_s, 1)
                act.wait_ge(y_evac_s, b + 1)
                act.wait_ge(y_evac_v, b + 1)
                act.dma_start(y_exp[bass.ds(b * P, P)], y_st[n % 2]).then_inc(y_sent[n % 2], 16)

            expert_blocks(act, expert)
            act.wait_ge(table_ready, 1)
            act.wait_ge(unused_filled, 16 * NOVER)
            overflow_blocks(act, expert)
            used = act.value_load(over_n[0:1, 0:1], min_val=0, max_val=NOVER)
            act.wait_ge(y_sent[0], 16 * (NE // 2) + 16 * ((used + 1) // 2))
            act.wait_ge(y_sent[1], 16 * (NE // 2) + 16 * (used // 2))
            nc.scalar.activation(xa_st[:, 0:1], xa_st[:, 0:1], ACT.Copy).then_inc(all_sent, 1)

            for t in range(NT):
                act.wait_ge(f_add, 2 * (t + 1))
                if t >= 2:
                    act.wait_ge(out_sent[t % 2], 32 * (t // 2))
                n = len(norms) + t
                nc.scalar.activation(out_st[t % 2], H[:, t], ACT.Square, scale=D ** -0.5,
                                     accum_out=ms[:, 4 + n % 2:5 + n % 2]).then_inc(n_sq, 1)

        @blk.vector
        def _(dve):
            nc.vector.memset(pad_t, MASKED).then_inc(fill_made, 1)
            nc.vector.memset(bias_src, MASKED).then_inc(fill_made, 1)
            nc.vector.memset(zeros, 0.0).then_inc(fill_made, 1)
            def scale_x(i, j):
                dve.wait_ge(x_rs[j], i + 1)
                nc.vector.tensor_scalar(x_in[j], x_in[j], rs[:, j:j + 1], None, ALU.mult).then_inc(xs_ready[j], 1)

            def evac_xT(i, j):
                dve.wait_ge(xt_done[j], i + 1)
                t = 2 * i + j
                for n in range(2):
                    g = g_mix[:, 4 * n:4 * n + 4].unsqueeze(2).to_broadcast([P, 4, P])
                    nc.vector.tensor_tensor(xT[:, 4 * n:4 * n + 4, bass.ds(t * P, P)], bank[n][:].rearrange("p (k t) -> p k t", k=4), g,
                                            ALU.mult).then_inc(xf_evac, 1)
                if not is_first(i, j):
                    dve.wait_ge(att_done, t - 1)
                make_lo(dve, split_x(t), x_lo[j], xT[:, :, bass.ds(t * P, P)], x_hi[j])

            def split_w_in(n):
                make_lo(dve, W_UVV_PLACE[n], w_uvv_lo[n], w_uvv[n], w_uvv_hi[n])

            def split_w(i, j):
                make_lo(dve, split_w_qk(i, j), w_qk_lo[j], w_qk[j], w_qk_hi[j])

            def split_chunk(n):
                c = slice(n * CH, (n + 1) * CH)
                make_lo(dve, split_xT(n), xT_lo[:, :, c], xT[:, :, c], xT_hi[:, :, c])

            scale_x(0, 0)
            split_w_in(1)
            dve.wait_ge(consts_here, 16 * 8)
            evac_xT(0, 0)
            for n in range(2):
                dve.wait_ge(sgu_t, n + 1)
                nc.vector.tensor_copy(sgu_wT[:, 4 * n:4 * n + 4], bank[6 + n][:].rearrange("p (h q) -> p h q", h=4)).then_inc(sgu_evac, 1)
            split_w_in(0)
            split_w_in(2)

            def tile_work(i, j, last):
                t = 2 * i + j
                nxt = (i, 1) if j == 0 else (i + 1, 0)
                if not last:
                    scale_x(*nxt)
                dve.wait_ge(v_rs, t + 1)
                dve.wait_ge(mix_done, t)
                nc.vector.scalar_tensor_tensor(v_n, v_g, rs[:, 2:3], gv_row, ALU.mult, ALU.mult).then_inc(vn_ready, 1)
                if not last:
                    evac_xT(*nxt)
                else:
                    split_chunk(0)
                    split_w(0, 0)
                dve.wait_ge(mix_done, t + 1)
                dve.wait_ge(ya_mul, t)
                nc.vector.tensor_tensor(mixed.rearrange("p (h d) -> p h d", h=NH), bank[5][:].rearrange("p (h d) -> p h d", h=NH),
                                        sgu_b.unsqueeze(2).to_broadcast([P, NH, HD]), ALU.add).then_inc(mix_bias, 1)
                dve.wait_ge(mix_bias, t + 1)
                dve.wait_ge(u_gelu, t + 1)
                dve.wait_ge(yan_ready, t)
                nc.vector.tensor_tensor(y_a, mixed, u_g, ALU.mult).then_inc(ya_mul, 1)
                dve.wait_ge(ya_rs, t + 1)
                dve.wait_ge(ya_stored[j], 32 * i)
                nc.vector.tensor_scalar(y_an[j], y_a, rs[:, 3:4], None, ALU.mult).then_inc(yan_ready, 1)

            tiles(dve, tile_work)

            for n in range(1, NCH):
                split_chunk(n)
            split_w(0, 1)
            for j in range(2):
                dve.wait_ge(ya_stored[j], 16 * 2 * NT // 2)
                dve.wait_ge(v_stored[j], 16 * NT // 2)

            def channel_tiles(i, last=False):
                for j in range(2):
                    dve.wait_ge(qk_done[j], i + 1)
                    for n in (0, 2):
                        nc.vector.tensor_copy(qk[:, 2 * i + j, n * CH:(n + 1) * CH], bank[3 * j + n][:]).then_inc(qk_evac_v[j], 1)
                    if not last:
                        split_w(i + 1, j)

            channel_tiles(0)
            with dve.Fori(1, NH // 2 - 1) as i:
                channel_tiles(i)
            channel_tiles(NH // 2 - 1, True)

            dve.wait_ge(bias_here, 16 * 3 * QC + 16 * 2 * NH * QROWS)
            def head_pair(hp):
                base = NSTEP * hp

                def scores(s):
                    keys, first, row_masked = NA_GROUPS[s // 2]
                    width = len(keys) * P
                    kind = s % 2
                    bias = (na_bias_row if row_masked else na_bias)[:, hp, kind:kind + 2, first:first + width // KC]
                    for n in range(2):
                        dve.wait_ge(s_done, 2 * (base + s) + n + 1)
                        if n == 0:
                            dve.wait_ge(pt_done, base + s - 1 if s >= 1 else base)
                        nc.vector.scalar_tensor_tensor(
                            na_p[s % 2][:, n, 0:width].rearrange("p (r c) -> p r c", c=KC),
                            bank[2 * (s % 2) + n][:, 0:width].rearrange("p (r c) -> p r c", c=KC), -NA_SCALE,
                            bias[:, n], ALU.mult, ALU.add).then_inc(s_biased, 1)
                    dve.wait_ge(s_biased, 2 * (base + s + 1))
                    nc.vector.tensor_reduce(na_st[:, 2 * (s % 2):2 * (s % 2) + 2], na_p[s % 2][:, :, 0:width], AX, ALU.min).then_inc(s_min, 1)

                def evac_pT(s):
                    width = len(NA_GROUPS[s // 2][0]) * P
                    dve.wait_ge(p_exp, 2 * (base + s + 1))
                    dve.wait_ge(o_evac, 2 * (base + s - 1) if s >= 1 else 2 * base)
                    nc.vector.reciprocal(na_st[:, 8 + 2 * (s % 2):10 + 2 * (s % 2)], na_st[:, 4 + 2 * (s % 2):6 + 2 * (s % 2)]).then_inc(s_rcp, 1)
                    dve.wait_ge(pt_done, base + s + 1)
                    dve.wait_ge(o_done, base + s - 1 if s >= 1 else base)
                    nc.vector.tensor_copy(na_pT[s % 2][:, 1, 0:width], bank[5][:, 0:width]).then_inc(pt_evac_v, 1)

                def evac_o(s):
                    g = s // 2
                    dve.wait_ge(o_done, base + s + 1)
                    dve.wait_ge(s_rcp, base + s + 1)
                    if s % 2 == 0:
                        dve.wait_ge(na_stored[g % 2], 32 * (3 * hp + g // 2))
                    for half in range(2):
                        rows = slice(half * HD, (half + 1) * HD)
                        o = bank[6 + s % 2][rows, 0:2 * P].rearrange("p (n d) -> p n d", n=2)[:, :, half * HD:(half + 1) * HD]
                        r = na_st[rows, 8 + 2 * (s % 2):10 + 2 * (s % 2)].unsqueeze(2).to_broadcast([HD, 2, HD])
                        nc.vector.tensor_tensor(na_o[g % 2][rows, 2 * (s % 2):2 * (s % 2) + 2], o, r, ALU.mult).then_inc(o_evac, 1)

                for s in range(NSTEP + 2):
                    if s < NSTEP:
                        scores(s)
                    if 1 <= s <= NSTEP:
                        evac_pT(s - 1)
                    if s >= 2:
                        evac_o(s - 2)

            head_pair(0)
            make_lo(dve, split_w_out(0), w_out_lo[0], w_out[0], w_out_hi[0])
            with dve.Fori(1, NPAIR) as hp:
                head_pair(hp)

            def scale_y(i, j):
                dve.wait_ge(x_rs[j], NT // 2 + i + 1)
                nc.vector.tensor_scalar(y_cat[j][:, HALF:], y_cat[j][:, HALF:], rs[:, j:j + 1], None, ALU.mult).then_inc(yb_ready[j], 1)

            def gain_evac(dst, n, gain, done):
                g = gain[:, 4 * n:4 * n + 4].unsqueeze(2).to_broadcast([P, 4, P])
                nc.vector.tensor_tensor(dst, bank[n][:].rearrange("p (k t) -> p k t", k=4), g, ALU.mult).then_inc(done, 1)

            def evac_yT(i, j):
                dve.wait_ge(yt_done[j], i + 1)
                if not is_first(i, j):
                    dve.wait_ge(wo_done, 2 * i + j - 1)
                for n in range(2):
                    gain_evac(y_T[j][:, 4 * n:4 * n + 4], n, g_out, yT_evac)

            def split_y_tile(i, j):
                make_lo(dve, split_y(2 * i + j), y_lo[j], y_T[j], y_hi[j])

            for j in range(2):
                scale_y(0, j)
            evac_yT(0, 0)
            make_lo(dve, split_w_out(1), w_out_lo[1], w_out[1], w_out_hi[1])
            split_y_tile(0, 0)

            def add_rows(i, j, last, last_pair):
                if not last:
                    nxt = (i, 1) if j == 0 else (i + 1, 0)
                    evac_yT(*nxt)
                    split_y_tile(*nxt)
                if not last_pair:
                    scale_y(i + 1, j)
                t = 2 * i + j
                dve.wait_ge(wo_done, t + 1)
                dve.wait_ge(xr_here[j], 32 * (i + 1))
                for n in range(2):
                    cols = slice(n * HALF, (n + 1) * HALF)
                    nc.vector.tensor_tensor(H[:, t, cols], bank[2 + 2 * j + n][:], x_res[j][:, cols], ALU.add).then_inc(h_added[j], 1)

            out_tiles(dve, add_rows)

            for what, n in order:
                if what == "pre":
                    dve.wait_ge(n_rs, n + 1)
                    src = mem_in[n % 2] if norms[n][0] == "mem" else H[:, norms[n][1]]
                    nc.vector.tensor_scalar(hs[n % 2], src, rs[:, 4 + n % 2:5 + n % 2], None, ALU.mult).then_inc(n_ready, 1)
                elif what == "T":
                    kind, t = norms[n]
                    dve.wait_ge(nt_done, n + 1)
                    if kind == "mem":
                        dst, gain = mem_T[:, :, t * P:(t + 1) * P], g_mem
                    elif kind == "h":
                        if t % TPC == 0 and t > 0:
                            dve.wait_ge(mm_done, n_groups["q", t // TPC - 1, XH - 1] + 1)
                        dst, gain = h_T[:, :, (t % TPC) * P:(t % TPC + 1) * P], g_xattn
                    else:
                        if t >= 2:
                            dve.wait_ge(mm_done, n_groups["route", t - 2] + 1)
                        dst, gain = r_T[t % 2], g_moe
                    for b in range(2):
                        gain_evac(dst[:, 4 * b:4 * b + 4], b, gain, nt_evac)
                elif what == "mm":
                    kind, *which = groups[n]
                    dve.wait_ge(mm_done, n + 1)
                    b = bank[4 + n % 2]
                    if kind == "xo":
                        t, half = which
                        cols = slice(half * HALF, (half + 1) * HALF)
                        nc.vector.tensor_tensor(H[:, t, cols], H[:, t, cols], b[:], ALU.add).then_inc(mm_evac, 1)
                    elif kind == "route":
                        nc.vector.tensor_copy(logit[:, which[0]], b[:, 0:NG + NE]).then_inc(mm_evac, 1)
                    else:
                        dst = {"k_mem": lambda: k_mem[:, which[0]], "v_mem": lambda: v_mem[:, which[0]],
                               "q": lambda: q_x[which[0] % 2][:, which[1]], "o": lambda: o_T[:, which[1]]}[kind]()
                        nc.vector.tensor_copy(dst, b[:]).then_inc(mm_evac, 1)
                elif what == "S":
                    k = 2 * (n % 4)
                    dve.wait_ge(sx_done, n + 1)
                    if n >= 4:
                        dve.wait_ge(px_ready, n - 3)
                    nc.vector.tensor_reduce(xa_st[:, k:k + 2], bank[6 + n % 2][:].rearrange("p (h m) -> p h m", h=2), AX, ALU.max).then_inc(sx_max, 1)
                    dve.wait_ge(sx_max, n + 1)
                    nc.vector.tensor_scalar(xa_st[:, 8 + k:10 + k], xa_st[:, k:k + 2], -XA_SCALE, None, ALU.mult).then_inc(sx_neg, 1)
                elif what == "px":
                    k = 2 * (n % 4)
                    dve.wait_ge(px_exp, 2 * (n + 1))
                    nc.vector.reciprocal(xa_st[:, 24 + k:26 + k], xa_st[:, 16 + k:18 + k]).then_inc(sx_rcp, 1)
                    dve.wait_ge(sx_rcp, n + 1)
                    r = xa_st[:, 24 + k:26 + k].unsqueeze(2).to_broadcast([P, 2, N_MEM])
                    nc.vector.tensor_tensor(p_x[n % 4], p_x[n % 4], r, ALU.mult).then_inc(px_ready, 1)

            done = [0]

            def step(ins):
                done[0] += 1
                ins.then_inc(route, 1)
                dve.wait_ge(route, done[0])

            def over_tokens(v, n):
                return v.unsqueeze(2).to_broadcast([P, NT, n])

            def first_max(out, scores, peak, order_of, tmp, best):
                n = scores.shape[-1]
                step(nc.vector.tensor_tensor(tmp, scores, over_tokens(peak, n), ALU.is_equal))
                step(nc.vector.tensor_tensor(tmp, tmp, order_of.unsqueeze(1).to_broadcast([P, NT, n]), ALU.mult))
                step(nc.vector.tensor_reduce(best, tmp, AX, ALU.max))
                step(nc.vector.tensor_tensor(out, tmp, over_tokens(best, n), ALU.is_equal))

            dve.wait_ge(route_const, 10)
            dve.wait_ge(mm_evac, len(groups))
            dve.wait_ge(mm_done, len(groups))
            lg, le = logit[:, :, 0:NG], logit[:, :, NG:]
            g_max, g_best, g_sum, g_top, e_max, e_best, e_max2, e_best2 = rs1[:8]
            e_diff, e_exp, e_sum, e_rcp = rs1[8:12]
            g_one = rs8[4][:, :, 0:NG]
            step(nc.vector.tensor_reduce(g_max, lg, AX, ALU.max))
            nc.vector.tensor_tensor(rs8[0][:, :, 0:NG], lg, over_tokens(g_max, NG), ALU.subtract).then_inc(route_exp, 1)
            first_max(g_one, lg, g_max, first_g, rs8[3][:, :, 0:NG], g_best)
            by_group = "p t (g e) -> p t g e"
            step(nc.vector.tensor_tensor(rt[0].rearrange(by_group, g=NG), le.rearrange(by_group, g=NG),
                                         g_one.unsqueeze(3).to_broadcast([P, NT, NG, EPG]), ALU.mult))
            e_sel, e_sel2, one1, one2 = rs8[5], rs8[6], rs8[9], rs8[11]
            step(nc.vector.tensor_reduce(e_sel, rt[0].rearrange("p t (g e) -> p t e g", g=NG), AX, ALU.add))
            step(nc.vector.tensor_reduce(e_max, e_sel, AX, ALU.max))
            first_max(one1, e_sel, e_max, first_e, rs8[7], e_best)
            step(nc.vector.scalar_tensor_tensor(e_sel2, one1, -3.0e38, e_sel, ALU.mult, ALU.add))
            step(nc.vector.tensor_reduce(e_max2, e_sel2, AX, ALU.max))
            first_max(one2, e_sel2, e_max2, first_e, rs8[8], e_best2)
            nc.vector.tensor_tensor(e_diff, e_max2, e_max, ALU.subtract).then_inc(route_exp, 1)
            for k, one in ((0, one1), (1, one2)):
                step(nc.vector.tensor_tensor(rt[1 + k].rearrange(by_group, g=NG), g_one.unsqueeze(3).to_broadcast([P, NT, NG, EPG]),
                                             one.unsqueeze(2).to_broadcast([P, NT, NG, EPG]), ALU.mult))
            nc.vector.tensor_tensor(rt[3], rt[1], rt[2], ALU.add).then_inc(chosen, 1)
            dve.wait_ge(exp_done, 2)
            step(nc.vector.tensor_reduce(g_sum, rs8[1][:, :, 0:NG], AX, ALU.add))
            step(nc.vector.reciprocal(g_top, g_sum))
            step(nc.vector.tensor_scalar(e_sum, e_exp, 1.0, None, ALU.add))
            step(nc.vector.reciprocal(e_rcp, e_sum))
            step(nc.vector.tensor_tensor(gate[:, 0], g_top, e_rcp, ALU.mult))
            step(nc.vector.tensor_tensor(gate[:, 1], gate[:, 0], e_exp, ALU.mult))
            earlier, rank, count = rt[5], rt[4], re[0]
            step(nc.vector.memset(earlier[:, 0], 0.0))
            dve.wait_ge(count_done, 1)
            per_tile = bank[3][:, 0:NT * NE].rearrange("p (t e) -> p t e", t=NT)
            for t in range(1, NT):
                step(nc.vector.tensor_tensor(earlier[:, t], per_tile[:, t - 1], earlier[:, t - 1], ALU.add))
            step(nc.vector.tensor_tensor(count, per_tile[:, NT - 1], earlier[:, NT - 1], ALU.add))
            step(nc.vector.tensor_tensor(rank, bank[2][:, 0:NT * NE].rearrange("p (t e) -> p t e", t=NT), earlier, ALU.add))
            n_over, over_incl, over_at, shift = re[1], re[2], re[3], re[4]
            step(nc.vector.tensor_tensor(r11, count.unsqueeze(2).to_broadcast([P, NE, NT - 1]),
                                         iota_j.unsqueeze(1).to_broadcast([P, NE, NT - 1]), ALU.is_gt))
            step(nc.vector.tensor_reduce(n_over, r11, AX, ALU.add))
            step(nc.vector.tensor_tensor_scan(over_incl, ones[:, 0:NE], n_over, 0.0, ALU.mult, ALU.add))
            step(nc.vector.tensor_tensor(over_at, over_incl, n_over, ALU.subtract))
            step(nc.vector.tensor_scalar(shift, over_at, float(P), float(P * (NE - 1)), ALU.mult, ALU.add))
            step(nc.vector.tensor_tensor(re[5], shift, iota_e, ALU.subtract))
            step(nc.vector.tensor_scalar(rt[6], rank, float(P), None, ALU.is_ge))
            step(nc.vector.tensor_tensor(rt[7], rt[6], re[5].unsqueeze(1).to_broadcast([P, NT, NE]), ALU.mult))
            step(nc.vector.tensor_tensor(rt[8], rt[7], rank, ALU.add))
            step(nc.vector.tensor_tensor(rt[9], rt[8], iota_e.unsqueeze(1).to_broadcast([P, NT, NE]), ALU.add))
            for k in range(2):
                step(nc.vector.tensor_tensor(rt[6 + k], rt[1 + k], rt[9], ALU.mult))
                step(nc.vector.tensor_reduce(rs1[12 + k], rt[6 + k], AX, ALU.add))
                nc.vector.tensor_copy(slot[:, k], rs1[12 + k]).then_inc(slot_ready, 1)
            step(nc.vector.tensor_tensor(r23, over_incl.unsqueeze(1).to_broadcast([P, NOVER, NE]),
                                         iota_b.unsqueeze(2).to_broadcast([P, NOVER, NE]), ALU.is_le))
            step(nc.vector.tensor_reduce(over_f, r23, AX, ALU.add))
            step(nc.vector.tensor_scalar(over_e, over_f, float(NE - 1), None, ALU.min))
            step(nc.vector.tensor_copy(over_n, over_incl[:, NE - 1:NE]))
            dve.wait_ge(table_dma, 32)
            nc.vector.tensor_copy(slot_rows_f[0:NBLK], slot_rows[0:NBLK]).then_inc(rows_f, 1)
            dve.wait_ge(rows_T, 1)
            nc.vector.tensor_copy(slot_src, bank[2][:, 0:NBLK]).then_inc(table_ready, 1)

            def evac_xg(b, n):
                dve.wait_ge(xgt_done, b + 1)
                for k in range(2):
                    gain_evac(x_gT[n % 2][:, 4 * k:4 * k + 4], k, g_moe, xgt_evac)

            def expert(b, half, n, r):
                dve.wait_ge(e_silu, b + 1)
                nc.vector.tensor_tensor(act_e[n % 2], silu_g, bank[2][:, FE:2 * FE], ALU.mult).then_inc(e_act, 1)
                dve.wait_ge(et_done, b + 1)
                nc.vector.tensor_copy(act_T[n % 2], bank[4][:, 0:P]).then_inc(et_evac, 1)
                evac_xg(b + 1, n + 1)
                dve.wait_ge(y_done, b + 1)
                dve.wait_ge(y_sent[n % 2], 16 * half)
                nc.vector.tensor_copy(y_st[n % 2][:, HALF:], bank[6][:]).then_inc(y_evac_v, 1)

            evac_xg(0, 0)
            expert_blocks(dve, expert)
            overflow_blocks(dve, expert)

            dve.wait_ge(consts_here, 16 * 9)

            def add_experts(t):
                dve.wait_ge(yg_here[t % 2], 32 * (t // 2 + 1))
                for k in range(2):
                    if k == 1:
                        dve.wait_ge(f_add, 2 * t + 1)
                    nc.vector.scalar_tensor_tensor(H[:, t], y_g[t % 2][k], gate[:, k, t:t + 1], H[:, t], ALU.mult, ALU.add).then_inc(f_add, 1)

            add_experts(0)
            for t in range(NT):
                if t + 1 < NT:
                    add_experts(t + 1)
                dve.wait_ge(n_rs, len(norms) + t + 1)
                n = len(norms) + t
                nc.vector.scalar_tensor_tensor(out_st[t % 2], H[:, t], rs[:, 4 + n % 2:5 + n % 2], gf_row, ALU.mult, ALU.mult).then_inc(f_out, 1)

        @blk.tensor
        def _(pe):
            def transposes(banks, src, blocks, done, waits=()):
                for s, w in waits:
                    pe.wait_ge(s, w)
                for k in range(blocks):
                    last = nc.tensor.transpose(banks[k // 4][:, (k % 4) * P:(k % 4 + 1) * P], src(k), ident)
                last.then_inc(done, 1)

            pe.wait_ge(ident_made, 2)

            def transpose_x(i, j):
                pe.wait_ge(xs_ready[j], i + 1)
                pe.wait_ge(xf_evac, 2 * (2 * i + j))
                for k in range(KT):
                    last = nc.tensor.transpose(bank[k // 4][:, (k % 4) * P:(k % 4 + 1) * P], x_in[j][:, k * P:(k + 1) * P], ident)
                last.then_inc(xt_done[j], 1)

            def project(i, j, out, n, done):
                split_products(out[:], [(x_hi[j][:, k], x_lo[j][:, k], w_uvv_hi[n][:, k], w_uvv_lo[n][:, k])
                                        for k in range(KT)]).then_inc(done, 1)

            transpose_x(0, 0)
            pe.wait_ge(sgu_w_here, 16)
            for n in range(2):
                for h in range(4 * n, 4 * n + 4):
                    last = nc.tensor.transpose(bank[6 + n][:, (h % 4) * P:(h % 4 + 1) * P], sgu_nat[:, h], ident)
                last.then_inc(sgu_t, 1)

            def tile_work(i, j, last):
                t = 2 * i + j
                first = isinstance(t, int) and t == 0
                pe.wait_ge(lo_made, split_x(t) + 1)
                pe.wait_ge(v_gelu, t)
                project(i, j, bank[2], 1, v_done)
                if first:
                    pe.wait_ge(lo_made, W_UVV_PLACE[0] + 1)
                pe.wait_ge(u_gelu, t)
                project(i, j, bank[3], 0, u_done)
                if j == 0:
                    transpose_x(i, 1)
                elif not last:
                    transpose_x(i + 1, 0)
                if first:
                    pe.wait_ge(lo_made, W_UVV_PLACE[2] + 1)
                pe.wait_ge(att_copied, t)
                project(i, j, bank[4], 2, att_done)
                pe.wait_ge(vn_ready, t + 1)
                if first:
                    pe.wait_ge(sgu_evac, 2)
                pe.wait_ge(mix_bias, t)
                for h in range(NH):
                    mm = nc.tensor.matmul(bank[5][:, h * HD:(h + 1) * HD], sgu_wT[:, h], v_n[:, h * HD:(h + 1) * HD],
                                          start=True, stop=True)
                mm.then_inc(mix_done, 1)

            tiles(pe, tile_work)

            pe.wait_ge(mix_bias, NT)
            pe.wait_ge(att_copied, NT)
            def channel_tiles(i):
                for j in range(2):
                    pe.wait_ge(lo_made, split_w_qk(i, j) + 1)
                    pe.wait_ge(qk_evac_v[j], 2 * i)
                    pe.wait_ge(qk_evac_s[j], i)
                    for n in range(NCH):
                        c = slice(n * CH, (n + 1) * CH)
                        if is_first(i, j):
                            pe.wait_ge(lo_made, split_xT(n) + 1)
                        last = split_products(bank[3 * j + n][:], [(w_qk_hi[j][:, k], w_qk_lo[j][:, k], xT_hi[:, k, c], xT_lo[:, k, c])
                                                                   for k in range(KT)])
                    last.then_inc(qk_done[j], 1)

            first_then_loop(pe, NH // 2, channel_tiles)

            for j in range(2):
                pe.wait_ge(qk_evac_v[j], NH)
                pe.wait_ge(qk_evac_s[j], NH // 2)
            def head_pair(hp):
                base = NSTEP * hp

                def scores(s):
                    g = s // 2
                    keys = NA_GROUPS[g][0]
                    if s % 2 == 0:
                        pe.wait_ge(diag_ready, 2 * (NKG * hp + g + 1))
                    pe.wait_ge(s_biased, 2 * (base + s) - 2 if s >= 1 else 2 * base)
                    for n in range(2):
                        block = 2 * (s % 2) + n
                        q = q_diag[g % 2][:, block].rearrange("p h r c -> p (h r c)")
                        row0 = keys[0] * QROWS
                        k = qk[:, NPAIR + hp].rearrange("p (r c) -> p r c", c=GW)
                        k = k[:, row0:row0 + QROWS * len(keys), COL_START[block]:COL_START[block] + KC]
                        nc.tensor.matmul(bank[2 * (s % 2) + n][:, 0:P * len(keys)], q, k, start=True, stop=True).then_inc(s_done, 1)

                def transpose_p(s):
                    nk = len(NA_GROUPS[s // 2][0])
                    pe.wait_ge(p_exp, 2 * (base + s + 1))
                    pe.wait_ge(pt_evac_s, base + s)
                    pe.wait_ge(pt_evac_v, base + s)
                    for n in range(2):
                        for k in range(nk):
                            last = nc.tensor.transpose(bank[4 + n][:, k * P:(k + 1) * P], na_p[s % 2][:, n, k * P:(k + 1) * P], ident)
                    last.then_inc(pt_done, 1)

                def values(s):
                    keys = NA_GROUPS[s // 2][0]
                    pe.wait_ge(pt_evac_s, base + s + 1)
                    pe.wait_ge(pt_evac_v, base + s + 1)
                    pe.wait_ge(vals_here[keys[-1] // 2], 16 * 4 * 2)
                    pe.wait_ge(vals_here[keys[0] // 2], 16 * 4 * 2)
                    pe.wait_ge(o_evac, 2 * (base + s - 1) if s >= 1 else 2 * base)
                    for n in range(2):
                        for k, kg in enumerate(keys):
                            last = nc.tensor.matmul(bank[6 + s % 2][:, n * P:(n + 1) * P], na_pT[s % 2][:, n, k * P:(k + 1) * P],
                                                    vals[:, 4 * kg + 2 * (s % 2) + n, bass.ds(hp * P, P)],
                                                    start=(k == 0), stop=(k == len(keys) - 1))
                    last.then_inc(o_done, 1)

                for s in range(NSTEP + 2):
                    if s < NSTEP:
                        scores(s)
                    if 1 <= s <= NSTEP:
                        transpose_p(s - 1)
                    if s >= 2:
                        values(s - 2)

            first_then_loop(pe, NPAIR, head_pair)

            for j in range(2):
                pe.wait_ge(na_stored[j], 16 * 2 * NPAIR * NKG // 2)

            def transpose_y(i, j):
                pe.wait_ge(yb_ready[j], i + 1)
                pe.wait_ge(yT_evac, 2 * (2 * i + j))
                for k in range(KT):
                    last = nc.tensor.transpose(bank[k // 4][:, (k % 4) * P:(k % 4 + 1) * P], y_cat[j][:, k * P:(k + 1) * P], ident)
                last.then_inc(yt_done[j], 1)

            transpose_y(0, 0)

            def out_tile(i, j, last):
                if j == 0:
                    transpose_y(i, 1)
                elif not last:
                    transpose_y(i + 1, 0)
                t = 2 * i + j
                pe.wait_ge(lo_made, split_y(t) + 1)
                pe.wait_ge(h_added[j], 2 * i)
                for n in range(2):
                    mm = split_products(bank[2 + 2 * j + n][:], [(y_hi[j][:, k], y_lo[j][:, k], w_out_hi[n][:, k], w_out_lo[n][:, k])
                                                                 for k in range(KT)])
                mm.then_inc(wo_done, 1)

            tiles(pe, out_tile)
            for j in range(2):
                pe.wait_ge(h_added[j], NT)

            for what, n in stages:
                if what == "T":
                    pe.wait_ge(n_ready, n + 1)
                    pe.wait_ge(nt_evac, 2 * n)
                    for k in range(KT):
                        last = nc.tensor.transpose(bank[k // 4][:, (k % 4) * P:(k % 4 + 1) * P], hs[n % 2][:, k * P:(k + 1) * P], ident)
                    last.then_inc(nt_done, 1)
                elif what == "mm":
                    kind, *which = groups[n]
                    b = bank[4 + n % 2]
                    if n >= 2:
                        pe.wait_ge(mm_evac, n - 1)
                    if kind == "k_mem":
                        pe.wait_ge(w_xkv_here, 16)
                        pe.wait_ge(nt_evac, 2 * 4)
                        h = which[0]
                        steps = [(w_xkv[:, k, h * P:(h + 1) * P], mem_T[:, k]) for k in range(KT)]
                    elif kind == "v_mem":
                        m = which[0]
                        steps = [(mem_T[:, k, m * P:(m + 1) * P], w_xkv[:, k, HALF:]) for k in range(KT)]
                    elif kind == "q":
                        c, h = which
                        pe.wait_ge(w_xq_here, 16)
                        pe.wait_ge(nt_evac, 2 * (n_norms["h", TPC * c + TPC - 1] + 1))
                        steps = [(w_xq[:, k, h * P:(h + 1) * P], h_T[:, k]) for k in range(KT)]
                    elif kind == "o":
                        c, h = which
                        pe.wait_ge(ptx_evac, 8 * (c + 1))
                        seq = 0 if c * CH < SEQ_P else 1
                        steps = [(v_mem[:, 2 * seq + m, h * P:(h + 1) * P], pT_x[:, h, m]) for m in range(2)]
                    elif kind == "xo":
                        t, half = which
                        pe.wait_ge(w_xo_here, 16)
                        pe.wait_ge(mm_evac, n_groups["o", t // TPC, XH - 1] + 1)
                        q = t % TPC
                        steps = [(o_T[:, h, q * P:(q + 1) * P], w_xo[:, h, half * HALF:(half + 1) * HALF]) for h in range(XH)]
                    else:
                        t = which[0]
                        pe.wait_ge(w_rt_here, 32)
                        pe.wait_ge(nt_evac, 2 * (n_norms["moe", t] + 1))
                        b = b[:, 0:NG + NE]
                        steps = [(r_T[t % 2][:, k], w_rt[:, k]) for k in range(KT)]
                    for k, (w, x) in enumerate(steps):
                        mm = nc.tensor.matmul(b if kind == "route" else b[:], w, x, start=(k == 0), stop=(k == len(steps) - 1))
                    mm.then_inc(mm_done, 1)
                elif what == "S":
                    c, t, hp = n // 8, (n % 8) // 2, n % 2
                    seq = 0 if c * CH < SEQ_P else 1
                    pe.wait_ge(mm_evac, n_groups["q", c, XH - 1] + 1)
                    if n >= 2:
                        pe.wait_ge(px_exp, 2 * (n - 1))
                    for h in (2 * hp, 2 * hp + 1):
                        mm = nc.tensor.matmul(bank[6 + n % 2][:, (h % 2) * N_MEM:(h % 2 + 1) * N_MEM],
                                              q_x[c % 2][:, h, t * P:(t + 1) * P], k_mem[:, h, seq * N_MEM:(seq + 1) * N_MEM],
                                              start=True, stop=True)
                    mm.then_inc(sx_done, 1)
                elif what == "PT":
                    pe.wait_ge(px_ready, n + 1)
                    if n >= 2:
                        pe.wait_ge(ptx_evac, n - 1)
                    for h in range(2):
                        for m in range(2):
                            last = nc.tensor.transpose(bank[2 + n % 2][:, (2 * h + m) * P:(2 * h + m + 1) * P],
                                                       p_x[n % 4][:, h, m * P:(m + 1) * P], ident)
                    last.then_inc(ptx_done, 1)

            pe.wait_ge(route_const, 10)
            pe.wait_ge(chosen, 1)
            pe.wait_ge(ptx_evac, 8 * NCH)
            flat = rt[3].rearrange("p t e -> p (t e)")
            nc.tensor.matmul(bank[2][:, 0:NT * NE], before, flat, start=True, stop=True)
            nc.tensor.matmul(bank[3][:, 0:NT * NE], ones, flat, start=True, stop=True).then_inc(count_done, 1)
            pe.wait_ge(rows_f, 1)
            nc.tensor.transpose(bank[2][:, 0:NBLK], slot_rows_f[0:NBLK], ident[0:NBLK, 0:NBLK]).then_inc(rows_T, 1)
            pe.wait_ge(table_ready, 1)

            def transpose_xg(b, half, n):
                pe.wait_ge(xg_here[n % 2], 16 * (half + 1))
                pe.wait_ge(xgt_evac, 2 * b)
                for k in range(KT):
                    last = nc.tensor.transpose(bank[k // 4][:, (k % 4) * P:(k % 4 + 1) * P], x_g[n % 2][:, k * P:(k + 1) * P], ident)
                last.then_inc(xgt_done, 1)

            def expert(b, half, n, r):
                pe.wait_ge(xgt_evac, 2 * (b + 1))
                pe.wait_ge(w_e_here[n], 48 * (r + 1))
                for k in range(KT):
                    mm = nc.tensor.matmul(bank[2][:, 0:2 * FE], x_gT[n % 2][:, k], w_gu[n][:, :, k], start=(k == 0), stop=(k == KT - 1))
                mm.then_inc(gu_done, 1)
                transpose_xg(b + 1, half + n % 2, n + 1)
                pe.wait_ge(e_act, b + 1)
                nc.tensor.transpose(bank[4][:, 0:P], act_e[n % 2], ident).then_inc(et_done, 1)
                pe.wait_ge(et_evac, b + 1)
                pe.wait_ge(y_evac_s, b)
                pe.wait_ge(y_evac_v, b)
                for k in range(2):
                    mm = nc.tensor.matmul(bank[5 + k][:], act_T[n % 2], w_dn[n][:, k * HALF:(k + 1) * HALF], start=True, stop=True)
                mm.then_inc(y_done, 1)

            transpose_xg(0, 0, 0)
            expert_blocks(pe, expert)
            overflow_blocks(pe, expert)

        return nc


INPUTS = ["x_prompt", "x_sample", "mem_prompt", "mem_sample", "g_mix", "w_in", "g_sgu_v", "sgu_w", "sgu_b", "na_rpb",
          "g_out_a", "g_out_b", "w_out", "g_xattn", "g_mem", "w_xq", "w_xkv", "w_xo", "g_moe", "w_router_group",
          "w_router_expert", "w_exp_gate", "w_exp_up", "w_exp_down", "g_final"]


def kernel(**inputs):
    import numpy as np
    import concourse.bacc as bacc
    from concourse.bass_utils import run_bass_kernel_spmd

    nc = bacc.Bacc("TRN2", target_bir_lowering=False, num_devices=1)
    arrays, aps = {}, {}
    for name in INPUTS:
        v = np.ascontiguousarray(inputs[name])
        arrays[f"in_{name}"] = v
        aps[name] = nc.dram_tensor(f"in_{name}", v.shape, mybir.dt.from_np(v.dtype), kind="ExternalInput").ap()
    outs = [nc.dram_tensor(f"out_{n}", (1, rows, D), F32, kind="ExternalOutput").ap() for n, rows in (("prompt", SEQ_P), ("sample", SEQ_S))]
    hymba_encoder(nc, aps, *outs)
    r = run_bass_kernel_spmd(nc, [arrays], core_ids=[0])
    return tuple(r.results[0][n] for n in ("out_prompt", "out_sample"))
```

```python
import concourse.bass as bass
from concourse import mybir
from contextlib import ExitStack

F32 = mybir.dt.float32
F32R = mybir.dt.float32r
I32 = mybir.dt.int32
ALU = mybir.AluOpType
ACT = mybir.ActivationFunctionType
AX = mybir.AxisListType.X

P = 128
D = 1024
KT = D // P
SEQ_P, SEQ_S = 512, 1024
T = SEQ_P + SEQ_S
NT = T // P
CH = 512
NCH = T // CH
N_MEM = 256
HALF = 512
NH = 8
HD = 64
NPAIR = NH // 2
GW = 64
KC = 32
QC = 16
QROWS = 4
GTOK = QROWS * GW
NKG = T // GTOK
KREL = 12
XH = 4
NG, EPG = 4, 8
NE = NG * EPG
FE = 128
EPS = 1e-6
MASKED = -1.0e30
NA_SCALE = HD ** -0.5
XA_SCALE = P ** -0.5
NA_GROUPS = [((0, 1), 4, False), ((0, 1), 0, False),
             ((2, 3), 4, False), ((2, 3, 4), 0, True), ((3, 4, 5), 0, True), ((4, 5), 0, False)]
COL_START = [0, 8, 24, 32]
NOVER = (2 * T + NE * (P - 1)) // P - NE
NOVER += 4 - NOVER % 4
NBLK = NE + NOVER
RING = 8
YRING = 4


def hymba_encoder(nc, a, y_prompt, y_sample):
    ctx = ExitStack()
    with ctx:
        def sem(name):
            return ctx.enter_context(nc.semaphore(name))

        def pair(name):
            return [sem(f"{name}_{j}") for j in range(2)]

        used = [0]

        def at(kb, *shape, dt=F32):
            used[0] += 1
            base = nc.sbuf_base + (-nc.sbuf_base) % 32
            return nc.alloc_sbuf_tensor_at(f"at_{kb}_{used[0]}".replace(".", "_"), [P, *shape], dt, offset=base + int(kb * 1024))[:]

        bank = [ctx.enter_context(nc.psum_tensor(f"bank{i}", [P, 512], F32)) for i in range(8)]

        def dram(name, shape, dt=F32):
            return nc.dram_tensor(name, shape, dt, kind="Internal").ap()

        y_mix = dram("y_mix", [T, 2 * HALF])
        v_att = dram("v_att", [T, HALF])
        rpb_pad = dram("rpb_pad", [NH * 15, 96])
        xn_moe = dram("xn_moe", [T, D])
        y_exp = dram("y_exp", [NBLK * P, D])

        ident = at(192, P)
        small = at(192.5, 224)
        g_mix, g_xattn, g_mem, g_moe, g_out = (small[:, 8 * n:8 * n + 8] for n in range(5))
        sgu_b = small[:, 40:48]
        neg_half = small[:, 48:49]
        eps = small[:, 49:50]
        ms = small[:, 64:96]
        ms_eps = small[:, 96:128]
        rs = small[:, 128:160]
        na_st = small[:, 160:192]
        xa_st = small[:, 192:224]
        w_uvv = [at(16 * n, KT, HALF) for n in range(3)]
        xT = at(48, KT, T)
        x_in = [at(144 + 4 * j, D) for j in range(2)]
        w_uvv_lo = [at(16 * n, KT, HALF, dt=F32R) for n in range(3)]
        w_uvv_hi = [at(96 + 16 * n, KT, HALF, dt=F32R) for n in range(3)]
        x_hi = [at(152 + 4 * j, KT, P, dt=F32R) for j in range(2)]
        x_lo = [at(160 + 4 * j, KT, P, dt=F32R) for j in range(2)]
        v_g, v_n, u_g, mixed, y_a = (at(168 + 2 * n, HALF) for n in range(5))
        y_an = [at(178 + 2 * j, HALF) for j in range(2)]
        v_st = [at(182 + 2 * j, HALF) for j in range(2)]
        sq_junk = at(186, HALF)
        x_junk0, x_junk = at(168, D), at(188, D)
        sgu_nat = at(188, NH, P)
        sgu_wT = at(194, NH, P)
        gv_row = at(198, HALF)
        na_bias = at(96, NPAIR, 3, KREL, KC)
        na_bias_row = at(114, NPAIR, 3, KREL, KC)
        w_qk = [at(132 + 4 * j, KT, P) for j in range(2)]
        w_qk_hi = [at(kb, KT, P, dt=F32R) for kb in (140, 194)]
        w_qk_lo = [at(132 + 4 * j, KT, P, dt=F32R) for j in range(2)]
        xT_hi = at(0, KT, T, dt=F32R)
        xT_lo = at(48, KT, T, dt=F32R)
        bias_src = at(200, 3, 15, KC)
        pad_t = at(206, 96)
        qk = at(144, NH, T)
        vals = at(0, NKG * 4, HALF)
        q_diag = [at(132 + 2 * j, 4, 2, QROWS, QC) for j in range(2)]
        na_o = [at(136 + j, 4, HD) for j in range(2)]
        na_p = [at(138 + 3 * j, 2, KREL * KC) for j in range(2)]
        na_pT = [at(194 + 3 * j, 2, KREL * KC) for j in range(2)]

        H = at(0, NT, D)
        w_out = [at(48 + 16 * n, KT, HALF) for n in range(2)]
        w_out_hi = [at(kb, KT, HALF, dt=F32R) for kb in (80, 128)]
        w_out_lo = [at(48 + 16 * n, KT, HALF, dt=F32R) for n in range(2)]
        y_cat = [at(96 + 4 * j, D) for j in range(2)]
        x_res = [at(104 + 4 * j, D) for j in range(2)]
        y_T = [at(112 + 4 * j, KT, P) for j in range(2)]
        y_hi = [at(176 + 4 * j, KT, P, dt=F32R) for j in range(2)]
        y_lo = [at(112 + 4 * j, KT, P, dt=F32R) for j in range(2)]
        yb_junk = at(200, HALF)
        mem_in = [at(kb, D) for kb in (120, 124, 184, 188)]
        w_xkv = at(144, KT, D)
        mem_T = at(64, KT, 4 * P)
        k_mem = at(128, XH, 4 * P)
        v_mem = at(136, 4, HALF)
        hs = [at(194 + 4 * j, D) for j in range(2)]
        w_xq = at(80, KT, HALF)
        w_xo = at(144, XH, D)
        w_xo_hi = at(176, XH, D, dt=F32R)
        w_xo_lo = at(144, XH, D, dt=F32R)
        h_T = at(48, KT, CH)
        q_x = [at(160, XH, CH), at(96 + 24, XH, CH)]
        p_x = [at(72 + 2 * n, 2, N_MEM) for n in range(4)]
        pT_x = at(96, XH, 2, CH)
        o_hi, o_lo = at(64, XH, CH, dt=F32R), at(112, XH, CH, dt=F32R)
        r_T = [at(168 + 4 * j, KT, P) for j in range(2)]
        w_rt = at(202, KT, NG + NE)
        logit = at(203.25, NT, NG + NE)
        gate = at(205, 2, NT)
        slot = at(205.25, 2, NT, dt=I32)
        slot_src = at(205.5, NBLK, dt=I32)
        over_e = at(205.75, NOVER, dt=I32)
        zeros = at(206.5, 256)
        over_n = at(206.25, 1, dt=I32)
        rt = [at(144 + 1.5 * n, NT, NE) for n in range(10)]
        rs8 = [at(160 + 0.375 * n, NT, EPG) for n in range(12)]
        rs1 = [at(164.5 + 0.0625 * n, NT) for n in range(16)]
        re = [at(165.5 + 0.125 * n, NE) for n in range(10)]
        r11 = at(176, NE, NT - 1)
        r23 = at(178, NOVER, NE)
        over_f = at(181, NOVER)
        iota_e = at(193.375, NE)
        place_i = at(193.875, NT, dt=I32)
        iota_b = at(193.5, NOVER)
        iota_j = at(193.625, NT - 1)
        first_g = at(193.6875, NG)
        first_e = at(193.75, EPG)
        token = at(193.8125, NT)
        before = at(184.25, P)
        ones = at(184.75, P)
        iota_p = at(185.25, P)
        iota_blk = at(185.75, NBLK)
        in_place = [at(kb, NT, P, dt=F32R) for kb in (186, 168)]
        in_block = [at(kb, NT, NBLK, dt=F32R) for kb in (174, 181.5)]

        slots_kb = [48 + 12 * n for n in range(RING)]
        w_gu = [at(kb, 2, KT, FE) for kb in slots_kb]
        w_dn = [at(kb + 8, D) for kb in slots_kb]
        x_g = [at(144 + 4 * j, D) for j in range(2)]
        x_gT = [at(152 + 4 * j, KT, P) for j in range(2)]
        silu_g = at(160, P)
        act_T = [at(161.5 + 0.5 * j, P) for j in range(2)]
        y_st = [at(164 + 4 * j, D) for j in range(2)]
        y_g = [[at(48 + 8 * j + 4 * n, D) for n in range(2)] for j in range(YRING)]
        out_st = [at(160 + 4 * j, D) for j in range(2)]
        gf_row = at(172, D)

        blk = ctx.enter_context(nc.Block())

        w_in_here = [sem(f"w_in_here_{n}") for n in range(3)]
        w_v_here = sem("w_v_here")
        consts_here = sem("consts_here")
        sgu_w_here = sem("sgu_w_here")
        x_here = pair("x_here")
        w_qk_here = pair("w_qk_here")
        pad_here, bias_here = sem("pad_here"), sem("bias_here")
        vals_here = [sem(f"vals_here_{n}") for n in range(NKG // 2)]
        v_stored, ya_stored = pair("v_stored"), pair("ya_stored")
        na_stored = pair("na_stored")
        const_made, ident_made, fill_made, bias_neg = (sem(n) for n in ("const_made", "ident_made", "fill_made", "bias_neg"))
        x_sq, x_eps, x_rs, xs_ready, xt_done = (pair(n) for n in ("x_sq", "x_eps", "x_rs", "xs_ready", "xt_done"))
        xf_evac = sem("xf_evac")
        sgu_t, sgu_evac = sem("sgu_t"), sem("sgu_evac")
        v_done, u_done, v_gelu, u_gelu, v_sq, v_eps, v_rs, vn_ready, mix_done, mix_bias, ya_mul, ya_sq, ya_eps, ya_rs, yan_ready = (
            sem(n) for n in ("v_done", "u_done", "v_gelu", "u_gelu", "v_sq", "v_eps", "v_rs", "vn_ready", "mix_done",
                             "mix_bias", "ya_mul", "ya_sq", "ya_eps", "ya_rs", "yan_ready"))
        att_done, att_copied = sem("att_done"), sem("att_copied")
        qk_done, qk_evac_v, qk_evac_s = pair("qk_done"), pair("qk_evac_v"), pair("qk_evac_s")
        hi_made, lo_made = sem("hi_made"), sem("lo_made")
        diag_zero, diag_ready, s_done, s_biased, s_min, p_exp, s_rcp = (
            sem(n) for n in ("diag_zero", "diag_ready", "s_done", "s_biased", "s_min", "p_exp", "s_rcp"))
        pt_done, pt_evac_s, pt_evac_v, o_done, o_evac = (
            sem(n) for n in ("pt_done", "pt_evac_s", "pt_evac_v", "o_done", "o_evac"))

        w_out_here, w_xkv_here, w_xq_here, w_xo_here, w_rt_here = (sem(n) for n in ("w_out_here", "w_xkv_here", "w_xq_here", "w_xo_here", "w_rt_here"))
        y_here, xr_here = pair("y_here"), pair("xr_here")
        yb_ready, yt_done = pair("yb_ready"), pair("yt_done")
        yT_evac, wo_done, h_added = sem("yT_evac"), sem("wo_done"), pair("h_added")
        mem_here = pair("mem_here")
        n_sq, n_eps, n_rs, n_ready, nt_done, nt_evac = (sem(n) for n in ("n_sq", "n_eps", "n_rs", "n_ready", "nt_done", "nt_evac"))
        xn_stored = pair("xn_stored")
        mm_done, mm_evac = sem("mm_done"), sem("mm_evac")
        sx_done, sx_max, sx_neg, px_exp, sx_rcp, px_ready, ptx_done, ptx_evac = (
            sem(n) for n in ("sx_done", "sx_max", "sx_neg", "px_exp", "sx_rcp", "px_ready", "ptx_done", "ptx_evac"))
        route, route_exp, exp_done, chosen, route_const, count_done, slot_ready = (
            sem(n) for n in ("route", "route_exp", "exp_done", "chosen", "route_const", "count_done", "slot_ready"))
        slots_done, table_ready = (
            sem(n) for n in ("slots_done", "table_ready"))
        w_e_here = [sem(f"w_e_here_{n}") for n in range(RING)]
        xg_here = pair("xg_here")
        xgt_done, xgt_evac, gu_done, e_silu, e_act, y_done, y_evac_s, y_evac_v = (
            sem(n) for n in ("xgt_done", "xgt_evac", "gu_done", "e_silu", "e_act", "y_done", "y_evac_s", "y_evac_v"))
        y_sent, all_sent, unused_filled = pair("y_sent"), sem("all_sent"), sem("unused_filled")
        f_add, f_out = sem("f_add"), sem("f_out")
        yg_here, out_sent = [sem(f"yg_here_{n}") for n in range(YRING)], pair("out_sent")

        TPC = CH // P
        norms = [("mem", n) for n in range(4)] + [("h", t) for t in range(NT)] + [("moe", t) for t in range(NT)]
        groups = []
        stages = []

        def mm(*group):
            stages.append(("mm", len(groups)))
            groups.append(group)

        def T_of(*norm):
            stages.append(("T", norms.index(norm)))

        def interleave(*lists):
            longest = max(len(calls) for calls in lists)
            for n in range(longest):
                for calls in lists:
                    for m in range(n * len(calls) // longest, (n + 1) * len(calls) // longest):
                        calls[m][0](*calls[m][1:])

        def routing_of(tiles):
            calls = [(T_of, "moe", tiles[0])]
            for t, nxt in zip(tiles, tiles[1:]):
                calls += [(mm, "route", t), (T_of, "moe", nxt)]
            return calls + [(mm, "route", tiles[-1])]

        def S(n):
            stages.append(("S", n))

        def PT(n):
            stages.append(("PT", n))

        for n in range(4):
            T_of("mem", n)
        interleave([(mm, "k_mem", h) for h in range(XH)] + [(mm, "v_mem", n) for n in range(2)],
                   [(T_of, "h", n) for n in range(TPC)])
        for n in range(2, 4):
            mm("v_mem", n)
        for h in range(XH):
            mm("q", 0, h)
        interleave([(S, n) for n in range(4)], [(T_of, "h", TPC + n) for n in range(TPC)])
        def xo_of(c):
            return [(mm, "xo", TPC * c + t, half) for t in range(TPC) for half in range(2)]

        for c in range(NCH):
            softmax = [] if c == 0 else [(S, 8 * c + n) for n in range(4)]
            for n in range(8):
                softmax.append((PT, 8 * c + n))
                if n < 4:
                    softmax.append((S, 8 * c + 4 + n))
            if c == 0:
                interleave(softmax, [(mm, "q", 1, h) for h in range(XH)])
            elif c + 1 < NCH:
                interleave(softmax, xo_of(c - 1), [(T_of, "h", TPC * (c + 1) + n) for n in range(TPC)]
                           + [(mm, "q", c + 1, h) for h in range(XH)])
            else:
                interleave(softmax, xo_of(c - 1), routing_of(range(TPC)))
            for h in range(XH):
                mm("o", c, h)
        xo, last = xo_of(NCH - 1), 2 * TPC
        interleave(xo, routing_of(range(TPC, 2 * TPC)) + [(T_of, "moe", last), (mm, "route", last)])
        T_of("moe", last + 1)
        T_of("moe", last + 2)
        mm("route", last + 1)
        T_of("moe", last + 3)
        mm("route", last + 2)
        mm("route", last + 3)
        place = {st: n for n, st in enumerate(stages)}
        sq_at, pre_at = {0: 0, 1: 0}, {0: 0}
        for n in range(2, len(norms)):
            sq_at[n] = place["T", n - 2] + 1
        for n in range(1, len(norms)):
            pre_at[n] = place["T", n - 1]
        for n, (kind, t) in enumerate(norms):
            if kind == "moe":
                after = place["mm", groups.index(("xo", t, 1))] + 1
                sq_at[n] = max(sq_at[n], after)
                pre_at[n] = max(pre_at[n], min(after + 1, place["T", n]))
        order = []
        scaled = 0
        for k, st in enumerate(stages):
            order += [("sq", n) for n in range(len(norms)) if sq_at[n] == k]
            order += [("pre", n) for n in range(len(norms)) if pre_at[n] == k]
            if st[0] == "PT":
                order += [("px", n) for n in range(scaled, st[1] + 1)]
                scaled = max(scaled, st[1] + 1)
            order.append(st)
            if st[0] == "S" and st[1] - 1 >= scaled:
                order += [("px", n) for n in range(scaled, st[1])]
                scaled = st[1]
        n_groups = {g: n for n, g in enumerate(groups)}
        n_norms = {g: n for n, g in enumerate(norms)}

        def norm_bank(n):
            kind, t = norms[n]
            return 2 if (kind == "mem" or kind == "moe" and t > 2 * TPC) and t % 2 == 1 else 0

        def expert_blocks(eng, body):
            rounds = NE // RING
            for n in range(RING):
                body(n, n // 2, n, 0)
            with eng.Fori(1, rounds - 1) as r:
                for n in range(RING):
                    body(RING * r + n, RING // 2 * r + n // 2, n, r)
            for n in range(RING):
                r = rounds - 1
                body(RING * r + n, RING // 2 * r + n // 2, n, r)

        def overflow_blocks(eng, body):
            used = eng.value_load(over_n[0:1, 0:1], min_val=0, max_val=NOVER)
            with eng.Fori(0, NOVER // 4) as i:
                for n in range(4):
                    with eng.If(used > 4 * i + n):
                        body(NE + 4 * i + n, NE // 2 + 2 * i + n // 2, n, NE // RING + i)

        NSTEP = 2 * NKG

        def is_first(i, j):
            return isinstance(i, int) and i == 0 and j == 0

        W_UVV_PLACE = {1: 1, 0: 3, 2: 4}

        def split_x(t):
            return 2 if isinstance(t, int) and t == 0 else 4 + t

        def split_xT(n):
            return 4 + NT + (0 if n == 0 else n + 1)

        def split_w_qk(i, j):
            if is_first(i, j):
                return split_xT(0) + 1
            return 4 + NT + NCH + 2 * i + j

        def split_w_out(n):
            return 4 + NT + NCH + NH + 2 * n

        def split_y(t):
            return 4 + NT + NCH + NH + (1 if isinstance(t, int) and t == 0 else 2 + t)

        SPLIT_W_XO = split_y(NT - 1) + 1

        def split_o(c, h):
            return SPLIT_W_XO + 1 + XH * c + h

        def make_hi(act, place, hi, x):
            nc.scalar.activation(hi, x, ACT.Copy).then_inc(hi_made, 1)

        def make_lo(dve, place, lo, x, hi):
            dve.wait_ge(hi_made, place + 1)
            nc.vector.tensor_tensor(lo, x, hi.bitcast(F32), ALU.subtract).then_inc(lo_made, 1)

        def split_products(out, terms):
            for k, (w_hi, w_lo, x_hi, x_lo) in enumerate(terms):
                nc.tensor.matmul(out, w_hi, x_hi, start=(k == 0), stop=False)
                nc.tensor.matmul(out, w_lo, x_hi, start=False, stop=False)
                last = nc.tensor.matmul(out, w_hi, x_lo, start=False, stop=(k == len(terms) - 1))
            return last

        def first_then_loop(eng, n, body):
            body(0)
            with eng.Fori(1, n) as i:
                body(i)

        def tiles(eng, body, pairs=NT // 2):
            for j in range(2):
                body(0, j, False)
            with eng.Fori(1, pairs - 1) as i:
                for j in range(2):
                    body(i, j, False)
            for j in range(2):
                body(pairs - 1, j, j == 1)

        def out_tiles(eng, body):
            for j in range(2):
                body(0, j, False, False)
            with eng.Fori(1, NT // 2 - 1) as i:
                for j in range(2):
                    body(i, j, False, False)
            for j in range(2):
                body(NT // 2 - 1, j, j == 1, True)

        @blk.sync
        def _(sp):
            w_in = a["w_in"][0].rearrange("(k p) n -> p k n", p=P)

            def column(name):
                return a[name][0].rearrange("(k p) -> p k", p=P)

            sp.dma_start(w_uvv[1][:, 0:KT // 2], w_in[:, 0:KT // 2, HALF:2 * HALF]).then_inc(w_v_here, 16)
            sp.dma_start(w_uvv[1][:, KT // 2:], w_in[:, KT // 2:, HALF:2 * HALF]).then_inc(w_in_here[1], 16)
            sp.dma_start(g_mix, column("g_mix"), allow_slow_non_contiguous=True).then_inc(consts_here, 16)
            sp.dma_start(sgu_nat, a["sgu_w"][0].rearrange("h p q -> p h q")).then_inc(sgu_w_here, 16)
            sp.dma_start(g_xattn, column("g_xattn"), allow_slow_non_contiguous=True).then_inc(consts_here, 16)
            sp.dma_start(g_mem, column("g_mem"), allow_slow_non_contiguous=True).then_inc(consts_here, 16)
            sp.dma_start(g_moe, column("g_moe"), allow_slow_non_contiguous=True).then_inc(consts_here, 16)
            sp.dma_start(g_out[:, 0:4], column("g_out_a"), allow_slow_non_contiguous=True).then_inc(consts_here, 16)
            sp.dma_start(g_out[:, 4:8], column("g_out_b"), allow_slow_non_contiguous=True).then_inc(consts_here, 16)
            sp.dma_start(sgu_b, a["sgu_b"][0].rearrange("h p -> p h"), allow_slow_non_contiguous=True).then_inc(consts_here, 16)
            sp.dma_start(gv_row, a["g_sgu_v"][0].partition_broadcast(P)).then_inc(consts_here, 16)
            sp.dma_start(w_uvv[0], w_in[:, :, 0:HALF]).then_inc(w_in_here[0], 16)
            sp.dma_start(w_uvv[2], w_in[:, :, 4 * HALF:5 * HALF]).then_inc(w_in_here[2], 16)

            rpb = a["na_rpb"][0]
            sp.wait_ge(fill_made, 1)
            sp.dma_start(pad_t[0:NH * 15, 39:55], rpb.rearrange("h r c -> (h r) c")[:, 7:23]).then_inc(pad_here, 16)
            sp.wait_ge(pad_here, 16)
            sp.dma_start(rpb_pad, pad_t[0:NH * 15, :]).then_inc(pad_here, 16)
            sp.wait_ge(pad_here, 32)
            sp.wait_ge(fill_made, 2)
            pad = rpb_pad.rearrange("(h r) c -> h r c", r=15)
            spread = 0
            for qc in range(QC):
                dst = bias_src[qc:P:QC]
                for kind in range(3):
                    start = (47, 39, 31)[kind] - qc
                    if kind == 0 and qc < 8:
                        d, s = dst[:, 0, :, 0:QC], rpb[:, :, 15 - qc:31 - qc]
                    elif kind == 2 and qc > 8:
                        d, s = dst[:, 2, :, QC:KC], rpb[:, :, 15 - qc:31 - qc]
                    else:
                        d, s = dst[:, kind], pad[:, :, start:start + KC]
                    sp.dma_start(d, s).then_inc(bias_here, 16)
                    spread += 16
            sp.wait_ge(bias_here, spread)

            def channel_tiles(i):
                for j in range(2):
                    sp.wait_ge(qk_done[j], i)
                    sp.dma_start(w_qk[j], w_in[:, :, bass.ds(2 * HALF + (2 * i + j) * P, P)]).then_inc(w_qk_here[j], 16)

            def spread_bias(h):
                for qr in range(QROWS):
                    p0 = (h % 2) * HD + qr * QC
                    src = bias_src[h * QC:(h + 1) * QC]
                    sp.dma_start(na_bias[p0:p0 + QC, h // 2], src[:, :, 3 - qr:15 - qr]).then_inc(bias_here, 16)
                    sp.dma_start(na_bias_row[p0:p0 + QC, h // 2, :, qr:qr + 8], src[:, :, 3:11]).then_inc(bias_here, 16)

            sp.wait_ge(att_done, NT)
            channel_tiles(0)
            sp.wait_ge(bias_neg, 2)
            for h in range(NH // 2):
                spread_bias(h)
            channel_tiles(1)
            for h in range(NH // 2, NH):
                spread_bias(h)
            with sp.Fori(2, NH // 2) as i:
                channel_tiles(i)

            for j in range(2):
                sp.wait_ge(v_stored[j], 16 * NT // 2)
                sp.wait_ge(qk_done[j], NH // 2)
            for g in range(NKG):
                rows = v_att[g * GTOK:(g + 1) * GTOK].rearrange("(r c) n -> r c n", c=GW)
                for n in range(4):
                    sp.dma_start(vals[:, 4 * g + n], rows[:, COL_START[n]:COL_START[n] + KC]).then_inc(vals_here[g // 2], 16)
            def store_group(hp, g):
                sp.wait_ge(o_evac, 4 * (NKG * hp + g + 1))
                for half in range(2):
                    dst = y_mix[g * GTOK:(g + 1) * GTOK, bass.ds(HALF + (2 * hp + half) * HD, HD)]
                    sp.dma_start(dst.rearrange("(n q) d -> q n d", n=4),
                                 na_o[g % 2][half * HD:(half + 1) * HD]).then_inc(na_stored[g % 2], 16)

            def head_pair(hp):
                for g in range(NKG):
                    store_group(hp, g)

            def load_w_out(part):
                n, k = part // KT, part % KT
                sp.dma_start(w_out[n][:, k], a["w_out"][0][k * P:(k + 1) * P, n * HALF:(n + 1) * HALF]).then_inc(w_out_here, 16)

            for g in range(NKG):
                store_group(0, g)
                for part in range(3 * g, min(3 * g + 3, 2 * KT)):
                    load_w_out(part)
            with sp.Fori(1, NPAIR - 1) as hp:
                head_pair(hp)
            for g in range(NKG - 1):
                store_group(NPAIR - 1, g)

            def load_rows(i, j, x_rows):
                if not (isinstance(i, int) and i == 0):
                    sp.wait_ge(yt_done[j], i)
                sp.dma_start(y_cat[j], y_mix[bass.ds((2 * i + j) * P, P)]).then_inc(y_here[j], 16)
                if not (isinstance(i, int) and i == 0):
                    sp.wait_ge(h_added[j], 2 * i)
                x_rows = x_rows.rearrange("(r n c) d -> n r c d", n=4, c=QC)
                for n in range(2):
                    sp.dma_start(x_res[j][n * HD:(n + 1) * HD], x_rows[2 * j + n]).then_inc(xr_here[j], 16)

            for j in range(2):
                sp.wait_ge(ya_stored[j], 16 * 2 * NT // 2)
            sp.wait_ge(na_stored[0], 32 * (3 * (NPAIR - 1) + 1))
            sp.wait_ge(s_biased, 2 * NPAIR * NSTEP)
            for j in range(2):
                load_rows(0, j, a["x_prompt"][0][0:GTOK])
            store_group(NPAIR - 1, NKG - 1)
            for j in range(2):
                sp.wait_ge(na_stored[j], 16 * 2 * NPAIR * NKG // 2)
            sp.dma_start(w_xkv, a["w_xkv"][0].rearrange("(k p) n -> p k n", p=P)).then_inc(w_xkv_here, 16)
            sp.dma_start(w_rt[:, :, 0:NG], a["w_router_group"][0].rearrange("(k p) n -> p k n", p=P)).then_inc(w_rt_here, 16)
            sp.dma_start(w_rt[:, :, NG:], a["w_router_expert"][0].rearrange("(k p) n -> p k n", p=P)).then_inc(w_rt_here, 16)
            for n, rows in enumerate((a["mem_prompt"][0], a["mem_sample"][0])):
                for j in range(2):
                    sp.dma_start(mem_in[2 * n + j], rows[j * P:(j + 1) * P]).then_inc(mem_here[j], 16)
            for j in range(2):
                load_rows(1, j, a["x_prompt"][0][GTOK:2 * GTOK])
            with sp.Fori(2, NT // 2) as i:
                for j in range(2):
                    load_rows(i, j, a["x_sample"][0][bass.ds(i * GTOK - SEQ_P, GTOK)])
            sp.wait_ge(wo_done, NT)
            sp.dma_start(w_xq, a["w_xq"][0].rearrange("(k p) n -> p k n", p=P)).then_inc(w_xq_here, 16)

            def load_expert(e, n, used):
                if used is not None:
                    sp.wait_ge(y_done, used)
                one = slice(e, e + 1) if isinstance(e, int) else bass.ds(e, 1)
                sp.dma_start(w_gu[n][:, 0], a["w_exp_gate"][0, one].rearrange("e (k p) f -> p (e k) f", p=P)).then_inc(w_e_here[n], 16)
                sp.dma_start(w_gu[n][:, 1], a["w_exp_up"][0, one].rearrange("e (k p) f -> p (e k) f", p=P)).then_inc(w_e_here[n], 16)
                sp.dma_start(w_dn[n], a["w_exp_down"][0, one].rearrange("e p d -> (e p) d")).then_inc(w_e_here[n], 16)

            sp.wait_ge(mm_done, 2 * XH)
            sp.dma_start(w_xo, a["w_xo"][0].rearrange("(k p) n -> p k n", p=P)).then_inc(w_xo_here, 16)
            sp.wait_ge(fill_made, 3)
            for b in range(NE, NBLK):
                sp.dma_start(y_exp[b * P:(b + 1) * P].rearrange("p (a c) -> p a c", c=256),
                             zeros.unsqueeze(1).to_broadcast([P, D // 256, 256])).then_inc(unused_filled, 16)

            first_moe = n_norms["moe", 0]
            for n in range(first_moe, len(norms)):
                t = norms[n][1]
                sp.wait_ge(n_ready, n + 1)
                sp.dma_start(xn_moe[t * P:(t + 1) * P], hs[n % 2]).then_inc(xn_stored[n % 2], 16)
                if t == TPC - 1:
                    sp.wait_ge(mm_done, n_groups["q", NCH - 1, XH - 1] + 1)
                    for e in (0, 3):
                        load_expert(e, e, None)
            sp.wait_ge(mm_done, len(groups))
            for e in (1, 2, 4, 5, 6, 7):
                load_expert(e, e, None)

            with sp.Fori(0, NE // RING - 1) as r:
                for n in range(RING):
                    load_expert(RING * (r + 1) + n, n, RING * r + n + 1)

            sp.wait_ge(table_ready, 1)

            def load_overflow(b, half, n, r):
                e = sp.value_load(over_e[0:1, bass.ds(b - NE, 1)], min_val=0, max_val=NE - 1)
                load_expert(e, n, b - 3)

            overflow_blocks(sp, load_overflow)

            sp.dma_start(gf_row, a["g_final"].partition_broadcast(P)).then_inc(consts_here, 16)
            for t in range(NT):
                sp.wait_ge(f_out, t + 1)
                g, base = t // 2, 0 if t < SEQ_P // P else SEQ_P // GTOK
                y = y_prompt if t < SEQ_P // P else y_sample
                y = y[0, (g - base) * GTOK:(g - base + 1) * GTOK].rearrange("(r n c) d -> n r c d", n=4, c=QC)
                for n in range(2):
                    sp.dma_start(y[2 * (t % 2) + n], out_st[t % 2][n * HD:(n + 1) * HD]).then_inc(out_sent[t % 2], 16)
            for j in range(2):
                sp.wait_ge(out_sent[j], 32 * NT // 2)
                sp.wait_ge(xn_stored[j], 16 * NT // 2)

        @blk.gpsimd
        def _(pool):
            xp, xsm = a["x_prompt"][0], a["x_sample"][0]
            for j in range(2):
                pool.dma_start(x_in[j], xp[j * P:(j + 1) * P]).then_inc(x_here[j], 16)
            pool.memset(neg_half, -0.5).then_inc(const_made, 1)
            pool.memset(eps, EPS).then_inc(const_made, 1)
            pool.memset(ident, 0.0).then_inc(ident_made, 1)
            pool.wait_ge(ident_made, 1)
            pool.affine_select(out=ident, in_=ident, compare_op=ALU.not_equal, fill=1.0, base=0,
                               pattern=[[-1, P]], channel_multiplier=1).then_inc(ident_made, 1)
            pool.wait_ge(const_made, 2)

            def rsqrt(col, squares, n_sq, eps_sem, n_eps, out_sem):
                pool.wait_ge(squares, n_sq)
                pool.tensor_tensor(ms_eps[:, col:col + 1], ms[:, col:col + 1], eps, ALU.add).then_inc(eps_sem, 1)
                pool.wait_ge(eps_sem, n_eps)
                pool.tensor_tensor(rs[:, col:col + 1], ms_eps[:, col:col + 1], neg_half, ALU.pow).then_inc(out_sem, 1)

            def load_x(rows, i, j):
                pool.wait_ge(xt_done[j], i)
                pool.dma_start(x_in[j], rows).then_inc(x_here[j], 16)

            def norm_x(i, j):
                rsqrt(j, x_sq[j], i + 1, x_eps[j], i + 1, x_rs[j])

            def tile_work(i, j, last, next_rows):
                t = 2 * i + j
                if j == 0:
                    norm_x(i, 1)
                elif not last:
                    norm_x(i + 1, 0)
                if next_rows is not None:
                    load_x(next_rows(j), i + 1, j)
                rsqrt(2, v_sq, t + 1, v_eps, t + 1, v_rs)
                rsqrt(3, ya_sq, t + 1, ya_eps, t + 1, ya_rs)

            norm_x(0, 0)
            for j in range(2):
                tile_work(0, j, False, lambda j: xp[(2 + j) * P:(3 + j) * P])
            pool.wait_ge(bias_here, 16 * 3 * QC)
            pool.tensor_scalar(bias_src, bias_src, -1.0, 0.0, ALU.mult, ALU.add).then_inc(bias_neg, 1)
            with pool.Fori(1, NT // 2 - 1) as i:
                for j in range(2):
                    tile_work(i, j, False, lambda j: xsm[bass.ds((2 * (i + 1) + j) * P - SEQ_P, P)])
            for j in range(2):
                tile_work(NT // 2 - 1, j, j == 1, None)

            pool.wait_ge(att_done, NT)
            pool.memset(na_bias_row, -MASKED).then_inc(bias_neg, 1)

            for j in range(2):
                pool.wait_ge(qk_done[j], NH // 2)
            for j in range(2):
                pool.memset(q_diag[j], 0.0).then_inc(diag_zero, 1)
            pool.wait_ge(diag_zero, 2)
            for j in range(2):
                pool.wait_ge(qk_evac_v[j], 2 * (NH // 2))
                pool.wait_ge(qk_evac_s[j], NH // 2)
            def head_pair(hp):
                for g in range(NKG):
                    pool.wait_ge(s_done, 2 * (NSTEP * hp + max(2 * g - 2, 0)))
                    for half in range(2):
                        rows = slice(half * HD, (half + 1) * HD)
                        q = qk[rows, hp, g * GTOK:(g + 1) * GTOK].rearrange("p (r n c) -> p n r c", n=4, c=QC)
                        pool.tensor_copy(q_diag[g % 2][rows, :, half], q).then_inc(diag_ready, 1)

            first_then_loop(pool, NPAIR, head_pair)

            def rsqrt_pair(i, j):
                n = i + 1 + NT // 2
                rsqrt(j, x_sq[j], n, x_eps[j], n, x_rs[j])

            tiles(pool, lambda i, j, last: rsqrt_pair(i, j))
            for n in range(len(norms)):
                rsqrt(4 + n % 2, n_sq, n + 1, n_eps, n + 1, n_rs)

            for dst, pattern, base, cm in ((iota_e, [[P, NE]], 0, 0), (iota_b, [[1, NOVER]], 0, 0),
                                           (iota_j, [[P, NT - 1]], P, 0), (first_g, [[-1, NG]], NG, 0),
                                           (first_e, [[-1, EPG]], EPG, 0), (token, [[P, NT]], 0, 1)):
                pool.iota(dst, pattern=pattern, base=base, channel_multiplier=cm,
                          allow_small_or_imprecise_dtypes=True).then_inc(route_const, 1)
            pool.wait_ge(mm_done, n_groups["xo", NT - 1, 1] + 1)
            pool.memset(before, 1.0).then_inc(route_const, 1)
            pool.memset(ones, 1.0).then_inc(route_const, 1)
            pool.wait_ge(route_const, 8)
            pool.affine_select(out=before, in_=before, compare_op=ALU.is_gt, fill=0.0, base=0,
                               pattern=[[1, P]], channel_multiplier=-1).then_inc(route_const, 1)
            for dst, pattern in ((iota_p, [[1, P]]), (iota_blk, [[P, NBLK]])):
                pool.iota(dst, pattern=pattern, base=0, channel_multiplier=0, allow_small_or_imprecise_dtypes=True).then_inc(route_const, 1)

            pool.wait_ge(table_ready, 1)
            for j in range(2):
                pool.wait_ge(xn_stored[j], 16 * NT // 2)

            def gather(rows, j):
                pool.indirect_dma_start(out=x_g[j], out_offset=None, in_=xn_moe,
                                        in_offset=bass.IndirectOffsetOnAxis(ap=rows, axis=0)).then_inc(xg_here[j], 16)

            for b in range(NE + 1):
                if b >= 2:
                    pool.wait_ge(xgt_done, b - 1)
                gather(slot_src[:, b:b + 1], b % 2)
            used = pool.value_load(over_n[0:1, 0:1], min_val=0, max_val=NOVER)
            for b in range(NE + 1, NBLK):
                with pool.If(used > b - NE - 1):
                    pool.wait_ge(xgt_done, b - 1)
                    gather(slot_src[:, b:b + 1], b % 2)

            pool.wait_ge(all_sent, 1)

            def gather_y(t):
                if t >= YRING:
                    pool.wait_ge(f_add, 2 * (t - YRING + 1))
                for k in range(2):
                    pool.indirect_dma_start(out=y_g[t % YRING][k], out_offset=None, in_=y_exp,
                                            in_offset=bass.IndirectOffsetOnAxis(ap=slot[:, k, t:t + 1], axis=0)).then_inc(yg_here[t % YRING], 16)

            for t in range(YRING - 1):
                gather_y(t)
            for t in range(NT):
                if t + YRING - 1 < NT:
                    gather_y(t + YRING - 1)
                n = len(norms) + t
                rsqrt(4 + n % 2, n_sq, n + 1, n_eps, n + 1, n_rs)

        @blk.scalar
        def _(act):
            def square_x(i, j):
                act.wait_ge(x_here[j], 16 * (i + 1))
                first = is_first(i, j)
                if not first:
                    act.wait_ge(sgu_t, 2)
                    act.wait_ge(x_sq[1 - j], i + j)
                nc.scalar.activation(x_junk0 if first else x_junk, x_in[j], ACT.Square,
                                     scale=D ** -0.5, accum_out=ms[:, j:j + 1]).then_inc(x_sq[j], 1)

            def split_w_in(n, ks=slice(0, KT)):
                act.wait_ge(w_in_here[n] if ks.stop == KT else w_v_here, 16)
                make_hi(act, W_UVV_PLACE[n] - (ks.stop < KT), w_uvv_hi[n][:, ks], w_uvv[n][:, ks])

            def split_x_tile(i, j):
                t = 2 * i + j
                act.wait_ge(xf_evac, 2 * (t + 1))
                if not is_first(i, j):
                    act.wait_ge(att_done, t - 1)
                make_hi(act, split_x(t), x_hi[j], xT[:, :, bass.ds(t * P, P)])

            def split_w(i, j):
                act.wait_ge(w_qk_here[j], 16 * (i + 1))
                act.wait_ge(qk_done[j], i)
                make_hi(act, split_w_qk(i, j), w_qk_hi[j], w_qk[j])

            square_x(0, 0)
            split_w_in(1, slice(0, KT // 2))
            split_w_in(1, slice(KT // 2, KT))
            split_x_tile(0, 0)
            split_w_in(0)
            split_w_in(2)

            def tile_work(i, j, last):
                t = 2 * i + j
                nxt = (i, 1) if j == 0 else (i + 1, 0)
                if not last:
                    square_x(*nxt)
                act.wait_ge(v_done, t + 1)
                act.wait_ge(vn_ready, t)
                nc.scalar.activation(v_g, bank[2][:], ACT.Gelu_apprx_tanh).then_inc(v_gelu, 1)
                act.wait_ge(v_gelu, t + 1)
                act.wait_ge(ya_sq, t)
                nc.scalar.activation(sq_junk, v_g, ACT.Square, scale=HALF ** -0.5,
                                     accum_out=ms[:, 2:3]).then_inc(v_sq, 1)
                act.wait_ge(u_done, t + 1)
                act.wait_ge(ya_mul, t)
                nc.scalar.activation(u_g, bank[3][:], ACT.Gelu_apprx_tanh).then_inc(u_gelu, 1)
                if not last:
                    split_x_tile(*nxt)
                act.wait_ge(att_done, t + 1)
                act.wait_ge(v_stored[j], 16 * i)
                nc.scalar.activation(v_st[j], bank[4][:], ACT.Copy).then_inc(att_copied, 1)
                act.wait_ge(att_copied, t + 1)
                act.dma_start(v_att[bass.ds(t * P, P)], v_st[j]).then_inc(v_stored[j], 16)
                if last:
                    make_hi(act, split_xT(0), xT_hi[:, :, 0:CH], xT[:, :, 0:CH])
                    split_w(0, 0)
                act.wait_ge(ya_mul, t + 1)
                act.wait_ge(v_sq, t + 1)
                nc.scalar.activation(sq_junk, y_a, ACT.Square, scale=HALF ** -0.5,
                                     accum_out=ms[:, 3:4]).then_inc(ya_sq, 1)
                act.wait_ge(yan_ready, t + 1)
                for r in range(2):
                    dst = y_mix[bass.ds(i * GTOK, GTOK), 0:HALF].rearrange("(n r c) d -> n r c d", n=4, r=QROWS)
                    act.dma_start(dst[:, 2 * j + r], y_an[j][r * GW:(r + 1) * GW]).then_inc(ya_stored[j], 16)

            tiles(act, tile_work)

            act.wait_ge(mix_done, NT)
            for n in range(1, NCH):
                make_hi(act, split_xT(n), xT_hi[:, :, n * CH:(n + 1) * CH], xT[:, :, n * CH:(n + 1) * CH])
            split_w(0, 1)
            for j in range(2):
                act.wait_ge(ya_stored[j], 16 * 2 * NT // 2)
                act.wait_ge(v_stored[j], 16 * NT // 2)

            def channel_tiles(i, last=False):
                for j in range(2):
                    act.wait_ge(qk_done[j], i + 1)
                    nc.scalar.activation(qk[:, 2 * i + j, CH:2 * CH], bank[3 * j + 1][:], ACT.Copy).then_inc(qk_evac_s[j], 1)
                    if not last:
                        split_w(i + 1, j)

            channel_tiles(0)
            with act.Fori(1, NH // 2 - 1) as i:
                channel_tiles(i)
            channel_tiles(NH // 2 - 1, True)

            def head_pair(hp):
                base = NSTEP * hp

                def exps(s):
                    width = len(NA_GROUPS[s // 2][0]) * P
                    act.wait_ge(s_min, base + s + 1)
                    for n in range(2):
                        p = na_p[s % 2][:, n, 0:width]
                        nc.scalar.activation(p, p, ACT.Exp, bias=na_st[:, 2 * (s % 2) + n:2 * (s % 2) + n + 1], scale=-1.0,
                                             accum_out=na_st[:, 4 + 2 * (s % 2) + n:5 + 2 * (s % 2) + n]).then_inc(p_exp, 1)

                def evac_pT(s):
                    width = len(NA_GROUPS[s // 2][0]) * P
                    act.wait_ge(pt_done, base + s + 1)
                    act.wait_ge(o_done, base + s - 1 if s >= 1 else base)
                    nc.scalar.activation(na_pT[s % 2][:, 0, 0:width], bank[4][:, 0:width], ACT.Copy).then_inc(pt_evac_s, 1)

                for s in range(NSTEP + 1):
                    if s < NSTEP:
                        exps(s)
                    if s >= 1:
                        evac_pT(s - 1)

            first_then_loop(act, NPAIR, head_pair)

            def square_y(i, j):
                act.wait_ge(y_here[j], 16 * (i + 1))
                act.wait_ge(x_sq[1 - j], NT // 2 + i + j)
                nc.scalar.activation(yb_junk, y_cat[j][:, HALF:], ACT.Square, scale=HALF ** -0.5,
                                     accum_out=ms[:, j:j + 1]).then_inc(x_sq[j], 1)

            def split_y_tile(i, j):
                t = 2 * i + j
                act.wait_ge(yT_evac, 2 * (t + 1))
                make_hi(act, split_y(t), y_hi[j], y_T[j])

            for j in range(2):
                square_y(0, j)
            act.wait_ge(w_out_here, 16 * 2 * KT)
            make_hi(act, split_w_out(0), w_out_hi[0], w_out[0])
            split_y_tile(0, 0)
            act.wait_ge(pt_done, NPAIR * NSTEP)
            for j in range(2):
                act.wait_ge(na_stored[j], 16 * 2 * NPAIR * NKG // 2)
            make_hi(act, split_w_out(1), w_out_hi[1], w_out[1])

            def out_tile(i, j, last, last_pair):
                if not last_pair:
                    square_y(i + 1, j)
                if not last:
                    split_y_tile(*((i, 1) if j == 0 else (i + 1, 0)))

            out_tiles(act, out_tile)

            def source(n):
                kind, t = norms[n]
                return mem_in[n] if kind == "mem" else H[:, t]

            def wait_source(eng, n):
                kind, t = norms[n]
                if kind == "mem":
                    eng.wait_ge(mem_here[n % 2], 32)
                elif kind == "h":
                    eng.wait_ge(h_added[t % 2], 2 * (t // 2 + 1))
                else:
                    eng.wait_ge(mm_evac, n_groups["xo", t, 1] + 1)

            act.wait_ge(x_sq[1], NT)
            for what, n in order:
                if what == "sq":
                    wait_source(act, n)
                    if n >= 2:
                        act.wait_ge(nt_done, n - 1)
                    stored = (n - n_norms["moe", 0]) // 2
                    if stored > 0:
                        act.wait_ge(xn_stored[n % 2], 16 * stored)
                    nc.scalar.activation(hs[n % 2], source(n), ACT.Square, scale=D ** -0.5,
                                         accum_out=ms[:, 4 + n % 2:5 + n % 2]).then_inc(n_sq, 1)
                elif what == "mm" and groups[n][0] == "o":
                    c, h = groups[n][1:]
                    act.wait_ge(mm_done, n + 1)
                    make_hi(act, split_o(c, h), o_hi[:, h], bank[4 + n % 2][:])
                elif what == "S":
                    if n == 0:
                        act.wait_ge(w_xo_here, 16)
                        make_hi(act, SPLIT_W_XO, w_xo_hi, w_xo)
                    act.wait_ge(sx_neg, n + 1)
                    if n >= 4:
                        act.wait_ge(ptx_done, n - 3)
                    for h in range(2):
                        k = 2 * (n % 4) + h
                        nc.scalar.activation(p_x[n % 4][:, h], bank[6 + n % 2][:, h * N_MEM:(h + 1) * N_MEM], ACT.Exp,
                                             bias=xa_st[:, 8 + k:9 + k], scale=XA_SCALE,
                                             accum_out=xa_st[:, 16 + k:17 + k]).then_inc(px_exp, 1)
                elif what == "PT":
                    c, t, hp = n // 8, (n % 8) // 2, n % 2
                    act.wait_ge(ptx_done, n + 1)
                    if n % 8 == 0 and c > 0:
                        act.wait_ge(mm_done, n_groups["o", c - 1, XH - 1] + 1)
                    nc.scalar.activation(pT_x[:, 2 * hp:2 * hp + 2, :, t * P:(t + 1) * P],
                                         bank[2 + n % 2][:].rearrange("p (h m t) -> p h m t", h=2, m=2), ACT.Copy).then_inc(ptx_evac, 1)

            act.wait_ge(route_exp, 1)
            nc.scalar.activation(rs8[1][:, :, 0:NG], rs8[0][:, :, 0:NG], ACT.Exp).then_inc(exp_done, 1)
            act.wait_ge(route_exp, 2)
            nc.scalar.activation(rs1[9], rs1[8], ACT.Exp).then_inc(exp_done, 1)

            def expert(b, half, n, r):
                act.wait_ge(gu_done, 2 * b + 1)
                nc.scalar.activation(silu_g, bank[2][:, 0:P], ACT.Silu).then_inc(e_silu, 1)
                act.wait_ge(y_done, b + 1)
                act.wait_ge(y_sent[n % 2], 16 * half)
                nc.scalar.activation(y_st[n % 2][:, 0:HALF], bank[5][:], ACT.Copy).then_inc(y_evac_s, 1)
                act.wait_ge(y_evac_s, b + 1)
                act.wait_ge(y_evac_v, b + 1)
                act.dma_start(y_exp[bass.ds(b * P, P)], y_st[n % 2]).then_inc(y_sent[n % 2], 16)

            expert_blocks(act, expert)
            act.wait_ge(table_ready, 1)
            act.wait_ge(unused_filled, 16 * NOVER)
            overflow_blocks(act, expert)
            used = act.value_load(over_n[0:1, 0:1], min_val=0, max_val=NOVER)
            act.wait_ge(y_sent[0], 16 * (NE // 2) + 16 * ((used + 1) // 2))
            act.wait_ge(y_sent[1], 16 * (NE // 2) + 16 * (used // 2))
            nc.scalar.activation(xa_st[:, 0:1], xa_st[:, 0:1], ACT.Copy).then_inc(all_sent, 1)

            for t in range(NT):
                act.wait_ge(f_add, 2 * (t + 1))
                if t >= 2:
                    act.wait_ge(out_sent[t % 2], 32 * (t // 2))
                n = len(norms) + t
                nc.scalar.activation(out_st[t % 2], H[:, t], ACT.Square, scale=D ** -0.5,
                                     accum_out=ms[:, 4 + n % 2:5 + n % 2]).then_inc(n_sq, 1)

        @blk.vector
        def _(dve):
            nc.vector.memset(pad_t, MASKED).then_inc(fill_made, 1)
            nc.vector.memset(bias_src, MASKED).then_inc(fill_made, 1)
            nc.vector.memset(zeros, 0.0).then_inc(fill_made, 1)
            def scale_x(i, j):
                dve.wait_ge(x_rs[j], i + 1)
                nc.vector.tensor_scalar(x_in[j], x_in[j], rs[:, j:j + 1], None, ALU.mult).then_inc(xs_ready[j], 1)

            def evac_xT(i, j):
                dve.wait_ge(xt_done[j], i + 1)
                t = 2 * i + j
                for n in range(2):
                    g = g_mix[:, 4 * n:4 * n + 4].unsqueeze(2).to_broadcast([P, 4, P])
                    nc.vector.tensor_tensor(xT[:, 4 * n:4 * n + 4, bass.ds(t * P, P)], bank[n][:].rearrange("p (k t) -> p k t", k=4), g,
                                            ALU.mult).then_inc(xf_evac, 1)
                if not is_first(i, j):
                    dve.wait_ge(att_done, t - 1)
                make_lo(dve, split_x(t), x_lo[j], xT[:, :, bass.ds(t * P, P)], x_hi[j])

            def split_w_in(n, ks=slice(0, KT)):
                make_lo(dve, W_UVV_PLACE[n] - (ks.stop < KT), w_uvv_lo[n][:, ks], w_uvv[n][:, ks], w_uvv_hi[n][:, ks])

            def split_w(i, j):
                make_lo(dve, split_w_qk(i, j), w_qk_lo[j], w_qk[j], w_qk_hi[j])

            def split_chunk(n):
                c = slice(n * CH, (n + 1) * CH)
                make_lo(dve, split_xT(n), xT_lo[:, :, c], xT[:, :, c], xT_hi[:, :, c])

            scale_x(0, 0)
            split_w_in(1, slice(0, KT // 2))
            split_w_in(1, slice(KT // 2, KT))
            dve.wait_ge(consts_here, 16 * 8)
            evac_xT(0, 0)
            for n in range(2):
                dve.wait_ge(sgu_t, n + 1)
                nc.vector.tensor_copy(sgu_wT[:, 4 * n:4 * n + 4], bank[6 + n][:].rearrange("p (h q) -> p h q", h=4)).then_inc(sgu_evac, 1)
            split_w_in(0)
            split_w_in(2)

            def tile_work(i, j, last):
                t = 2 * i + j
                nxt = (i, 1) if j == 0 else (i + 1, 0)
                if not last:
                    scale_x(*nxt)
                dve.wait_ge(v_rs, t + 1)
                dve.wait_ge(mix_done, t)
                nc.vector.scalar_tensor_tensor(v_n, v_g, rs[:, 2:3], gv_row, ALU.mult, ALU.mult).then_inc(vn_ready, 1)
                if not last:
                    evac_xT(*nxt)
                else:
                    split_chunk(0)
                    split_w(0, 0)
                dve.wait_ge(mix_done, t + 1)
                dve.wait_ge(ya_mul, t)
                nc.vector.tensor_tensor(mixed.rearrange("p (h d) -> p h d", h=NH), bank[5][:].rearrange("p (h d) -> p h d", h=NH),
                                        sgu_b.unsqueeze(2).to_broadcast([P, NH, HD]), ALU.add).then_inc(mix_bias, 1)
                dve.wait_ge(mix_bias, t + 1)
                dve.wait_ge(u_gelu, t + 1)
                dve.wait_ge(yan_ready, t)
                nc.vector.tensor_tensor(y_a, mixed, u_g, ALU.mult).then_inc(ya_mul, 1)
                dve.wait_ge(ya_rs, t + 1)
                dve.wait_ge(ya_stored[j], 32 * i)
                nc.vector.tensor_scalar(y_an[j], y_a, rs[:, 3:4], None, ALU.mult).then_inc(yan_ready, 1)

            tiles(dve, tile_work)

            for n in range(1, NCH):
                split_chunk(n)
            split_w(0, 1)
            for j in range(2):
                dve.wait_ge(ya_stored[j], 16 * 2 * NT // 2)
                dve.wait_ge(v_stored[j], 16 * NT // 2)

            def channel_tiles(i, last=False):
                for j in range(2):
                    dve.wait_ge(qk_done[j], i + 1)
                    for n in (0, 2):
                        nc.vector.tensor_copy(qk[:, 2 * i + j, n * CH:(n + 1) * CH], bank[3 * j + n][:]).then_inc(qk_evac_v[j], 1)
                    if not last:
                        split_w(i + 1, j)

            channel_tiles(0)
            with dve.Fori(1, NH // 2 - 1) as i:
                channel_tiles(i)
            channel_tiles(NH // 2 - 1, True)

            dve.wait_ge(bias_here, 16 * 3 * QC + 16 * 2 * NH * QROWS)
            def head_pair(hp):
                base = NSTEP * hp

                def scores(s):
                    keys, first, row_masked = NA_GROUPS[s // 2]
                    width = len(keys) * P
                    kind = s % 2
                    bias = (na_bias_row if row_masked else na_bias)[:, hp, kind:kind + 2, first:first + width // KC]
                    for n in range(2):
                        dve.wait_ge(s_done, 2 * (base + s) + n + 1)
                        if n == 0:
                            dve.wait_ge(pt_done, base + s - 1 if s >= 1 else base)
                        nc.vector.scalar_tensor_tensor(
                            na_p[s % 2][:, n, 0:width].rearrange("p (r c) -> p r c", c=KC),
                            bank[2 * (s % 2) + n][:, 0:width].rearrange("p (r c) -> p r c", c=KC), -NA_SCALE,
                            bias[:, n], ALU.mult, ALU.add).then_inc(s_biased, 1)
                    dve.wait_ge(s_biased, 2 * (base + s + 1))
                    nc.vector.tensor_reduce(na_st[:, 2 * (s % 2):2 * (s % 2) + 2], na_p[s % 2][:, :, 0:width], AX, ALU.min).then_inc(s_min, 1)

                def evac_pT(s):
                    width = len(NA_GROUPS[s // 2][0]) * P
                    dve.wait_ge(p_exp, 2 * (base + s + 1))
                    dve.wait_ge(o_evac, 2 * (base + s - 1) if s >= 1 else 2 * base)
                    nc.vector.reciprocal(na_st[:, 8 + 2 * (s % 2):10 + 2 * (s % 2)], na_st[:, 4 + 2 * (s % 2):6 + 2 * (s % 2)]).then_inc(s_rcp, 1)
                    dve.wait_ge(pt_done, base + s + 1)
                    dve.wait_ge(o_done, base + s - 1 if s >= 1 else base)
                    nc.vector.tensor_copy(na_pT[s % 2][:, 1, 0:width], bank[5][:, 0:width]).then_inc(pt_evac_v, 1)

                def evac_o(s):
                    g = s // 2
                    dve.wait_ge(o_done, base + s + 1)
                    dve.wait_ge(s_rcp, base + s + 1)
                    if s % 2 == 0:
                        dve.wait_ge(na_stored[g % 2], 32 * (3 * hp + g // 2))
                    for half in range(2):
                        rows = slice(half * HD, (half + 1) * HD)
                        o = bank[6 + s % 2][rows, 0:2 * P].rearrange("p (n d) -> p n d", n=2)[:, :, half * HD:(half + 1) * HD]
                        r = na_st[rows, 8 + 2 * (s % 2):10 + 2 * (s % 2)].unsqueeze(2).to_broadcast([HD, 2, HD])
                        nc.vector.tensor_tensor(na_o[g % 2][rows, 2 * (s % 2):2 * (s % 2) + 2], o, r, ALU.mult).then_inc(o_evac, 1)

                for s in range(NSTEP + 2):
                    if s < NSTEP:
                        scores(s)
                    if 1 <= s <= NSTEP:
                        evac_pT(s - 1)
                    if s >= 2:
                        evac_o(s - 2)

            first_then_loop(dve, NPAIR, head_pair)

            def scale_y(i, j):
                dve.wait_ge(x_rs[j], NT // 2 + i + 1)
                nc.vector.tensor_scalar(y_cat[j][:, HALF:], y_cat[j][:, HALF:], rs[:, j:j + 1], None, ALU.mult).then_inc(yb_ready[j], 1)

            def gain_evac(dst, n, gain, done, first_bank=0):
                g = gain[:, 4 * n:4 * n + 4].unsqueeze(2).to_broadcast([P, 4, P])
                nc.vector.tensor_tensor(dst, bank[first_bank + n][:].rearrange("p (k t) -> p k t", k=4), g, ALU.mult).then_inc(done, 1)

            def evac_yT(i, j):
                dve.wait_ge(yt_done[j], i + 1)
                if not is_first(i, j):
                    dve.wait_ge(wo_done, 2 * i + j - 1)
                for n in range(2):
                    gain_evac(y_T[j][:, 4 * n:4 * n + 4], n, g_out, yT_evac)

            def split_y_tile(i, j):
                make_lo(dve, split_y(2 * i + j), y_lo[j], y_T[j], y_hi[j])

            for j in range(2):
                scale_y(0, j)
            make_lo(dve, split_w_out(0), w_out_lo[0], w_out[0], w_out_hi[0])
            evac_yT(0, 0)
            split_y_tile(0, 0)
            make_lo(dve, split_w_out(1), w_out_lo[1], w_out[1], w_out_hi[1])

            def add_rows(i, j, last, last_pair):
                if not last:
                    nxt = (i, 1) if j == 0 else (i + 1, 0)
                    evac_yT(*nxt)
                    split_y_tile(*nxt)
                if not last_pair:
                    scale_y(i + 1, j)
                t = 2 * i + j
                dve.wait_ge(wo_done, t + 1)
                dve.wait_ge(xr_here[j], 32 * (i + 1))
                for n in range(2):
                    cols = slice(n * HALF, (n + 1) * HALF)
                    nc.vector.tensor_tensor(H[:, t, cols], bank[2 + 2 * j + n][:], x_res[j][:, cols], ALU.add).then_inc(h_added[j], 1)

            out_tiles(dve, add_rows)

            for what, n in order:
                if what == "pre":
                    dve.wait_ge(n_rs, n + 1)
                    src = mem_in[n] if norms[n][0] == "mem" else H[:, norms[n][1]]
                    nc.vector.tensor_scalar(hs[n % 2], src, rs[:, 4 + n % 2:5 + n % 2], None, ALU.mult).then_inc(n_ready, 1)
                elif what == "T":
                    kind, t = norms[n]
                    dve.wait_ge(nt_done, n + 1)
                    if kind == "mem":
                        dst, gain = mem_T[:, :, t * P:(t + 1) * P], g_mem
                    elif kind == "h":
                        if t % TPC == 0 and t > 0:
                            dve.wait_ge(mm_done, n_groups["q", t // TPC - 1, XH - 1] + 1)
                        dst, gain = h_T[:, :, (t % TPC) * P:(t % TPC + 1) * P], g_xattn
                    else:
                        if t >= 2:
                            dve.wait_ge(mm_done, n_groups["route", t - 2] + 1)
                        dst, gain = r_T[t % 2], g_moe
                    for b in range(2):
                        gain_evac(dst[:, 4 * b:4 * b + 4], b, gain, nt_evac, norm_bank(n))
                elif what == "mm":
                    kind, *which = groups[n]
                    dve.wait_ge(mm_done, n + 1)
                    b = bank[4 + n % 2]
                    if kind == "xo":
                        t, half = which
                        cols = slice(half * HALF, (half + 1) * HALF)
                        nc.vector.tensor_tensor(H[:, t, cols], H[:, t, cols], b[:], ALU.add).then_inc(mm_evac, 1)
                    elif kind == "o":
                        c, h = which
                        dve.wait_ge(hi_made, split_o(c, h) + 1)
                        nc.vector.tensor_tensor(o_lo[:, h], b[:], o_hi[:, h].bitcast(F32), ALU.subtract).then_inc(mm_evac, 1)
                    elif kind == "route":
                        nc.vector.tensor_copy(logit[:, which[0]], b[:, 0:NG + NE]).then_inc(mm_evac, 1)
                    else:
                        dst = {"k_mem": lambda: k_mem[:, which[0]], "v_mem": lambda: v_mem[:, which[0]],
                               "q": lambda: q_x[which[0] % 2][:, which[1]]}[kind]()
                        nc.vector.tensor_copy(dst, b[:]).then_inc(mm_evac, 1)
                elif what == "S":
                    if n == 0:
                        make_lo(dve, SPLIT_W_XO, w_xo_lo, w_xo, w_xo_hi)
                    k = 2 * (n % 4)
                    dve.wait_ge(sx_done, n + 1)
                    if n >= 4:
                        dve.wait_ge(px_ready, n - 3)
                    nc.vector.tensor_reduce(xa_st[:, k:k + 2], bank[6 + n % 2][:].rearrange("p (h m) -> p h m", h=2), AX, ALU.max).then_inc(sx_max, 1)
                    dve.wait_ge(sx_max, n + 1)
                    nc.vector.tensor_scalar(xa_st[:, 8 + k:10 + k], xa_st[:, k:k + 2], -XA_SCALE, None, ALU.mult).then_inc(sx_neg, 1)
                elif what == "px":
                    k = 2 * (n % 4)
                    dve.wait_ge(px_exp, 2 * (n + 1))
                    nc.vector.reciprocal(xa_st[:, 24 + k:26 + k], xa_st[:, 16 + k:18 + k]).then_inc(sx_rcp, 1)
                    dve.wait_ge(sx_rcp, n + 1)
                    r = xa_st[:, 24 + k:26 + k].unsqueeze(2).to_broadcast([P, 2, N_MEM])
                    nc.vector.tensor_tensor(p_x[n % 4], p_x[n % 4], r, ALU.mult).then_inc(px_ready, 1)

            done = [0]

            def step(ins):
                done[0] += 1
                ins.then_inc(route, 1)
                dve.wait_ge(route, done[0])

            def over_tokens(v, n):
                return v.unsqueeze(2).to_broadcast([P, NT, n])

            def first_max(out, scores, peak, order_of, tmp, best):
                n = scores.shape[-1]
                step(nc.vector.tensor_tensor(tmp, scores, over_tokens(peak, n), ALU.is_equal))
                step(nc.vector.tensor_tensor(tmp, tmp, order_of.unsqueeze(1).to_broadcast([P, NT, n]), ALU.mult))
                step(nc.vector.tensor_reduce(best, tmp, AX, ALU.max))
                step(nc.vector.tensor_tensor(out, tmp, over_tokens(best, n), ALU.is_equal))

            dve.wait_ge(route_const, 6)
            dve.wait_ge(mm_evac, len(groups))
            dve.wait_ge(mm_done, len(groups))
            lg, le = logit[:, :, 0:NG], logit[:, :, NG:]
            g_max, g_best, g_sum, g_top, e_max, e_best, e_max2, e_best2 = rs1[:8]
            e_diff, e_exp, e_sum, e_rcp = rs1[8:12]
            g_one = rs8[4][:, :, 0:NG]
            step(nc.vector.tensor_reduce(g_max, lg, AX, ALU.max))
            nc.vector.tensor_tensor(rs8[0][:, :, 0:NG], lg, over_tokens(g_max, NG), ALU.subtract).then_inc(route_exp, 1)
            first_max(g_one, lg, g_max, first_g, rs8[3][:, :, 0:NG], g_best)
            by_group = "p t (g e) -> p t g e"
            step(nc.vector.tensor_tensor(rt[0].rearrange(by_group, g=NG), le.rearrange(by_group, g=NG),
                                         g_one.unsqueeze(3).to_broadcast([P, NT, NG, EPG]), ALU.mult))
            e_sel, e_sel2, one1, one2 = rs8[5], rs8[6], rs8[9], rs8[11]
            step(nc.vector.tensor_reduce(e_sel, rt[0].rearrange("p t (g e) -> p t e g", g=NG), AX, ALU.add))
            step(nc.vector.tensor_reduce(e_max, e_sel, AX, ALU.max))
            first_max(one1, e_sel, e_max, first_e, rs8[7], e_best)
            step(nc.vector.scalar_tensor_tensor(e_sel2, one1, -3.0e38, e_sel, ALU.mult, ALU.add))
            step(nc.vector.tensor_reduce(e_max2, e_sel2, AX, ALU.max))
            first_max(one2, e_sel2, e_max2, first_e, rs8[8], e_best2)
            nc.vector.tensor_tensor(e_diff, e_max2, e_max, ALU.subtract).then_inc(route_exp, 1)
            for k, one in ((0, one1), (1, one2)):
                step(nc.vector.tensor_tensor(rt[1 + k].rearrange(by_group, g=NG), g_one.unsqueeze(3).to_broadcast([P, NT, NG, EPG]),
                                             one.unsqueeze(2).to_broadcast([P, NT, NG, EPG]), ALU.mult))
            nc.vector.tensor_tensor(rt[3], rt[1], rt[2], ALU.add).then_inc(chosen, 1)
            dve.wait_ge(exp_done, 2)
            step(nc.vector.tensor_reduce(g_sum, rs8[1][:, :, 0:NG], AX, ALU.add))
            step(nc.vector.reciprocal(g_top, g_sum))
            step(nc.vector.tensor_scalar(e_sum, e_exp, 1.0, None, ALU.add))
            step(nc.vector.reciprocal(e_rcp, e_sum))
            step(nc.vector.tensor_tensor(gate[:, 0], g_top, e_rcp, ALU.mult))
            step(nc.vector.tensor_tensor(gate[:, 1], gate[:, 0], e_exp, ALU.mult))
            earlier, rank = rt[5], rt[4]
            sums, same_e, by_e = (rt[n].rearrange("p t e -> p (t e)") for n in (6, 7, 8))
            so_far, same = (v.rearrange("p (e t) -> p e t", e=NE) for v in (sums, same_e))
            step(nc.vector.memset(same, 1.0))
            step(nc.vector.memset(same[:, :, 0], 0.0))
            dve.wait_ge(count_done, 1)
            per_tile = bank[3][:, 0:NT * NE].rearrange("p (t e) -> p t e", t=NT)
            step(nc.vector.tensor_copy(by_e.rearrange("p (e t) -> p e t", e=NE), per_tile.rearrange("p t e -> p e t")))
            step(nc.vector.tensor_tensor_scan(sums, same_e, by_e, 0.0, ALU.mult, ALU.add))
            count = so_far[:, :, NT - 1]
            step(nc.vector.tensor_tensor(earlier, so_far.rearrange("p e t -> p t e"), per_tile, ALU.subtract))
            step(nc.vector.tensor_tensor(rank, bank[2][:, 0:NT * NE].rearrange("p (t e) -> p t e", t=NT), earlier, ALU.add))
            n_over, over_incl, over_at, shift = re[1], re[2], re[3], re[4]
            step(nc.vector.tensor_tensor(r11, count.unsqueeze(2).to_broadcast([P, NE, NT - 1]),
                                         iota_j.unsqueeze(1).to_broadcast([P, NE, NT - 1]), ALU.is_gt))
            step(nc.vector.tensor_reduce(n_over, r11, AX, ALU.add))
            step(nc.vector.tensor_tensor_scan(over_incl, ones[:, 0:NE], n_over, 0.0, ALU.mult, ALU.add))
            step(nc.vector.tensor_tensor(over_at, over_incl, n_over, ALU.subtract))
            step(nc.vector.tensor_scalar(shift, over_at, float(P), float(P * (NE - 1)), ALU.mult, ALU.add))
            step(nc.vector.tensor_tensor(re[5], shift, iota_e, ALU.subtract))
            step(nc.vector.tensor_scalar(rt[6], rank, float(P), None, ALU.is_ge))
            step(nc.vector.tensor_tensor(rt[7], rt[6], re[5].unsqueeze(1).to_broadcast([P, NT, NE]), ALU.mult))
            step(nc.vector.tensor_tensor(rt[8], rt[7], rank, ALU.add))
            step(nc.vector.tensor_tensor(rt[9], rt[8], iota_e.unsqueeze(1).to_broadcast([P, NT, NE]), ALU.add))
            dve.wait_ge(route_const, 11)
            for k in range(2):
                slot_f, place_f, block_f = rs1[12 + k], rs1[10 + k], rs1[14 + k]
                step(nc.vector.tensor_tensor(rt[6 + k], rt[1 + k], rt[9], ALU.mult))
                step(nc.vector.tensor_reduce(slot_f, rt[6 + k], AX, ALU.add))
                step(nc.vector.tensor_copy(slot[:, k], slot_f))
                step(nc.vector.tensor_scalar(place_i, slot[:, k], P - 1, None, ALU.bitwise_and))
                step(nc.vector.tensor_copy(place_f, place_i))
                step(nc.vector.tensor_tensor(block_f, slot_f, place_f, ALU.subtract))
                step(nc.vector.tensor_tensor(in_place[k], over_tokens(place_f, P), iota_p.unsqueeze(1).to_broadcast([P, NT, P]), ALU.is_equal))
                step(nc.vector.tensor_tensor(in_block[k], over_tokens(block_f, NBLK), iota_blk.unsqueeze(1).to_broadcast([P, NT, NBLK]),
                                             ALU.is_equal))
                nc.vector.tensor_tensor(in_block[k], in_block[k].bitcast(F32), over_tokens(token, NBLK), ALU.mult).then_inc(slot_ready, 1)
            step(nc.vector.tensor_tensor(r23, over_incl.unsqueeze(1).to_broadcast([P, NOVER, NE]),
                                         iota_b.unsqueeze(2).to_broadcast([P, NOVER, NE]), ALU.is_le))
            step(nc.vector.tensor_reduce(over_f, r23, AX, ALU.add))
            step(nc.vector.tensor_scalar(over_e, over_f, float(NE - 1), None, ALU.min))
            step(nc.vector.tensor_copy(over_n, over_incl[:, NE - 1:NE]))
            dve.wait_ge(slots_done, 1)
            nc.vector.tensor_copy(slot_src, bank[2][:, 0:NBLK]).then_inc(table_ready, 1)

            def evac_xg(b, n):
                dve.wait_ge(xgt_done, b + 1)
                for k in range(2):
                    gain_evac(x_gT[n % 2][:, 4 * k:4 * k + 4], k, g_moe, xgt_evac)

            def expert(b, half, n, r):
                dve.wait_ge(e_silu, b + 1)
                dve.wait_ge(gu_done, 2 * b + 2)
                nc.vector.tensor_tensor(act_T[n % 2], silu_g, bank[4][:, 0:P], ALU.mult).then_inc(e_act, 1)
                evac_xg(b + 1, n + 1)
                dve.wait_ge(y_done, b + 1)
                dve.wait_ge(y_sent[n % 2], 16 * half)
                nc.vector.tensor_copy(y_st[n % 2][:, HALF:], bank[6][:]).then_inc(y_evac_v, 1)

            evac_xg(0, 0)
            expert_blocks(dve, expert)
            overflow_blocks(dve, expert)

            dve.wait_ge(consts_here, 16 * 9)

            def add_experts(t):
                dve.wait_ge(yg_here[t % YRING], 32 * (t // YRING + 1))
                for k in range(2):
                    if k == 1:
                        dve.wait_ge(f_add, 2 * t + 1)
                    nc.vector.scalar_tensor_tensor(H[:, t], y_g[t % YRING][k], gate[:, k, t:t + 1], H[:, t], ALU.mult, ALU.add).then_inc(f_add, 1)

            add_experts(0)
            for t in range(NT):
                if t + 1 < NT:
                    add_experts(t + 1)
                dve.wait_ge(n_rs, len(norms) + t + 1)
                n = len(norms) + t
                nc.vector.scalar_tensor_tensor(out_st[t % 2], H[:, t], rs[:, 4 + n % 2:5 + n % 2], gf_row, ALU.mult, ALU.mult).then_inc(f_out, 1)

        @blk.tensor
        def _(pe):
            pe.wait_ge(ident_made, 2)

            def transpose_x(i, j):
                pe.wait_ge(xs_ready[j], i + 1)
                pe.wait_ge(xf_evac, 2 * (2 * i + j))
                for k in range(KT):
                    last = nc.tensor.transpose(bank[k // 4][:, (k % 4) * P:(k % 4 + 1) * P], x_in[j][:, k * P:(k + 1) * P], ident)
                last.then_inc(xt_done[j], 1)

            def project(i, j, out, n, done):
                split_products(out[:], [(x_hi[j][:, k], x_lo[j][:, k], w_uvv_hi[n][:, k], w_uvv_lo[n][:, k])
                                        for k in range(KT)]).then_inc(done, 1)

            transpose_x(0, 0)
            pe.wait_ge(sgu_w_here, 16)
            for n in range(2):
                for h in range(4 * n, 4 * n + 4):
                    last = nc.tensor.transpose(bank[6 + n][:, (h % 4) * P:(h % 4 + 1) * P], sgu_nat[:, h], ident)
                last.then_inc(sgu_t, 1)

            def tile_work(i, j, last):
                t = 2 * i + j
                first = isinstance(t, int) and t == 0
                pe.wait_ge(lo_made, split_x(t) + 1)
                pe.wait_ge(v_gelu, t)
                project(i, j, bank[2], 1, v_done)
                if first:
                    pe.wait_ge(lo_made, W_UVV_PLACE[0] + 1)
                pe.wait_ge(u_gelu, t)
                project(i, j, bank[3], 0, u_done)
                if j == 0:
                    transpose_x(i, 1)
                elif not last:
                    transpose_x(i + 1, 0)
                if first:
                    pe.wait_ge(lo_made, W_UVV_PLACE[2] + 1)
                pe.wait_ge(att_copied, t)
                project(i, j, bank[4], 2, att_done)
                pe.wait_ge(vn_ready, t + 1)
                if first:
                    pe.wait_ge(sgu_evac, 2)
                pe.wait_ge(mix_bias, t)
                for h in range(NH):
                    mm = nc.tensor.matmul(bank[5][:, h * HD:(h + 1) * HD], sgu_wT[:, h], v_n[:, h * HD:(h + 1) * HD],
                                          start=True, stop=True)
                mm.then_inc(mix_done, 1)

            tiles(pe, tile_work)

            pe.wait_ge(mix_bias, NT)
            pe.wait_ge(att_copied, NT)
            def channel_tiles(i):
                for j in range(2):
                    pe.wait_ge(lo_made, split_w_qk(i, j) + 1)
                    pe.wait_ge(qk_evac_v[j], 2 * i)
                    pe.wait_ge(qk_evac_s[j], i)
                    for n in range(NCH):
                        c = slice(n * CH, (n + 1) * CH)
                        if is_first(i, j):
                            pe.wait_ge(lo_made, split_xT(n) + 1)
                        last = split_products(bank[3 * j + n][:], [(w_qk_hi[j][:, k], w_qk_lo[j][:, k], xT_hi[:, k, c], xT_lo[:, k, c])
                                                                   for k in range(KT)])
                    last.then_inc(qk_done[j], 1)

            first_then_loop(pe, NH // 2, channel_tiles)

            for j in range(2):
                pe.wait_ge(qk_evac_v[j], NH)
                pe.wait_ge(qk_evac_s[j], NH // 2)
            def head_pair(hp):
                base = NSTEP * hp

                def scores(s):
                    g = s // 2
                    keys = NA_GROUPS[g][0]
                    if s % 2 == 0:
                        pe.wait_ge(diag_ready, 2 * (NKG * hp + g + 1))
                    pe.wait_ge(s_biased, 2 * (base + s) - 2 if s >= 1 else 2 * base)
                    for n in range(2):
                        block = 2 * (s % 2) + n
                        q = q_diag[g % 2][:, block].rearrange("p h r c -> p (h r c)")
                        row0 = keys[0] * QROWS
                        k = qk[:, NPAIR + hp].rearrange("p (r c) -> p r c", c=GW)
                        k = k[:, row0:row0 + QROWS * len(keys), COL_START[block]:COL_START[block] + KC]
                        nc.tensor.matmul(bank[2 * (s % 2) + n][:, 0:P * len(keys)], q, k, start=True, stop=True).then_inc(s_done, 1)

                def transpose_p(s):
                    nk = len(NA_GROUPS[s // 2][0])
                    pe.wait_ge(p_exp, 2 * (base + s + 1))
                    pe.wait_ge(pt_evac_s, base + s)
                    pe.wait_ge(pt_evac_v, base + s)
                    for n in range(2):
                        for k in range(nk):
                            last = nc.tensor.transpose(bank[4 + n][:, k * P:(k + 1) * P], na_p[s % 2][:, n, k * P:(k + 1) * P], ident)
                    last.then_inc(pt_done, 1)

                def values(s):
                    keys = NA_GROUPS[s // 2][0]
                    pe.wait_ge(pt_evac_s, base + s + 1)
                    pe.wait_ge(pt_evac_v, base + s + 1)
                    pe.wait_ge(vals_here[keys[-1] // 2], 16 * 4 * 2)
                    pe.wait_ge(vals_here[keys[0] // 2], 16 * 4 * 2)
                    pe.wait_ge(o_evac, 2 * (base + s - 1) if s >= 1 else 2 * base)
                    for n in range(2):
                        for k, kg in enumerate(keys):
                            last = nc.tensor.matmul(bank[6 + s % 2][:, n * P:(n + 1) * P], na_pT[s % 2][:, n, k * P:(k + 1) * P],
                                                    vals[:, 4 * kg + 2 * (s % 2) + n, bass.ds(hp * P, P)],
                                                    start=(k == 0), stop=(k == len(keys) - 1))
                    last.then_inc(o_done, 1)

                for s in range(NSTEP + 2):
                    if s < NSTEP:
                        scores(s)
                    if 1 <= s <= NSTEP:
                        transpose_p(s - 1)
                    if s >= 2:
                        values(s - 2)

            first_then_loop(pe, NPAIR, head_pair)

            pe.wait_ge(o_evac, 2 * NPAIR * NSTEP)

            def transpose_y(i, j):
                pe.wait_ge(yb_ready[j], i + 1)
                pe.wait_ge(yT_evac, 2 * (2 * i + j))
                for k in range(KT):
                    last = nc.tensor.transpose(bank[k // 4][:, (k % 4) * P:(k % 4 + 1) * P], y_cat[j][:, k * P:(k + 1) * P], ident)
                last.then_inc(yt_done[j], 1)

            transpose_y(0, 0)

            def out_tile(i, j, last):
                if j == 0:
                    transpose_y(i, 1)
                elif not last:
                    transpose_y(i + 1, 0)
                t = 2 * i + j
                pe.wait_ge(lo_made, split_y(t) + 1)
                pe.wait_ge(h_added[j], 2 * i)
                for n in range(2):
                    if n == 1 and is_first(i, j):
                        pe.wait_ge(lo_made, split_w_out(1) + 1)
                    mm = split_products(bank[2 + 2 * j + n][:], [(y_hi[j][:, k], y_lo[j][:, k], w_out_hi[n][:, k], w_out_lo[n][:, k])
                                                                 for k in range(KT)])
                mm.then_inc(wo_done, 1)

            tiles(pe, out_tile)
            for j in range(2):
                pe.wait_ge(h_added[j], NT)

            for what, n in stages:
                if what == "T":
                    pe.wait_ge(n_ready, n + 1)
                    b = norm_bank(n)
                    before_n = [m for m in range(n) if norm_bank(m) == b]
                    if before_n:
                        pe.wait_ge(nt_evac, 2 * (before_n[-1] + 1))
                    if b == 2 and n > 4:
                        pe.wait_ge(ptx_evac, 8 * NCH)
                    for k in range(KT):
                        last = nc.tensor.transpose(bank[b + k // 4][:, (k % 4) * P:(k % 4 + 1) * P], hs[n % 2][:, k * P:(k + 1) * P], ident)
                    last.then_inc(nt_done, 1)
                elif what == "mm":
                    kind, *which = groups[n]
                    b = bank[4 + n % 2]
                    if n >= 2:
                        pe.wait_ge(mm_evac, n - 1)
                    if kind == "k_mem":
                        pe.wait_ge(w_xkv_here, 16)
                        pe.wait_ge(nt_evac, 2 * 4)
                        h = which[0]
                        steps = [(w_xkv[:, k, h * P:(h + 1) * P], mem_T[:, k]) for k in range(KT)]
                    elif kind == "v_mem":
                        m = which[0]
                        steps = [(mem_T[:, k, m * P:(m + 1) * P], w_xkv[:, k, HALF:]) for k in range(KT)]
                    elif kind == "q":
                        c, h = which
                        pe.wait_ge(w_xq_here, 16)
                        pe.wait_ge(nt_evac, 2 * (n_norms["h", TPC * c + TPC - 1] + 1))
                        steps = [(w_xq[:, k, h * P:(h + 1) * P], h_T[:, k]) for k in range(KT)]
                    elif kind == "o":
                        c, h = which
                        pe.wait_ge(ptx_evac, 8 * (c + 1))
                        seq = 0 if c * CH < SEQ_P else 1
                        steps = [(v_mem[:, 2 * seq + m, h * P:(h + 1) * P], pT_x[:, h, m]) for m in range(2)]
                    elif kind == "xo":
                        t, half = which
                        pe.wait_ge(lo_made, SPLIT_W_XO + 1)
                        pe.wait_ge(mm_evac, n_groups["o", t // TPC, XH - 1] + 1)
                        rows, cols = slice(t % TPC * P, (t % TPC + 1) * P), slice(half * HALF, (half + 1) * HALF)
                        split_products(b[:], [(o_hi[:, h, rows], o_lo[:, h, rows], w_xo_hi[:, h, cols], w_xo_lo[:, h, cols])
                                              for h in range(XH)]).then_inc(mm_done, 1)
                        continue
                    else:
                        t = which[0]
                        pe.wait_ge(w_rt_here, 32)
                        pe.wait_ge(nt_evac, 2 * (n_norms["moe", t] + 1))
                        b = b[:, 0:NG + NE]
                        steps = [(r_T[t % 2][:, k], w_rt[:, k]) for k in range(KT)]
                    for k, (w, x) in enumerate(steps):
                        mm = nc.tensor.matmul(b if kind == "route" else b[:], w, x, start=(k == 0), stop=(k == len(steps) - 1))
                    mm.then_inc(mm_done, 1)
                elif what == "S":
                    c, t, hp = n // 8, (n % 8) // 2, n % 2
                    seq = 0 if c * CH < SEQ_P else 1
                    pe.wait_ge(mm_evac, n_groups["q", c, XH - 1] + 1)
                    if n >= 2:
                        pe.wait_ge(px_exp, 2 * (n - 1))
                    for h in (2 * hp, 2 * hp + 1):
                        mm = nc.tensor.matmul(bank[6 + n % 2][:, (h % 2) * N_MEM:(h % 2 + 1) * N_MEM],
                                              q_x[c % 2][:, h, t * P:(t + 1) * P], k_mem[:, h, seq * N_MEM:(seq + 1) * N_MEM],
                                              start=True, stop=True)
                    mm.then_inc(sx_done, 1)
                elif what == "PT":
                    pe.wait_ge(px_ready, n + 1)
                    pe.wait_ge(nt_evac, 2 * 4)
                    if n >= 2:
                        pe.wait_ge(ptx_evac, n - 1)
                    for h in range(2):
                        for m in range(2):
                            last = nc.tensor.transpose(bank[2 + n % 2][:, (2 * h + m) * P:(2 * h + m + 1) * P],
                                                       p_x[n % 4][:, h, m * P:(m + 1) * P], ident)
                    last.then_inc(ptx_done, 1)

            pe.wait_ge(route_const, 9)
            pe.wait_ge(chosen, 1)
            pe.wait_ge(ptx_evac, 8 * NCH)
            flat = rt[3].rearrange("p t e -> p (t e)")
            nc.tensor.matmul(bank[2][:, 0:NT * NE], before, flat, start=True, stop=True)
            nc.tensor.matmul(bank[3][:, 0:NT * NE], ones, flat, start=True, stop=True).then_inc(count_done, 1)
            for k in range(2):
                pe.wait_ge(slot_ready, k + 1)
                for t in range(NT):
                    last = nc.tensor.matmul(bank[2][:, 0:NBLK], in_place[k][:, t], in_block[k][:, t],
                                            start=(k == 0 and t == 0), stop=(k == 1 and t == NT - 1))
            last.then_inc(slots_done, 1)
            pe.wait_ge(table_ready, 1)

            def transpose_xg(b, half, n):
                pe.wait_ge(xg_here[n % 2], 16 * (half + 1))
                pe.wait_ge(xgt_evac, 2 * b)
                for k in range(KT):
                    last = nc.tensor.transpose(bank[k // 4][:, (k % 4) * P:(k % 4 + 1) * P], x_g[n % 2][:, k * P:(k + 1) * P], ident)
                last.then_inc(xgt_done, 1)

            def expert(b, half, n, r):
                pe.wait_ge(xgt_evac, 2 * (b + 1))
                pe.wait_ge(w_e_here[n], 48 * (r + 1))
                for half_gu, out in enumerate((bank[2], bank[4])):
                    for k in range(KT):
                        mm = nc.tensor.matmul(out[:, 0:P], w_gu[n][:, half_gu, k], x_gT[n % 2][:, k], start=(k == 0), stop=(k == KT - 1))
                    mm.then_inc(gu_done, 1)
                transpose_xg(b + 1, half + n % 2, n + 1)
                pe.wait_ge(e_act, b + 1)
                pe.wait_ge(y_evac_s, b)
                pe.wait_ge(y_evac_v, b)
                for k in range(2):
                    mm = nc.tensor.matmul(bank[5 + k][:], act_T[n % 2], w_dn[n][:, k * HALF:(k + 1) * HALF], start=True, stop=True)
                mm.then_inc(y_done, 1)

            transpose_xg(0, 0, 0)
            expert_blocks(pe, expert)
            overflow_blocks(pe, expert)

        return nc


INPUTS = ["x_prompt", "x_sample", "mem_prompt", "mem_sample", "g_mix", "w_in", "g_sgu_v", "sgu_w", "sgu_b", "na_rpb",
          "g_out_a", "g_out_b", "w_out", "g_xattn", "g_mem", "w_xq", "w_xkv", "w_xo", "g_moe", "w_router_group",
          "w_router_expert", "w_exp_gate", "w_exp_up", "w_exp_down", "g_final"]


def kernel(**inputs):
    import numpy as np
    import concourse.bacc as bacc
    from concourse.bass_utils import run_bass_kernel_spmd

    nc = bacc.Bacc("TRN2", target_bir_lowering=False, num_devices=1)
    arrays, aps = {}, {}
    for name in INPUTS:
        v = np.ascontiguousarray(inputs[name])
        arrays[f"in_{name}"] = v
        aps[name] = nc.dram_tensor(f"in_{name}", v.shape, mybir.dt.from_np(v.dtype), kind="ExternalInput").ap()
    outs = [nc.dram_tensor(f"out_{n}", (1, rows, D), F32, kind="ExternalOutput").ap() for n, rows in (("prompt", SEQ_P), ("sample", SEQ_S))]
    hymba_encoder(nc, aps, *outs)
    r = run_bass_kernel_spmd(nc, [arrays], core_ids=[0])
    return tuple(r.results[0][n] for n in ("out_prompt", "out_sample"))
```
